# Optimizing a Trainium2 kernel written in Bass

```python
import math
import jax, jax.numpy as jnp
from jax import lax
import numpy as np

D_MODEL = 2048
BATCH = 1
SEQ = 256
DEPTH = 1
DEC_BATCH = 1
DEC_SEQ = 256
PAST_LEN = 128

HEAD_DIM = 128
NA_HEADS = 8
GQA_Q_HEADS = 8
GQA_KV_HEADS = 2
GRID_W = 64
NA_ROWS_MAX = 8
NA_COLS = 16
NA_QCOL_BLOCK = 16
NA_KCOL_BLOCK = NA_QCOL_BLOCK + NA_COLS
Q_BLOCK = 128
ROPE_THETA = 10000.0
PLE_DIM = 256
D_FF = -(-8 * D_MODEL // (3 * 256)) * 256
RMS_EPS = 1e-6
NEG_INF = -1e30

NA_WIDTH = NA_HEADS * HEAD_DIM
GQA_Q_WIDTH = GQA_Q_HEADS * HEAD_DIM
GQA_KV_WIDTH = GQA_KV_HEADS * HEAD_DIM
IN_COLS = 3 * NA_WIDTH + GQA_Q_WIDTH + 2 * GQA_KV_WIDTH + 2 * D_MODEL

kernel_name = "hybrid_natten_gqa_sandwich_encoder"

def rmsnorm(x, g):
    xf = x.astype(jnp.float32)
    y = xf * lax.rsqrt(jnp.mean(xf * xf, axis=-1, keepdims=True) + RMS_EPS)
    return (y * g.astype(jnp.float32)).astype(x.dtype)

def neighbourhood_attention(q, k, v, rpb):
    B, S, H, Dh = q.shape
    rows = S // GRID_W
    kh = min(NA_ROWS_MAX, rows)
    n_cb = GRID_W // NA_QCOL_BLOCK
    scale = 1.0 / math.sqrt(Dh)
    qc = np.arange(GRID_W).reshape(n_cb, NA_QCOL_BLOCK)
    cs = np.clip(qc - NA_COLS // 2, 0, GRID_W - NA_COLS)
    kc0 = np.clip(np.arange(n_cb) * NA_QCOL_BLOCK - NA_COLS // 2, 0, GRID_W - NA_KCOL_BLOCK)
    kc = kc0[:, None] + np.arange(NA_KCOL_BLOCK)
    col_ok = (kc[:, None, :] >= cs[..., None]) & (kc[:, None, :] < cs[..., None] + NA_COLS)
    dc_idx = np.clip(kc[:, None, :] - qc[..., None], -(NA_COLS - 1), NA_COLS - 1) + NA_COLS - 1
    col_bias = rpb.astype(jnp.float32)[:, :, dc_idx]
    col_ok = jnp.asarray(col_ok)[None, None, :, :, None, :]

    qg = q.reshape(B, rows, n_cb, NA_QCOL_BLOCK, H, Dh)
    kg = k.reshape(B, rows, GRID_W, H, Dh)[:, :, kc]
    vg = v.reshape(B, rows, GRID_W, H, Dh)[:, :, kc]

    def row_step(r):
        rs = jnp.clip(r - kh // 2, 0, rows - kh)
        q_r = lax.dynamic_index_in_dim(qg, r, axis=1, keepdims=False)
        k_r = lax.dynamic_slice_in_dim(kg, rs, kh, axis=1)
        v_r = lax.dynamic_slice_in_dim(vg, rs, kh, axis=1)
        s = jnp.einsum('bjqhd,bijkhd->bhjqik', q_r, k_r,
                       preferred_element_type=jnp.float32) * scale
        dr_idx = rs + jnp.arange(kh) - r + NA_ROWS_MAX - 1
        bias = jnp.take(col_bias, dr_idx, axis=1).transpose(0, 2, 3, 1, 4)
        s = jnp.where(col_ok, s + bias[None], NEG_INF)
        pr = jax.nn.softmax(s, axis=(-2, -1))
        return jnp.einsum('bhjqik,bijkhd->bjqhd', pr.astype(v.dtype), v_r)

    out = lax.map(row_step, jnp.arange(rows))
    return out.transpose(1, 0, 2, 3, 4, 5).reshape(B, S, H * Dh)

def axial_rope(x):
    S = x.shape[1]
    t = jnp.arange(S)
    half = x.shape[-1] // 2
    inv_freq = ROPE_THETA ** (-jnp.arange(0, half, 2, dtype=jnp.float32) / half)
    xf = x.astype(jnp.float32)

    def rot(xs, pos):
        ang = pos.astype(jnp.float32)[:, None] * inv_freq[None, :]
        cos = jnp.concatenate([jnp.cos(ang), jnp.cos(ang)], axis=-1)[None, :, None, :]
        sin = jnp.concatenate([jnp.sin(ang), jnp.sin(ang)], axis=-1)[None, :, None, :]
        x1, x2 = jnp.split(xs, 2, axis=-1)
        return xs * cos + jnp.concatenate([-x2, x1], axis=-1) * sin

    y = jnp.concatenate([rot(xf[..., :half], t // GRID_W), rot(xf[..., half:], t % GRID_W)], axis=-1)
    return y.astype(x.dtype)

def gqa_attention(q, k, v):
    B, S, Hq, Dh = q.shape
    Hkv = k.shape[2]
    G = Hq // Hkv
    nb = S // Q_BLOCK
    scale = 1.0 / math.sqrt(Dh)
    qb = q.reshape(B, nb, Q_BLOCK, Hkv, G, Dh).transpose(1, 0, 2, 3, 4, 5)

    def block(q_blk):
        s = jnp.einsum('bqhgd,bkhd->bhgqk', q_blk, k, preferred_element_type=jnp.float32) * scale
        pr = jax.nn.softmax(s, axis=-1)
        return jnp.einsum('bhgqk,bkhd->bqhgd', pr.astype(v.dtype), v)

    o = lax.map(block, qb)
    return o.transpose(1, 0, 2, 3, 4, 5).reshape(B, S, Hq * Dh)

def encoder_layer(h, p_l, g_pre_mix, w_in, rpb, g_q, g_k, w_branch_a, w_branch_b, w_out,
                  g_post_mix, g_pre_ffn, w_ffn_in, w_ffn_out, g_post_ffn, w_ple, w_ple_gate, g_ple):
    B, S, _ = h.shape
    xn = rmsnorm(h, g_pre_mix)
    proj = xn @ w_in
    offs = np.cumsum([NA_WIDTH, NA_WIDTH, NA_WIDTH, GQA_Q_WIDTH, GQA_KV_WIDTH, GQA_KV_WIDTH, D_MODEL])
    qa, ka, va, qb, kb, vb, gate_a, gate_b = jnp.split(proj, offs, axis=-1)
    qa = qa.reshape(B, S, NA_HEADS, HEAD_DIM)
    ka = ka.reshape(B, S, NA_HEADS, HEAD_DIM)
    va = va.reshape(B, S, NA_HEADS, HEAD_DIM)
    qb = axial_rope(rmsnorm(qb.reshape(B, S, GQA_Q_HEADS, HEAD_DIM), g_q))
    kb = axial_rope(rmsnorm(kb.reshape(B, S, GQA_KV_HEADS, HEAD_DIM), g_k))
    vb = vb.reshape(B, S, GQA_KV_HEADS, HEAD_DIM)
    ya = neighbourhood_attention(qa, ka, va, rpb) @ w_branch_a
    yb = gqa_attention(qb, kb, vb) @ w_branch_b
    mix = (jax.nn.sigmoid(gate_a) * ya + jax.nn.sigmoid(gate_b) * yb) @ w_out
    h = h + rmsnorm(mix, g_post_mix)
    gu = rmsnorm(h, g_pre_ffn) @ w_ffn_in
    g, u = jnp.split(gu, 2, axis=-1)
    h = h + rmsnorm((jax.nn.silu(g) * u) @ w_ffn_out, g_post_ffn)
    e = p_l @ w_ple
    h = h + rmsnorm(jax.nn.sigmoid(h @ w_ple_gate) * e, g_ple)
    return h

def setup_inputs(seed: int = 0) -> dict:
    key = jax.random.key(seed)
    ks = jax.random.split(key, 24)
    f32 = jnp.float32

    def w(k, shape, fan_in):
        return jax.random.normal(k, shape, f32) * fan_in ** -0.5

    def gain(k, shape):
        return 1.0 + 0.1 * jax.random.normal(k, shape, f32)

    return {
        "x_prompt": jax.random.normal(ks[0], (BATCH, SEQ, D_MODEL), f32),
        "x_sample": jax.random.normal(ks[1], (DEC_BATCH, DEC_SEQ, D_MODEL), f32),
        "p_prompt": jax.random.normal(ks[2], (DEPTH, BATCH, SEQ, PLE_DIM), f32),
        "p_sample": jax.random.normal(ks[3], (DEPTH, DEC_BATCH, DEC_SEQ, PLE_DIM), f32),
        "g_pre_mix": gain(ks[4], (DEPTH, D_MODEL)),
        "w_in": w(ks[5], (DEPTH, D_MODEL, IN_COLS), D_MODEL),
        "rpb": 0.1 * jax.random.normal(ks[6], (DEPTH, NA_HEADS, 2 * NA_ROWS_MAX - 1, 2 * NA_COLS - 1), f32),
        "g_q": gain(ks[7], (DEPTH, HEAD_DIM)),
        "g_k": gain(ks[8], (DEPTH, HEAD_DIM)),
        "w_branch_a": w(ks[9], (DEPTH, NA_WIDTH, D_MODEL), NA_WIDTH),
        "w_branch_b": w(ks[10], (DEPTH, GQA_Q_WIDTH, D_MODEL), GQA_Q_WIDTH),
        "w_out": w(ks[11], (DEPTH, D_MODEL, D_MODEL), D_MODEL),
        "g_post_mix": gain(ks[12], (DEPTH, D_MODEL)),
        "g_pre_ffn": gain(ks[13], (DEPTH, D_MODEL)),
        "w_ffn_in": w(ks[14], (DEPTH, D_MODEL, 2 * D_FF), D_MODEL),
        "w_ffn_out": w(ks[15], (DEPTH, D_FF, D_MODEL), D_FF),
        "g_post_ffn": gain(ks[16], (DEPTH, D_MODEL)),
        "w_ple": w(ks[17], (DEPTH, PLE_DIM, D_MODEL), PLE_DIM),
        "w_ple_gate": w(ks[18], (DEPTH, D_MODEL, D_MODEL), D_MODEL),
        "g_ple": gain(ks[19], (DEPTH, D_MODEL)),
    }

def reference(x_prompt, x_sample, p_prompt, p_sample, g_pre_mix, w_in, rpb, g_q, g_k,
              w_branch_a, w_branch_b, w_out, g_post_mix, g_pre_ffn, w_ffn_in, w_ffn_out,
              g_post_ffn, w_ple, w_ple_gate, g_ple):
    h_p = x_prompt
    h_s = x_sample
    for i in range(DEPTH):
        lw = (g_pre_mix[i], w_in[i], rpb[i], g_q[i], g_k[i], w_branch_a[i], w_branch_b[i], w_out[i],
              g_post_mix[i], g_pre_ffn[i], w_ffn_in[i], w_ffn_out[i], g_post_ffn[i],
              w_ple[i], w_ple_gate[i], g_ple[i])
        h_p = encoder_layer(h_p, p_prompt[i], *lw)
        h_s = encoder_layer(h_s, p_sample[i], *lw)
    y_prompt = h_p
    y_sample = h_s
    return (y_prompt, y_sample)


_drawn_inputs = setup_inputs


def setup_inputs(seed=0):
    import zlib

    import numpy as np

    out = dict(_drawn_inputs(seed))
    spreads = {}
    factors = {}
    for name, (base, spread) in spreads.items():
        noise = np.random.default_rng([zlib.crc32(name.encode()), seed]).standard_normal(out[name].shape)
        drawn = base * np.exp(spread * noise) if base else spread * noise
        out[name] = __import__('jax').numpy.asarray(drawn.astype(out[name].dtype))
    for name, factor in factors.items():
        out[name] = (out[name] * factor).astype(out[name].dtype)
    return out
```

```python
from contextlib import ExitStack

import numpy as np

import concourse.bass as bass
from concourse import mybir

F32 = mybir.dt.float32
F32R = mybir.dt.float32r
ALU = mybir.AluOpType
ACT = mybir.ActivationFunctionType
AX_X = mybir.AxisListType.X

P = 128
T = 512
GROUPS = 2
S = T // GROUPS
TT = T // P
D = 2048
KT = D // P
DH = 128
HEADS = 8
KV = 2
PER_KV = HEADS // KV
GRID = 64
NA_COLS = 16
NA_ROWS_MAX = 8
DF = 5632
FT = DF // P
CH = 4
CHUNKS = FT // CH
PLE = 256
EPS = 1e-6
SCALE = DH ** -0.5
NEG = -1e30
HALF = 8
PADC = 128
E_ROWS = 6

C_QA, C_KA, C_VA = 0, HEADS * DH, 2 * HEADS * DH
C_QB = 3 * HEADS * DH
C_KB = C_QB + HEADS * DH
C_VB = C_KB + KV * DH
C_GA = C_VB + KV * DH
C_GB = C_GA + D

HEAD_UNITS = 8
GROUP_UNITS = 2 + PER_KV * HEAD_UNITS
N_BRANCH = KV * GROUP_UNITS
N_OUT = N_BRANCH + KT
N_EMBED_A = N_OUT + KT
N_FFN = N_EMBED_A + 1
IN_UNITS, OUT_UNITS = 2 * CH, KT // 4
CHUNK_UNITS = IN_UNITS + OUT_UNITS
N_EMBED_B = N_FFN + CHUNKS * CHUNK_UNITS
N_PLE = N_EMBED_B + 1
N_END = N_PLE + KT

NORM_MIX = 1 + KV * (1 + PER_KV)
NORM_FFN_IN = NORM_MIX + 1
NORM_FFN = NORM_MIX + 2
NORM_PLE = NORM_MIX + 3

G_PRE, G_POST, G_FFN, G_PFFN, G_PLE = range(5)
B_SCORE, B_PT, B_NORM, B_MISC = 2, 4, 6, 7
IN_BANKS = (4, 5, 6, 7, 0, 1, 2, 3)
OUT_BANKS = (4, 0, 4, 0)
EMBED_A_BANKS = ((2, 3, 4, 5), (0, 1, 2, 3))
EMBED_B_BANKS = ((4, 5, 6, 7), (1, 2, 3, 4))
PLE_BANKS = (6, 7)
BIAS_PARTS = HEADS * E_ROWS * GRID // T


def shape_constants():
    half = DH // 2
    inv = (np.float32(10000.0) ** (-np.arange(0, half, 2, dtype=np.float32) / np.float32(half))).astype(np.float32)
    t = np.arange(T) % S
    ang = np.zeros((P, T), np.float32)
    for d in range(DH):
        pos = (t // GRID if d < half else t % GRID).astype(np.float32)
        ang[d] = pos * inv[d % (half // 2)]
    cos, sin = np.cos(ang).astype(np.float32), np.sin(ang).astype(np.float32)
    rot = np.zeros((P, P), np.float32)
    for m in range(P):
        if m % half < half // 2:
            rot[m + half // 2, m] = -1.0
        else:
            rot[m - half // 2, m] = 1.0
    flip = np.zeros((P, P), np.float32)
    for m in range(P):
        flip[(m // GRID) * GRID + GRID - 1 - m % GRID, m] = 1.0
    qc = np.arange(P)[:, None] % GRID
    kc = np.arange(GRID)[None, :]
    first = np.clip(qc - NA_COLS // 2, 0, GRID - NA_COLS)
    mask = np.where((kc >= first) & (kc < first + NA_COLS), 0.0, NEG).astype(np.float32)
    return {"rope_cos": cos, "rope_sin": sin, "rope_rot": rot, "flip": flip, "col_mask": mask,
            "ident": np.eye(P, dtype=np.float32)}


def build(nc, xT, pT, gains, gains_qk, w_in, rpb, w_branch_a, w_branch_b, w_out, w_ffn_in, w_ffn_out,
          w_ple, w_ple_gate, rope_cos, rope_sin, rope_rot, flip, col_mask, ident, yT):
    ctx = ExitStack()
    with ctx:
        KB = 1024
        R_X = 16512
        R_Q = R_X + 64 * KB
        R_O = R_Q + 64 * KB
        R_W = R_O + 32 * KB
        R_S = R_W + 40 * KB

        def at(name, off, shape, dt=F32):
            return nc.alloc_sbuf_tensor_at(name, shape, dt, offset=off)

        act_hi = at("act_hi", R_X, [P, KT, T], F32R)
        act_lo = at("act_lo", R_X + 32 * KB, [P, KT, T], F32R)
        bias = at("bias", R_Q, [P, HEADS, E_ROWS, GRID])
        cos_t = at("cos_t", R_Q + 12 * KB, [P, T])
        sin_t = at("sin_t", R_Q + 14 * KB, [P, T])
        k_rope = at("k_rope", R_Q + 16 * KB, [P, T])
        vb_tok = at("vb_tok", R_Q + 18 * KB, [P, TT, DH])
        qa_f = at("qa_f", R_Q + 20 * KB, [P, T])
        ka_f = at("ka_f", R_Q + 22 * KB, [P, T])
        va_f = at("va_f", R_Q + 24 * KB, [P, T])
        va_tok = at("va_tok", R_Q + 26 * KB, [P, TT, DH])
        q_rope = at("q_rope", R_Q + 28 * KB, [P, T])
        qk_raw = at("qk_raw", R_Q + 30 * KB, [P, T])
        qk_gain = at("qk_gain", R_Q + 32 * KB, [P, T])
        qk_sq = at("qk_sq", R_Q + 34 * KB, [P, T])
        rope_c = at("rope_c", R_Q + 36 * KB, [P, T])
        rope_s = at("rope_s", R_Q + 38 * KB, [P, T])
        x_sq = [rope_c, rope_s]
        na_scores = at("na_scores", R_Q + 40 * KB, [P, TT, S])
        probs = at("probs", R_Q + 44 * KB, [P, TT, S])
        probs_T = at("probs_T", R_Q + 48 * KB, [P, GROUPS, 2, S])
        vb_f = at("vb_f", R_Q + 52 * KB, [P, T])
        rot_t = at("rot_t", R_Q + 54 * KB, [P, P])
        gate_out = at("gate_out", R_Q + 60 * KB, [P, 2, T])
        bias_flipped = at("bias_flipped", R_Q + 40 * KB, [P, HEADS, E_ROWS, GRID])
        flip_t = at("flip_t", R_Q + 55 * KB, [P, P])
        mask_t = at("mask_t", R_Q + 55 * KB + 512, [P, GRID])
        rpb_pad = at("rpb_pad", R_Q + 53 * KB, [HEADS * (2 * NA_ROWS_MAX - 1), PADC])
        head_hi = at("head_hi", R_Q, [P, KT, T], F32R)
        head_lo = at("head_lo", R_Q + 32 * KB, [P, KT, T], F32R)
        x_f = at("x_f", R_O, [P, KT, T])
        head_f = at("head_f", R_O, [P, KT, T])
        gate_in = at("gate_in", R_O, [P, 2, 2, T])
        mix_a = at("mix_a", R_O + 8 * KB, [P, T])
        mix_b = at("mix_b", R_O + 10 * KB, [P, T])
        resid = at("resid", R_O, [P, KT, T])
        hid_hi = at("hid_hi", R_Q, [P, CH, T], F32R)
        hid_lo = at("hid_lo", R_Q + 8 * KB, [P, CH, T], F32R)
        embed = at("embed", R_Q, [P, 8, T])
        sums = at("sums", R_Q + 16 * KB, [P, KT, T])
        p_hi = at("p_hi", R_Q + 48 * KB, [P, 2, T], F32R)
        p_lo = at("p_lo", R_Q + 52 * KB, [P, 2, T], F32R)
        p_f = at("p_f", R_Q + 56 * KB, [P, 2, T])
        tmp = at("tmp", R_Q + 56 * KB, [P, 2, T])
        sq = at("sq", R_Q + 60 * KB, [P, 2, T])
        w_raw = at("w_raw", R_W, [P, 2, HALF, P])
        w_hi = at("w_hi", R_W + 8 * KB, [P, 4, HALF, P], F32R)
        w_lo = at("w_lo", R_W + 24 * KB, [P, 4, HALF, P], F32R)
        ident_t = at("ident_t", R_S, [P, P])
        ones = at("ones", R_S + 512, [P, P])
        rstd = at("rstd", R_S + 1024, [P, T])
        sq_sum = at("sq_sum", R_S + 3 * KB, [P, T])
        diag = at("diag", R_S + 5 * KB, [P, TT, P])
        g_t = at("g_t", R_S + 7 * KB, [P, 5, KT])
        tiny = R_S + 7 * KB + 320
        gqk_t = at("gqk_t", tiny, [P, 2])
        minus_half = at("minus_half", tiny + 32, [P, TT])
        var = at("var", tiny + 64, [P, TT])
        rs = at("rs", tiny + 96, [P, TT])
        top = at("top", tiny + 128, [P, 2, TT])
        neg_top = at("neg_top", tiny + 160, [P, 2, TT])
        psum_p = at("psum_p", tiny + 192, [P, 2, TT])
        inv_p = at("inv_p", tiny + 224, [P, 2, TT])

        bank = ctx.enter_context(nc.psum_tensor("bank", [P, 8, T], F32))

        gate_dram = nc.dram_tensor("gate_dram", [KT, 2, P, T], F32, kind="Internal")
        embed_dram = nc.dram_tensor("embed_dram", [8, P, T], F32, kind="Internal")
        pad_dram = nc.dram_tensor("pad_dram", [HEADS * (2 * NA_ROWS_MAX - 1), PADC], F32, kind="Internal")

        def sem(name):
            return ctx.enter_context(nc.semaphore(name))

        raw_landed = [sem("raw_landed0"), sem("raw_landed1")]
        hi_ready = sem("hi_ready")
        lo_ready = sem("lo_ready")
        unit_done = sem("unit_done")
        unit_read = sem("unit_read")
        x_landed = [sem(f"x_landed{i}") for i in range(4)]
        const_landed = sem("const_landed")
        mask_landed = sem("mask_landed")
        ident_landed = sem("ident_landed")
        gains_landed = sem("gains_landed")
        ones_set = sem("ones_set")
        pad_set = sem("pad_set")
        rpb_landed = sem("rpb_landed")
        pad_stored = sem("pad_stored")
        table_landed = sem("table_landed")
        flipped = sem("flipped")
        bias_read = sem("bias_read")
        x_hi_ready = sem("x_hi_ready")
        x_lo_ready = sem("x_lo_ready")
        x_sq_ready = sem("x_sq_ready")
        x_sq_added = sem("x_sq_added")
        rstd_ready = sem("rstd_ready")
        norm_summed = sem("norm_summed")
        norm_var = sem("norm_var")
        norm_root = sem("norm_root")
        norm_diag = sem("norm_diag")
        norm_spread = sem("norm_spread")
        qk_sq_ready = sem("qk_sq_ready")
        qk_gain_ready = sem("qk_gain_ready")
        qk_rotated = sem("qk_rotated")
        rope_s_ready = sem("rope_s_ready")
        rope_c_ready = sem("rope_c_ready")
        rope_added = sem("rope_added")
        rope_done = sem("rope_done")
        vb_turned = sem("vb_turned")
        vb_tok_ready = sem("vb_tok_ready")
        score_b = sem("score_b")
        top_b = sem("top_b")
        neg_top_b = sem("neg_top_b")
        exp_b = sem("exp_b")
        inv_b = sem("inv_b")
        probs_b = sem("probs_b")
        turned_b = sem("turned_b")
        pT_b = sem("pT_b")
        head_b = sem("head_b")
        head_b_read = sem("head_b_read")
        score_a = sem("score_a")
        biased_a = sem("biased_a")
        top_a = sem("top_a")
        neg_top_a = sem("neg_top_a")
        exp_a = sem("exp_a")
        inv_a = sem("inv_a")
        probs_a = sem("probs_a")
        va_turned = sem("va_turned")
        va_tok_ready = sem("va_tok_ready")
        turned_a = sem("turned_a")
        pT_a = sem("pT_a")
        head_a = sem("head_a")
        head_a_read = sem("head_a_read")
        gate_stored = [sem("gate_stored0"), sem("gate_stored1")]
        head_hi_ready = sem("head_hi_ready")
        head_lo_ready = sem("head_lo_ready")
        gate_landed = [sem("gate_landed0"), sem("gate_landed1")]
        gates_open = sem("gates_open")
        mixed = sem("mixed")
        mix_hi_ready = sem("mix_hi_ready")
        mix_lo_ready = sem("mix_lo_ready")
        resid_landed = sem("resid_landed")
        p_landed = sem("p_landed")
        p_hi_ready = sem("p_hi_ready")
        p_lo_ready = sem("p_lo_ready")
        sq_ready = sem("sq_ready")
        sq_added = sem("sq_added")
        normed = sem("normed")
        resid_ready = sem("resid_ready")
        resid_hi_ready = sem("resid_hi_ready")
        resid_lo_ready = sem("resid_lo_ready")
        h_sq_ready = sem("h_sq_ready")
        h_sq_added = sem("h_sq_added")
        embed_half = sem("embed_half")
        embed_read = sem("embed_read")
        embed_stored = sem("embed_stored")
        embed_landed = sem("embed_landed")
        sums_zero = sem("sums_zero")
        silu_ready = sem("silu_ready")
        hid_ready = sem("hid_ready")
        hid_hi_ready = sem("hid_hi_ready")
        hid_lo_ready = sem("hid_lo_ready")
        ple_sig = sem("ple_sig")
        ple_ready = sem("ple_ready")
        y_ready = sem("y_ready")
        y_stored = sem("y_stored")

        w_in_v = w_in.rearrange("(k p) n -> p k n", p=P)
        wa_v = w_branch_a.rearrange("(k p) n -> p k n", p=P)
        wb_v = w_branch_b.rearrange("(k p) n -> p k n", p=P)
        wo_v = w_out.rearrange("(k p) n -> p k n", p=P)
        wi_v = w_ffn_in.rearrange("(k p) n -> p k n", p=P)
        wf_v = w_ffn_out.rearrange("(k p) n -> p k n", p=P)
        wp_v = w_ple.rearrange("(k p) n -> p k n", p=P)
        wg_v = w_ple_gate.rearrange("(k p) n -> p k n", p=P)
        x_v = xT.rearrange("(k p) t -> p k t", p=P)
        p_v = pT.rearrange("(k p) t -> p k t", p=P)
        y_v = yT.rearrange("(k p) t -> p k t", p=P)

        block = ctx.enter_context(nc.Block())

        @block.sync
        def _(sp):
            def fetch(n, half, src, shape=None):
                sp.wait_ge(lo_ready, 2 * n + half + 1)
                dst = w_raw[:, half] if shape is None else w_raw[:, half].rearrange("p s c -> p (s c)").rearrange(
                    "p (k c) -> p k c", k=shape)
                sp.dma_start(dst, src).then_inc(raw_landed[half], 16)

            def fetch_tall(n, view, col):
                for half in range(2):
                    fetch(n, half, view[:, half * HALF:(half + 1) * HALF, bass.ds(col, P)])

            for i in range(4):
                sp.dma_start(x_f[:, 4 * i:4 * i + 4], x_v[:, 4 * i:4 * i + 4]).then_inc(x_landed[i], 16)
                if i == 0:
                    fetch_tall(0, w_in_v, C_KB)
            for j in range(KV):
                n0 = j * GROUP_UNITS
                if j:
                    fetch_tall(n0, w_in_v, C_KB + j * DH)
                fetch_tall(n0 + 1, w_in_v, C_VB + j * DH)
                with sp.Fori(1, PER_KV + 1) as r:
                    n = r * HEAD_UNITS + (n0 + 2 - HEAD_UNITS)
                    h = j * PER_KV - 1
                    fetch_tall(n, w_in_v, r * DH + (C_QB + h * DH))
                    fetch_tall(n + 1, w_in_v, r * DH + (C_KA + h * DH))
                    fetch_tall(n + 2, w_in_v, r * DH + (C_QA + h * DH))
                    fetch_tall(n + 3, w_in_v, r * DH + (C_VA + h * DH))
                    for i in range(2):
                        fetch_tall(n + 4 + i, w_in_v, r * 2 * P + (C_GA + (2 * h + i) * P))
                    for i in range(2):
                        fetch_tall(n + 6 + i, w_in_v, r * 2 * P + (C_GB + (2 * h + i) * P))
            for m in range(2):
                fetch(N_BRANCH + m, 0, wa_v[:, :, m * P:(m + 1) * P])
                fetch(N_BRANCH + m, 1, wb_v[:, :, m * P:(m + 1) * P])
            for slot in range(2):
                sp.wait_ge(gate_stored[slot], 16 * KT)
            sp.wait_ge(head_lo_ready, KT)
            for slot in range(2):
                sp.dma_start(gate_in[:, slot], gate_dram.ap()[slot].rearrange("g p t -> p g t")).then_inc(
                    gate_landed[slot], 16)
            with sp.Fori(1, KT // 2) as i:
                for slot in range(2):
                    n = i * 2 + (N_BRANCH + slot)
                    fetch(n, 0, wa_v[:, :, bass.ds(i * 2 * P + slot * P, P)])
                    fetch(n, 1, wb_v[:, :, bass.ds(i * 2 * P + slot * P, P)])
                    sp.wait_ge(unit_read, n)
                    sp.dma_start(gate_in[:, slot], gate_dram.ap()[bass.ds(i * 2 + slot, 1)].rearrange(
                        "m g p t -> p (m g) t")).then_inc(gate_landed[slot], 16)
            for m in range(2):
                fetch_tall(N_OUT + m, wo_v, m * P)
            sp.wait_ge(mix_lo_ready, KT)
            sp.dma_start(p_f[:], p_v).then_inc(p_landed, 16)
            sp.dma_start(resid[:], x_v).then_inc(resid_landed, 16)
            with sp.Fori(1, KT // 2) as i:
                for m in range(2):
                    fetch_tall(i * 2 + (N_OUT + m), wo_v, i * 2 * P + m * P)

            def fetch_embed(n, first):
                for half in range(2):
                    fetch(n, half, wp_v[:, :, (first + 4 * half) * P:(first + 4 * half + 4) * P], 2)

            def fetch_in(n, f):
                for i in range(CH):
                    fetch_tall(n + 2 * i, wi_v, f * P + i * P)
                    fetch_tall(n + 2 * i + 1, wi_v, f * P + (DF + i * P))

            def fetch_out(n, f):
                for u in range(OUT_UNITS):
                    for half in range(2):
                        fetch(n + u, half, wf_v[:, bass.ds(f + 2 * half, 2), u * 4 * P:(u + 1) * 4 * P], 2)

            fetch_embed(N_EMBED_A, 0)
            fetch_in(N_FFN, 0)
            with sp.Fori(1, CHUNKS) as c:
                n = c * CHUNK_UNITS + (N_FFN - OUT_UNITS)
                fetch_out(n, c * CH - CH)
                fetch_in(n + OUT_UNITS, c * CH)
            fetch_out(N_EMBED_B - OUT_UNITS, FT - CH)
            fetch_embed(N_EMBED_B, 8)
            for m in range(2):
                fetch_tall(N_PLE + m, wg_v, m * P)
            sp.wait_ge(normed, 2 * KT)
            sp.dma_start(sums[:, 0:8], embed_dram.ap().rearrange("m p t -> p m t")).then_inc(embed_landed, 16)
            with sp.Fori(1, KT // 2) as i:
                for m in range(2):
                    fetch_tall(i * 2 + (N_PLE + m), wg_v, i * 2 * P + m * P)
            for k in range(KT):
                sp.wait_ge(y_ready, k + 1)
                sp.dma_start(y_v[:, k], resid[:, k]).then_inc(y_stored, 16)
            sp.wait_ge(y_stored, 16 * KT)

        @block.gpsimd
        def _(pool):
            def root(q):
                pool.wait_ge(norm_var, q + 1)
                nc.gpsimd.tensor_tensor(rs[:], var[:], minus_half[:], ALU.pow).then_inc(norm_root, 1)

            nc.gpsimd.memset(rpb_pad[:], 0.0).then_inc(pad_set, 1)
            nc.gpsimd.memset(ones[:], 1.0).then_inc(ones_set, 1)
            nc.gpsimd.memset(minus_half[:], -0.5).then_inc(ones_set, 1)
            for k in range(KT):
                if k % 4 == 0:
                    pool.wait_ge(x_landed[k // 4], 16)
                if k >= 2:
                    pool.wait_ge(x_sq_added, k - 1)
                nc.gpsimd.tensor_tensor(x_sq[k % 2][:], x_f[:, k], x_f[:, k], ALU.mult).then_inc(x_sq_ready, 1)
            pool.wait_ge(ones_set, 2)
            root(0)
            nc.gpsimd.memset(sq_sum[:], 0.0).then_inc(sq_added, 1)
            with pool.Fori(1, NORM_MIX) as q:
                root(q)
            root(NORM_MIX)
            for k in range(KT):
                pool.wait_ge(h_sq_ready, k + 1)
                if k == 0:
                    nc.gpsimd.tensor_copy(sq_sum[:], sq[:, 0]).then_inc(h_sq_added, 1)
                else:
                    pool.wait_ge(h_sq_added, k)
                    nc.gpsimd.tensor_tensor(sq_sum[:], sq_sum[:], sq[:, k % 2], ALU.add).then_inc(h_sq_added, 1)
            root(NORM_FFN_IN)
            nc.gpsimd.memset(sums[:], 0.0).then_inc(sums_zero, 1)
            nc.gpsimd.memset(sq_sum[:], 0.0).then_inc(sq_added, 1)
            root(NORM_FFN)
            nc.gpsimd.memset(sq_sum[:], 0.0).then_inc(sq_added, 1)
            root(NORM_PLE)

        @block.scalar
        def _(act):
            def split_hi(n, par, half, free=True):
                act.wait_ge(raw_landed[half], 16 * n + 16)
                nc.scalar.copy(w_hi[:, 2 * par + half], w_raw[:, half]).then_inc(hi_ready, 1)

            def next_hi(n, par):
                act.wait_ge(unit_done, n + 1)
                for half in range(2):
                    split_hi(n + 2, par, half)

            act.dma_start(g_t[:], gains).then_inc(gains_landed, 16)
            act.dma_start(gqk_t[:], gains_qk).then_inc(gains_landed, 16)
            act.wait_ge(pad_set, 1)
            act.dma_start(rpb_pad[:, 48:48 + 2 * NA_COLS - 1], rpb).then_inc(rpb_landed, 16)
            act.dma_start(ident_t[:], ident).then_inc(ident_landed, 16)
            act.dma_start(mask_t[:], col_mask).then_inc(mask_landed, 16)
            act.dma_start(flip_t[:], flip).then_inc(mask_landed, 16)
            act.dma_start(cos_t[:], rope_cos).then_inc(const_landed, 16)
            act.dma_start(sin_t[:], rope_sin).then_inc(const_landed, 16)
            act.dma_start(rot_t[:], rope_rot).then_inc(const_landed, 16)

            act.wait_ge(gains_landed, 32)

            def x_hi(k):
                if k % 4 == 0:
                    act.wait_ge(x_landed[k // 4], 16)
                nc.scalar.activation(act_hi[:, k], x_f[:, k], ACT.Identity,
                                     scale=g_t[:, G_PRE, k:k + 1]).then_inc(x_hi_ready, 1)

            split_hi(0, 0, 0)
            for k in range(HALF):
                x_hi(k)
            split_hi(0, 0, 1)
            for k in range(HALF, KT):
                x_hi(k)
            act.wait_ge(rpb_landed, 16)
            act.dma_start(pad_dram.ap(), rpb_pad[:]).then_inc(pad_stored, 16)
            split_hi(1, 1, 0)
            split_hi(1, 1, 1)
            act.wait_ge(pad_stored, 16)
            rows = 2 * NA_ROWS_MAX - 1
            for h in range(HEADS):
                for rl in range(2):
                    first = (h * rows + NA_ROWS_MAX - 1 - 2 - rl) * PADC
                    act.dma_start(bias_flipped[rl * GRID:(rl + 1) * GRID, h],
                                  bass.AP(pad_dram, first, [[1, GRID], [PADC, E_ROWS], [1, GRID]])).then_inc(
                                      table_landed, 16)

            def head_norm_inputs(n, g):
                act.wait_ge(unit_read, n + 2)
                nc.scalar.activation(qk_sq[:], qk_raw[:], ACT.Square).then_inc(qk_sq_ready, 1)
                nc.scalar.activation(qk_gain[:], qk_raw[:], ACT.Identity,
                                     scale=gqk_t[:, g:g + 1]).then_inc(qk_gain_ready, 1)

            def exps(ready, value, src, which, scale, done):
                act.wait_ge(ready, value)
                for t in range(TT):
                    ins = nc.scalar.activation(probs[:, t], src[:, t], ACT.Exp, bias=neg_top[:, which, t:t + 1],
                                               scale=scale, accum_out=psum_p[:, which, t:t + 1])
                    ins.then_inc(done, 1)

            def evacuate_pT(ready, value, done):
                act.wait_ge(ready, value)
                for g in range(GROUPS):
                    nc.scalar.copy(probs_T[:, g].rearrange("p a b -> p (a b)"), bank[:, B_PT + g]).then_inc(done, 1)

            def store_gate(n, slot, m, which):
                act.wait_ge(unit_read, n + 2)
                act.dma_start(gate_dram.ap()[bass.ds(m, 1), which].rearrange("m p t -> p (m t)"),
                              gate_out[:, slot]).then_inc(gate_stored[slot], 16)

            scores = bank[:, B_SCORE:B_SCORE + 2].rearrange("p g (q s) -> p (g q) s", q=2)
            for j in range(KV):
                n0 = j * GROUP_UNITS
                next_hi(n0, 0)
                head_norm_inputs(n0, 1)
                next_hi(n0 + 1, 1)
                with act.Fori(0, PER_KV) as r:
                    n = r * HEAD_UNITS + (n0 + 2)
                    hd = r + j * PER_KV
                    next_hi(n, 0)
                    head_norm_inputs(n, 0)
                    next_hi(n + 1, 1)
                    next_hi(n + 2, 0)
                    exps(neg_top_b, hd + 1, scores, 0, SCALE, exp_b)
                    next_hi(n + 3, 1)
                    evacuate_pT(turned_b, hd + 1, pT_b)
                    exps(neg_top_a, hd + 1, na_scores, 1, 1.0, exp_a)
                    next_hi(n + 4, 0)
                    store_gate(n + 4, 0, r * 2 + 2 * j * PER_KV, 0)
                    next_hi(n + 5, 1)
                    store_gate(n + 5, 1, r * 2 + (2 * j * PER_KV + 1), 0)
                    evacuate_pT(turned_a, hd + 1, pT_a)
                    next_hi(n + 6, 0)
                    store_gate(n + 6, 0, r * 2 + 2 * j * PER_KV, 1)
                    act.wait_ge(unit_done, n + 8)
                    store_gate(n + 7, 1, r * 2 + (2 * j * PER_KV + 1), 1)
                    next_hi(n + 7, 1)
            for k in range(KT):
                if k == 0:
                    act.wait_ge(head_a_read, HEADS)
                nc.scalar.copy(head_hi[:, k], head_f[:, k]).then_inc(head_hi_ready, 1)
            with act.Fori(0, KT // 2) as i:
                for slot in range(2):
                    n = i * 2 + (N_BRANCH + slot)
                    act.wait_ge(gate_landed[slot], i * 16 + 16)
                    nc.scalar.activation(gate_in[:, slot], gate_in[:, slot], ACT.Sigmoid).then_inc(gates_open, 1)
                    next_hi(n, slot)
                    act.wait_ge(mixed, i * 2 + (slot + 1))
                    nc.scalar.copy(act_hi[:, bass.ds(i * 2 + slot, 1)], mix_a[:].rearrange(
                        "p (a t) -> p a t", a=1)).then_inc(mix_hi_ready, 1)
            act.wait_ge(p_landed, 16)
            nc.scalar.copy(p_hi[:], p_f[:]).then_inc(p_hi_ready, 1)
            with act.Fori(0, KT // 2) as i:
                for m in range(2):
                    n = i * 2 + (N_OUT + m)
                    act.wait_ge(unit_read, n + 2)
                    act.wait_ge(sq_added, i * 2 + (m + 1))
                    nc.scalar.activation(sq[:, m:m + 1], sums[:, bass.ds(i * 2 + m, 1)], ACT.Square).then_inc(sq_ready, 1)
                    next_hi(n, m)

            def embed_part(first, count, banks):
                for i in range(count):
                    nc.scalar.copy(embed[:, first + i], bank[:, banks[i]]).then_inc(embed_read, 1)

            act.wait_ge(embed_half, 1)
            embed_part(0, 4, EMBED_A_BANKS[0])
            act.wait_ge(unit_done, N_EMBED_A + 1)
            embed_part(4, 4, EMBED_A_BANKS[1])
            for half in range(2):
                split_hi(N_EMBED_A + 2, 0, half)
            act.wait_ge(embed_read, 8)
            act.dma_start(embed_dram.ap().rearrange("m p t -> p m t"), embed[:]).then_inc(embed_stored, 16)
            for k in range(KT):
                act.wait_ge(resid_ready, k + 1)
                nc.scalar.activation(act_hi[:, k], resid[:, k], ACT.Identity,
                                     scale=g_t[:, G_FFN, k:k + 1]).then_inc(resid_hi_ready, 1)
                if k >= 2:
                    act.wait_ge(h_sq_added, k - 1)
                nc.scalar.activation(sq[:, k % 2], resid[:, k], ACT.Square).then_inc(h_sq_ready, 1)

            def ffn_in(n, f, first=False):
                for i in range(CH):
                    par = (N_FFN + 2 * i) % 2
                    next_hi(n + 2 * i, par)
                    act.wait_ge(unit_read, n + 2 * i + 1)
                    nc.scalar.activation(tmp[:, 0], tmp[:, 0], ACT.Silu).then_inc(silu_ready, 1)
                    act.wait_ge(unit_done, n + 2 * i + 2)
                    split_hi(n + 2 * i + 3, 1 - par, 0)
                    if first and i == 0:
                        act.wait_ge(embed_stored, 16)
                    act.wait_ge(hid_ready, f + i + 1)
                    nc.scalar.copy(hid_hi[:, i], sq[:, 0]).then_inc(hid_hi_ready, 1)
                    split_hi(n + 2 * i + 3, 1 - par, 1)

            def ffn_out(n):
                for u in range(OUT_UNITS):
                    next_hi(n + u, (N_FFN + u) % 2)

            ffn_in(N_FFN, 0, True)
            with act.Fori(1, CHUNKS) as c:
                n = c * CHUNK_UNITS + (N_FFN - OUT_UNITS)
                ffn_out(n)
                ffn_in(n + OUT_UNITS, c * CH)
            for u in range(OUT_UNITS):
                n = N_EMBED_B - OUT_UNITS + u
                next_hi(n, n % 2)
                act.wait_ge(unit_read, n + 1)
                for i in range(4):
                    k = 4 * u + i
                    act.wait_ge(sq_added, KT + k + 1)
                    nc.scalar.activation(sq[:, k % 2], sums[:, k], ACT.Square).then_inc(sq_ready, 1)
            act.wait_ge(embed_half, 2)
            embed_part(0, 4, EMBED_B_BANKS[0])
            act.wait_ge(unit_done, N_EMBED_B + 1)
            embed_part(4, 4, EMBED_B_BANKS[1])
            for half in range(2):
                split_hi(N_EMBED_B + 2, (N_EMBED_B + 2) % 2, half)
            for k in range(KT):
                act.wait_ge(resid_ready, KT + k + 1)
                nc.scalar.copy(act_hi[:, k], resid[:, k]).then_inc(resid_hi_ready, 1)

            def ple_tile(n, m_done, par, m_at, more=True):
                if more:
                    next_hi(n, par)
                act.wait_ge(unit_read, n)
                nc.scalar.activation(tmp[:, 0], tmp[:, 0], ACT.Sigmoid).then_inc(ple_sig, 1)
                act.wait_ge(ple_ready, m_done + 1)
                act.wait_ge(sq_added, m_done + (2 * KT + 3))
                nc.scalar.activation(sq[:, par:par + 1], m_at, ACT.Square).then_inc(sq_ready, 1)

            with act.Fori(0, KT // 2 - 1) as i:
                for m in range(2):
                    ple_tile(i * 2 + (N_PLE + m), i * 2 + m, (N_PLE + m) % 2, sums[:, bass.ds(i * 2 + m, 1)])
            for m in range(KT - 2, KT):
                ple_tile(N_PLE + m, m, (N_PLE + m) % 2, sums[:, m:m + 1], False)

        @block.vector
        def _(dve):
            def split_lo(n, par, half):
                dve.wait_ge(hi_ready, 2 * n + half + 1)
                nc.vector.tensor_tensor(w_lo[:, 2 * par + half], w_raw[:, half],
                                        w_hi[:, 2 * par + half].bitcast(F32), ALU.subtract).then_inc(lo_ready, 1)

            def next_lo(n, par):
                for half in range(2):
                    split_lo(n + 2, par, half)

            def mean_square(q, width, src_bank):
                dve.wait_ge(norm_summed, q + 1)
                nc.vector.tensor_scalar(var[:], bank[:, src_bank, 0:TT], 1.0 / width, EPS, ALU.mult,
                                        ALU.add).then_inc(norm_var, 1)

            def diagonal(q, first=False):
                dve.wait_ge(norm_root, q + 1)
                if not first:
                    dve.wait_ge(norm_spread, q)
                nc.vector.tensor_tensor(diag[:], ident_t[:].unsqueeze(1).to_broadcast([P, TT, P]),
                                        rs[:].unsqueeze(2).to_broadcast([P, TT, P]), ALU.mult).then_inc(norm_diag, 1)

            def evacuate(n, par, dst):
                dve.wait_ge(unit_done, n + 1)
                nc.vector.tensor_tensor(dst, bank[:, par], rstd[:], ALU.mult).then_inc(unit_read, 1)

            nc.vector.memset(top[:], 0.0).then_inc(lo_ready, 1)
            nc.vector.memset(neg_top[:], 0.0).then_inc(lo_ready, 1)
            nc.vector.memset(inv_p[:], 0.0).then_inc(unit_read, 1)
            dve.wait_ge(gains_landed, 32)

            def x_lo(k):
                dve.wait_ge(x_hi_ready, k + 1)
                nc.vector.scalar_tensor_tensor(act_lo[:, k], x_f[:, k], g_t[:, G_PRE, k:k + 1],
                                               act_hi[:, k].bitcast(F32), ALU.mult, ALU.subtract).then_inc(x_lo_ready, 1)
                dve.wait_ge(x_sq_ready, k + 1)
                if k == 0:
                    nc.vector.tensor_copy(sq_sum[:], x_sq[0][:]).then_inc(x_sq_added, 1)
                else:
                    dve.wait_ge(x_sq_added, k)
                    nc.vector.tensor_tensor(sq_sum[:], sq_sum[:], x_sq[k % 2][:], ALU.add).then_inc(x_sq_added, 1)

            split_lo(0, 0, 0)
            for k in range(HALF):
                x_lo(k)
            split_lo(0, 0, 1)
            for k in range(HALF, KT):
                x_lo(k)
            split_lo(1, 1, 0)
            split_lo(1, 1, 1)
            mean_square(0, D, B_NORM)
            dve.wait_ge(ident_landed, 16)
            diagonal(0, True)
            dve.wait_ge(norm_spread, 1)
            nc.vector.tensor_copy(rstd[:], bank[:, B_NORM]).then_inc(rstd_ready, 1)
            dve.wait_ge(rstd_ready, 1)

            def rope(e, q, dst):
                mean_square(q, DH, B_NORM)
                dve.wait_ge(qk_rotated, e + 1)
                nc.vector.tensor_tensor(rope_s[:], bank[:, B_MISC], sin_t[:], ALU.mult).then_inc(rope_s_ready, 1)
                diagonal(q)
                dve.wait_ge(qk_gain_ready, e + 1)
                nc.vector.tensor_tensor(rope_c[:], qk_gain[:], cos_t[:], ALU.mult).then_inc(rope_c_ready, 1)
                dve.wait_ge(rope_c_ready, e + 1)
                nc.vector.tensor_tensor(rope_c[:], rope_c[:], rope_s[:], ALU.add).then_inc(rope_added, 1)
                dve.wait_ge(rope_added, e + 1)
                dve.wait_ge(norm_spread, q + 1)
                nc.vector.tensor_tensor(dst[:], rope_c[:], bank[:, B_NORM], ALU.mult).then_inc(rope_done, 1)

            def normalise(exp_sem, value, which, inv_sem, done):
                dve.wait_ge(exp_sem, value * TT)
                nc.vector.reciprocal(inv_p[:, which], psum_p[:, which]).then_inc(inv_sem, 1)
                dve.wait_ge(inv_sem, value)
                for t in range(TT):
                    nc.vector.tensor_scalar(probs[:, t], probs[:, t], inv_p[:, which, t:t + 1], None,
                                            ALU.mult).then_inc(done, 1)

            def bias_parts(first, end):
                dve.wait_ge(mask_landed, 32)
                for i in range(first, end):
                    dve.wait_ge(flipped, i + 1)
                    nc.vector.tensor_tensor(
                        bias[:].rearrange("p h e c -> p (h e) c")[:, 8 * i:8 * i + 8],
                        bank[:, B_SCORE + i % 4].rearrange("p (a c) -> p a c", c=GRID),
                        mask_t[:].unsqueeze(1).to_broadcast([P, 8, GRID]), ALU.add).then_inc(bias_read, 1)

            scores = bank[:, B_SCORE:B_SCORE + 2].rearrange("p g (q s) -> p (g q) s", q=2)
            for j in range(KV):
                n0 = j * GROUP_UNITS
                e0 = j * (PER_KV + 1)
                evacuate(n0, 0, qk_raw[:])
                next_lo(n0, 0)
                if j == 0:
                    bias_parts(0, 4)
                    dve.wait_ge(const_landed, 48)
                rope(e0, e0 + 1, k_rope)
                evacuate(n0 + 1, 1, vb_f[:])
                next_lo(n0 + 1, 1)
                if j == 0:
                    bias_parts(4, BIAS_PARTS)
                dve.wait_ge(vb_turned, j + 1)
                nc.vector.tensor_copy(vb_tok[:].rearrange("p a b -> p (a b)"), bank[:, B_PT]).then_inc(vb_tok_ready, 1)
                with dve.Fori(0, PER_KV) as r:
                    n = r * HEAD_UNITS + (n0 + 2)
                    hd = r + j * PER_KV
                    evacuate(n, 0, qk_raw[:])
                    next_lo(n, 0)
                    evacuate(n + 1, 1, ka_f[:])
                    next_lo(n + 1, 1)
                    rope(r + (e0 + 1), r + (e0 + 2), q_rope)
                    evacuate(n + 2, 0, qa_f[:])
                    next_lo(n + 2, 0)
                    dve.wait_ge(score_b, hd + 1)
                    nc.vector.tensor_reduce(top[:, 0], scores, AX_X, ALU.max).then_inc(top_b, 1)
                    dve.wait_ge(top_b, hd + 1)
                    nc.vector.tensor_scalar(neg_top[:, 0], top[:, 0], -SCALE, None, ALU.mult).then_inc(neg_top_b, 1)
                    normalise(exp_b, hd + 1, 0, inv_b, probs_b)
                    evacuate(n + 3, 1, va_f[:])
                    next_lo(n + 3, 1)
                    dve.wait_ge(score_a, hd + 1)
                    for g in range(GROUPS):
                        for qi in range(2):
                            nc.vector.scalar_tensor_tensor(
                                na_scores[:, 2 * g + qi], bank[:, B_SCORE + g, qi * S:(qi + 1) * S], SCALE,
                                bias[:].rearrange("p h e c -> p h (e c)")[
                                    :, bass.ds(hd, 1), (2 - 2 * qi) * GRID:(6 - 2 * qi) * GRID].rearrange(
                                        "p h c -> p (h c)"),
                                ALU.mult, ALU.add).then_inc(biased_a, 1)
                    dve.wait_ge(biased_a, hd * TT + TT)
                    nc.vector.tensor_reduce(top[:, 1], na_scores[:], AX_X, ALU.max).then_inc(top_a, 1)
                    dve.wait_ge(top_a, hd + 1)
                    nc.vector.tensor_scalar(neg_top[:, 1], top[:, 1], -1.0, None, ALU.mult).then_inc(neg_top_a, 1)
                    normalise(exp_a, hd + 1, 1, inv_a, probs_a)
                    evacuate(n + 4, 0, gate_out[:, 0])
                    next_lo(n + 4, 0)
                    dve.wait_ge(va_turned, hd + 1)
                    nc.vector.tensor_copy(va_tok[:].rearrange("p a b -> p (a b)"), bank[:, B_NORM]).then_inc(va_tok_ready, 1)
                    dve.wait_ge(head_b, hd + 1)
                    nc.vector.tensor_copy(head_f[:, bass.ds(hd + HEADS, 1)], bank[:, B_MISC:B_MISC + 1]).then_inc(head_b_read, 1)
                    evacuate(n + 5, 1, gate_out[:, 1])
                    next_lo(n + 5, 1)
                    dve.wait_ge(gate_stored[0], hd * 32 + 16)
                    evacuate(n + 6, 0, gate_out[:, 0])
                    next_lo(n + 6, 0)
                    dve.wait_ge(head_a, hd + 1)
                    nc.vector.tensor_copy(head_f[:, bass.ds(hd, 1)], bank[:, B_MISC:B_MISC + 1]).then_inc(head_a_read, 1)
                    dve.wait_ge(gate_stored[1], hd * 32 + 16)
                    evacuate(n + 7, 1, gate_out[:, 1])
                    next_lo(n + 7, 1)
                    for slot in range(2):
                        dve.wait_ge(gate_stored[slot], hd * 32 + 32)
            for k in range(KT):
                dve.wait_ge(head_hi_ready, k + 1)
                nc.vector.tensor_tensor(head_lo[:, k], head_f[:, k], head_hi[:, k].bitcast(F32),
                                        ALU.subtract).then_inc(head_lo_ready, 1)
            with dve.Fori(0, KT // 2) as i:
                for slot in range(2):
                    n = i * 2 + (N_BRANCH + slot)
                    m = i * 2 + slot
                    dve.wait_ge(unit_done, n + 1)
                    dve.wait_ge(gates_open, m + 1)
                    nc.vector.tensor_tensor(mix_a[:], bank[:, 2 * slot], gate_in[:, slot, 0], ALU.mult)
                    nc.vector.tensor_tensor(mix_b[:], bank[:, 2 * slot + 1], gate_in[:, slot, 1], ALU.mult).then_inc(unit_read, 1)
                    dve.wait_ge(unit_read, n + 2)
                    nc.vector.tensor_tensor(mix_a[:], mix_a[:], mix_b[:], ALU.add).then_inc(mixed, 1)
                    next_lo(n, slot)
                    dve.wait_ge(mix_hi_ready, m + 1)
                    nc.vector.tensor_tensor(act_lo[:, bass.ds(m, 1)], mix_a[:].rearrange("p (a t) -> p a t", a=1),
                                            act_hi[:, bass.ds(m, 1)].bitcast(F32), ALU.subtract).then_inc(mix_lo_ready, 1)
                    dve.wait_ge(mix_lo_ready, m + 1)
            dve.wait_ge(p_hi_ready, 1)
            nc.vector.tensor_tensor(p_lo[:], p_f[:], p_hi[:].bitcast(F32), ALU.subtract).then_inc(p_lo_ready, 1)

            def add_square(count, slot, starts):
                dve.wait_ge(sq_ready, count + 1)
                dve.wait_ge(sq_added, count + starts)
                nc.vector.tensor_tensor(sq_sum[:], sq_sum[:], sq[:, slot], ALU.add).then_inc(sq_added, 1)

            def out_tile(n, m, par, more=True):
                dve.wait_ge(unit_done, n + 1)
                nc.vector.tensor_copy(sums[:, bass.ds(m, 1)], bank[:, par:par + 1]).then_inc(unit_read, 1)
                if more:
                    next_lo(n, par)
                add_square(m, par, 1)

            with dve.Fori(0, KT // 2 - 1) as i:
                for m in range(2):
                    out_tile(i * 2 + (N_OUT + m), i * 2 + m, m)
            out_tile(N_OUT + KT - 2, KT - 2, 0)
            out_tile(N_OUT + KT - 1, KT - 1, 1, False)
            next_lo(N_OUT + KT - 1, 1)

            def residual(which, gain_in, norm_bank, gain_out):
                def scaled(k):
                    if which or k >= 2:
                        dve.wait_ge(resid_ready, which * KT + k - 1)
                    nc.vector.scalar_tensor_tensor(tmp[:, k % 2], sums[:, k], g_t[:, gain_in, k:k + 1],
                                                   bank[:, norm_bank], ALU.mult, ALU.mult).then_inc(normed, 1)

                def low(k):
                    dve.wait_ge(resid_hi_ready, which * KT + k + 1)
                    if gain_out is None:
                        nc.vector.tensor_tensor(act_lo[:, k], resid[:, k], act_hi[:, k].bitcast(F32),
                                                ALU.subtract).then_inc(resid_lo_ready, 1)
                    else:
                        nc.vector.scalar_tensor_tensor(act_lo[:, k], resid[:, k], g_t[:, gain_out, k:k + 1],
                                                       act_hi[:, k].bitcast(F32), ALU.mult,
                                                       ALU.subtract).then_inc(resid_lo_ready, 1)

                scaled(0)
                for k in range(KT):
                    if k + 1 < KT:
                        scaled(k + 1)
                    dve.wait_ge(normed, which * KT + k + 1)
                    nc.vector.tensor_tensor(resid[:, k], resid[:, k], tmp[:, k % 2], ALU.add).then_inc(resid_ready, 1)
                    if k:
                        low(k - 1)
                low(KT - 1)

            mean_square(NORM_MIX, D, B_NORM)
            diagonal(NORM_MIX)
            dve.wait_ge(resid_landed, 16)
            dve.wait_ge(norm_spread, NORM_MIX + 1)
            residual(0, G_POST, B_NORM, G_FFN)
            next_lo(N_EMBED_A, N_EMBED_A % 2)
            mean_square(NORM_FFN_IN, D, B_MISC)
            diagonal(NORM_FFN_IN)
            dve.wait_ge(norm_spread, NORM_FFN_IN + 1)
            nc.vector.tensor_copy(rstd[:], bank[:, B_MISC]).then_inc(rstd_ready, 1)
            dve.wait_ge(rstd_ready, 2)

            def ffn_in(n, f):
                for i in range(CH):
                    par = (N_FFN + 2 * i) % 2
                    b = IN_BANKS[2 * i]
                    dve.wait_ge(unit_done, n + 2 * i + 1)
                    nc.vector.tensor_tensor(tmp[:, 0], bank[:, b], rstd[:], ALU.mult).then_inc(unit_read, 1)
                    next_lo(n + 2 * i, par)
                    dve.wait_ge(unit_done, n + 2 * i + 2)
                    nc.vector.tensor_tensor(tmp[:, 1], bank[:, IN_BANKS[2 * i + 1]], rstd[:], ALU.mult).then_inc(unit_read, 1)
                    dve.wait_ge(silu_ready, f + i + 1)
                    dve.wait_ge(unit_read, n + 2 * i + 2)
                    if not (isinstance(f, int) and f + i == 0):
                        dve.wait_ge(hid_lo_ready, f + i)
                    nc.vector.tensor_tensor(sq[:, 0], tmp[:, 0], tmp[:, 1], ALU.mult).then_inc(hid_ready, 1)
                    split_lo(n + 2 * i + 3, 1 - par, 0)
                    dve.wait_ge(hid_hi_ready, f + i + 1)
                    nc.vector.tensor_tensor(hid_lo[:, i], sq[:, 0], hid_hi[:, i].bitcast(F32),
                                            ALU.subtract).then_inc(hid_lo_ready, 1)
                    split_lo(n + 2 * i + 3, 1 - par, 1)

            def ffn_out(n, last):
                for u in range(OUT_UNITS):
                    dve.wait_ge(unit_done, n + u + 1)
                    for i in range(4):
                        m = 4 * u + i
                        ins = nc.vector.tensor_tensor(sums[:, m], sums[:, m], bank[:, OUT_BANKS[u] + i], ALU.add)
                    ins.then_inc(unit_read, 1)
                    if last:
                        if u < OUT_UNITS - 1:
                            next_lo(n + u, (n + u) % 2)
                        for i in range(4):
                            add_square(KT + 4 * u + i, (4 * u + i) % 2, 2)
                    else:
                        next_lo(n + u, (N_FFN + u) % 2)

            ffn_in(N_FFN, 0)
            dve.wait_ge(sums_zero, 1)
            with dve.Fori(1, CHUNKS) as c:
                n = c * CHUNK_UNITS + (N_FFN - OUT_UNITS)
                ffn_out(n, False)
                ffn_in(n + OUT_UNITS, c * CH)
            ffn_out(N_EMBED_B - OUT_UNITS, True)
            next_lo(N_EMBED_B - 1, (N_EMBED_B - 1) % 2)
            mean_square(NORM_FFN, D, 0)
            diagonal(NORM_FFN)
            dve.wait_ge(norm_spread, NORM_FFN + 1)
            residual(1, G_PFFN, 0, None)
            next_lo(N_EMBED_B, N_EMBED_B % 2)
            dve.wait_ge(embed_landed, 16)
            dve.wait_ge(embed_read, 16)

            def ple_tile(n, m, par, slot, emb, more=True):
                dve.wait_ge(unit_done, n + 1)
                nc.vector.tensor_copy(tmp[:, 0], bank[:, PLE_BANKS[slot]]).then_inc(unit_read, 1)
                if more:
                    next_lo(n, par)
                dve.wait_ge(ple_sig, m + 1)
                nc.vector.tensor_tensor(sums[:, bass.ds(m, 1)], tmp[:, 0:1], emb, ALU.mult).then_inc(ple_ready, 1)
                add_square(m + 2 * KT, par, 3)

            with dve.Fori(0, 4) as i:
                for s in range(2):
                    m = i * 2 + s
                    ple_tile(i * 2 + (N_PLE + s), m, (N_PLE + s) % 2, s, sums[:, bass.ds(m, 1)])
            with dve.Fori(4, 7) as i:
                for s in range(2):
                    ple_tile(i * 2 + (N_PLE + s), i * 2 + s, (N_PLE + s) % 2, s, embed[:, bass.ds(i * 2 + s - 8, 1)])
            for m in range(KT - 2, KT):
                ple_tile(N_PLE + m, m, (N_PLE + m) % 2, m % 2, embed[:, m - 8:m - 7], False)
            mean_square(NORM_PLE, D, 0)
            diagonal(NORM_PLE)
            dve.wait_ge(norm_spread, NORM_PLE + 1)
            for k in range(KT + 1):
                if k < KT:
                    if k >= 2:
                        dve.wait_ge(y_ready, k - 1)
                    nc.vector.scalar_tensor_tensor(tmp[:, k % 2], sums[:, k], g_t[:, G_PLE, k:k + 1],
                                                   bank[:, 0], ALU.mult, ALU.mult).then_inc(normed, 1)
                if k:
                    dve.wait_ge(normed, 2 * KT + k)
                    nc.vector.tensor_tensor(resid[:, k - 1], resid[:, k - 1], tmp[:, (k - 1) % 2],
                                            ALU.add).then_inc(y_ready, 1)

        @block.tensor
        def _(pe):
            def unit(n, par, terms, fillers=0, gate=None, middle=None, free=True,
                     half_sem=None):
                if free:
                    pe.wait_ge(unit_read, n - fillers)
                for idx, (b, hi, lo, start, stop) in enumerate(terms):
                    half, sub = divmod(idx, HALF)
                    slot = 2 * par + half
                    if sub == 0:
                        if half and middle:
                            middle()
                        pe.wait_ge(lo_ready, 2 * n + (half + 3))
                    if gate:
                        gate(idx)
                    nc.tensor.matmul(bank[:, b], w_hi[:, slot, sub], hi, start=start, stop=False)
                    nc.tensor.matmul(bank[:, b], w_hi[:, slot, sub], lo, start=False, stop=False)
                    last = nc.tensor.matmul(bank[:, b], w_lo[:, slot, sub], hi, start=False, stop=stop)
                    if half_sem is not None and idx == HALF - 1:
                        last.then_inc(half_sem, 1)
                last.then_inc(unit_done, 1)

            def tall(b):
                return [(b, act_hi[:, k], act_lo[:, k], k == 0, k == KT - 1) for k in range(KT)]

            def sum_tokens(src, b):
                for t in range(TT):
                    last = nc.tensor.matmul(bank[:, b, t:t + 1], src[:, t * P:(t + 1) * P], ones[:, 0:1],
                                            start=True, stop=True)
                last.then_inc(norm_summed, 1)

            def spread(q, b):
                pe.wait_ge(norm_diag, q + 1)
                nc.tensor.matmul(bank[:, b], ones[:], diag[:].rearrange("p a b -> p (a b)"), start=True,
                                 stop=True).then_inc(norm_spread, 1)

            def turn_values(src, b, done):
                for t in range(TT):
                    last = nc.tensor.transpose(bank[:, b, t * P:(t + 1) * P], src[:, t * P:(t + 1) * P], ident_t[:])
                last.then_inc(done, 1)

            def turn_probs(done):
                for g in range(GROUPS):
                    for kc in range(2):
                        for qi in range(2):
                            last = nc.tensor.transpose(bank[:, B_PT + g, kc * S + qi * P:kc * S + (qi + 1) * P],
                                                       probs[:, 2 * g + qi, kc * P:(kc + 1) * P], ident_t[:])
                last.then_inc(done, 1)

            def score(q, k, done):
                for g in range(GROUPS):
                    for qi in range(2):
                        t = 2 * g + qi
                        last = nc.tensor.matmul(bank[:, B_SCORE + g, qi * S:(qi + 1) * S], q[:, t * P:(t + 1) * P],
                                                k[:, g * S:(g + 1) * S], start=True, stop=True)
                last.then_inc(done, 1)

            def values(v_tok, done):
                for g in range(GROUPS):
                    for kc in range(2):
                        last = nc.tensor.matmul(bank[:, B_MISC, g * S:(g + 1) * S], v_tok[:, 2 * g + kc],
                                                probs_T[:, g, kc], start=kc == 0, stop=kc == 1)
                last.then_inc(done, 1)

            def sum_and_rotate(e):
                pe.wait_ge(qk_sq_ready, e + 1)
                sum_tokens(qk_sq, B_NORM)
                pe.wait_ge(qk_gain_ready, e + 1)
                nc.tensor.matmul(bank[:, B_MISC], rot_t[:], qk_gain[:], start=True, stop=True).then_inc(qk_rotated, 1)

            unit(0, 0, tall(0), gate=lambda k: pe.wait_ge(x_lo_ready, k + 1), free=False)
            pe.wait_ge(ones_set, 2)
            pe.wait_ge(x_sq_added, KT)
            sum_tokens(sq_sum, B_NORM)

            def flip_bias(first, end):
                flat = bias_flipped[:].rearrange("p h e c -> p (h e c)")
                for i in range(first, end):
                    nc.tensor.matmul(bank[:, B_SCORE + i % 4], flip_t[:], flat[:, i * T:(i + 1) * T], start=True,
                                     stop=True).then_inc(flipped, 1)

            pe.wait_ge(table_landed, 16 * 2 * HEADS)
            pe.wait_ge(mask_landed, 32)
            flip_bias(0, 4)
            spread(0, B_NORM)
            pe.wait_ge(const_landed, 48)
            for j in range(KV):
                n0 = j * GROUP_UNITS
                e0 = j * (PER_KV + 1)
                if j:
                    unit(n0, 0, tall(0))
                unit(n0 + 1, 1, tall(1), middle=lambda: sum_and_rotate(e0))
                spread(e0 + 1, B_NORM)
                if j == 0:
                    pe.wait_ge(bias_read, 4)
                    flip_bias(4, BIAS_PARTS)
                pe.wait_ge(unit_read, n0 + 3)
                turn_values(vb_f, B_PT, vb_turned)
                with pe.Fori(0, PER_KV) as r:
                    n = r * HEAD_UNITS + (n0 + 2)
                    hd = r + j * PER_KV
                    unit(n, 0, tall(0))
                    unit(n + 1, 1, tall(1))
                    sum_and_rotate(r + (e0 + 1))
                    unit(n + 2, 0, tall(0), middle=lambda: spread(r + (e0 + 2), B_NORM))
                    pe.wait_ge(rope_done, r + (e0 + 2))
                    score(q_rope, k_rope, score_b)
                    unit(n + 3, 1, tall(1))
                    pe.wait_ge(probs_b, hd * TT + TT)
                    turn_probs(turned_b)
                    pe.wait_ge(unit_read, n + 4)
                    score(qa_f, ka_f, score_a)
                    unit(n + 4, 0, tall(0))
                    pe.wait_ge(unit_read, n + 5)
                    turn_values(va_f, B_NORM, va_turned)
                    pe.wait_ge(pT_b, hd * 2 + 2)
                    pe.wait_ge(vb_tok_ready, j + 1)
                    values(vb_tok, head_b)
                    unit(n + 5, 1, tall(1))
                    pe.wait_ge(probs_a, hd * TT + TT)
                    turn_probs(turned_a)
                    unit(n + 6, 0, tall(0))
                    pe.wait_ge(pT_a, hd * 2 + 2)
                    pe.wait_ge(va_tok_ready, hd + 1)
                    pe.wait_ge(head_b_read, hd + 1)
                    values(va_tok, head_a)
                    unit(n + 7, 1, tall(1))

            def branch(slot):
                return [(2 * slot + k // HEADS, head_hi[:, k], head_lo[:, k], k % HEADS == 0,
                         k % HEADS == HEADS - 1) for k in range(KT)]

            unit(N_BRANCH, 0, branch(0), gate=lambda k: pe.wait_ge(head_lo_ready, k + 1))
            unit(N_BRANCH + 1, 1, branch(1))
            with pe.Fori(1, KT // 2) as i:
                for slot in range(2):
                    unit(i * 2 + (N_BRANCH + slot), slot, branch(slot))
            unit(N_OUT, 0, tall(0), gate=lambda k: pe.wait_ge(mix_lo_ready, k + 1))
            unit(N_OUT + 1, 1, tall(1))
            with pe.Fori(1, KT // 2) as i:
                for m in range(2):
                    unit(i * 2 + (N_OUT + m), m, tall(m))

            def embed_unit(n, banks, reads, squares, b):
                terms = [(banks[half][m], p_hi[:, k], p_lo[:, k], k == 0, k == 1)
                         for half in range(2) for k in range(2) for m in range(4)]

                def middle():
                    pe.wait_ge(sq_added, squares)
                    sum_tokens(sq_sum, b)
                    pe.wait_ge(embed_read, reads)

                unit(n, n % 2, terms, middle=middle, free=False, half_sem=embed_half)

            pe.wait_ge(p_lo_ready, 1)
            embed_unit(N_EMBED_A, EMBED_A_BANKS, 4, KT + 1, B_NORM)
            spread(NORM_MIX, B_NORM)
            unit(N_FFN, N_FFN % 2, tall(IN_BANKS[0]), gate=lambda k: pe.wait_ge(resid_lo_ready, k + 1), free=False)
            pe.wait_ge(h_sq_added, KT)
            pe.wait_ge(embed_read, 8)
            sum_tokens(sq_sum, B_MISC)
            unit(N_FFN + 1, (N_FFN + 1) % 2, tall(IN_BANKS[1]), free=False,
                 middle=lambda: spread(NORM_FFN_IN, B_MISC))

            def ffn_in(n, first):
                for i in range(first, IN_UNITS):
                    unit(n + i, (N_FFN + i) % 2, tall(IN_BANKS[i]), fillers=1)

            def ffn_out(n, f):
                for u in range(OUT_UNITS):
                    terms = [(OUT_BANKS[u] + m, hid_hi[:, k], hid_lo[:, k], k == 0, k == CH - 1)
                             for k in range(CH) for m in range(4)]

                    def gate(idx):
                        if idx % 4 == 0:
                            pe.wait_ge(hid_lo_ready, f + (idx // 4 + 1))
                    unit(n + u, (N_FFN + u) % 2, terms, fillers=1, gate=gate if u == 0 else None)

            ffn_in(N_FFN, 2)
            with pe.Fori(1, CHUNKS) as c:
                n = c * CHUNK_UNITS + (N_FFN - OUT_UNITS)
                ffn_out(n, c * CH - CH)
                ffn_in(n + OUT_UNITS, 0)
            ffn_out(N_EMBED_B - OUT_UNITS, FT - CH)
            pe.wait_ge(unit_read, N_EMBED_B - 1)
            embed_unit(N_EMBED_B, EMBED_B_BANKS, 12, 2 * KT + 2, 0)
            spread(NORM_FFN, 0)
            unit(N_PLE, N_PLE % 2, tall(PLE_BANKS[0]), gate=lambda k: pe.wait_ge(resid_lo_ready, KT + k + 1), free=False)
            unit(N_PLE + 1, (N_PLE + 1) % 2, tall(PLE_BANKS[1]), free=False)
            with pe.Fori(1, KT // 2) as i:
                for m in range(2):
                    unit(i * 2 + (N_PLE + m), (N_PLE + m) % 2, tall(PLE_BANKS[m]), fillers=2)
            pe.wait_ge(sq_added, 3 * KT + 3)
            sum_tokens(sq_sum, 0)
            spread(NORM_PLE, 0)


def kernel(x_prompt, x_sample, p_prompt, p_sample, g_pre_mix, w_in, rpb, g_q, g_k, w_branch_a, w_branch_b,
           w_out, g_post_mix, g_pre_ffn, w_ffn_in, w_ffn_out, g_post_ffn, w_ple, w_ple_gate, g_ple):
    import concourse.bacc as bacc
    from concourse.bass_utils import run_bass_kernel_spmd

    def lay(a):
        return np.ascontiguousarray(a)

    def column(g):
        return np.asarray(g)[0].reshape(KT, P).T

    feeds = {
        "xT": lay(np.concatenate([np.asarray(x_prompt)[0], np.asarray(x_sample)[0]]).T),
        "pT": lay(np.concatenate([np.asarray(p_prompt)[0, 0], np.asarray(p_sample)[0, 0]]).T),
        "gains": lay(np.stack([column(g) for g in (g_pre_mix, g_post_mix, g_pre_ffn, g_post_ffn, g_ple)], axis=1)),
        "gains_qk": lay(np.stack([np.asarray(g_q)[0], np.asarray(g_k)[0]], axis=1)),
        "w_in": lay(np.asarray(w_in)[0]),
        "rpb": lay(np.asarray(rpb)[0].reshape(-1, 2 * NA_COLS - 1)),
        "w_branch_a": lay(np.asarray(w_branch_a)[0]),
        "w_branch_b": lay(np.asarray(w_branch_b)[0]),
        "w_out": lay(np.asarray(w_out)[0]),
        "w_ffn_in": lay(np.asarray(w_ffn_in)[0]),
        "w_ffn_out": lay(np.asarray(w_ffn_out)[0]),
        "w_ple": lay(np.asarray(w_ple)[0]),
        "w_ple_gate": lay(np.asarray(w_ple_gate)[0]),
    }
    feeds.update(shape_constants())
    nc = bacc.Bacc("TRN2", target_bir_lowering=False, num_devices=1)
    aps = {name: nc.dram_tensor(name, a.shape, mybir.dt.from_np(a.dtype), kind="ExternalInput").ap()
           for name, a in feeds.items()}
    aps["yT"] = nc.dram_tensor("yT", (D, T), F32, kind="ExternalOutput").ap()
    build(nc, **aps)
    y = run_bass_kernel_spmd(nc, [feeds], core_ids=[0]).results[0]["yT"]
    return lay(y[:, :S].T)[None], lay(y[:, S:].T)[None]
```

```python
from contextlib import ExitStack

import numpy as np

import concourse.bass as bass
from concourse import mybir

F32 = mybir.dt.float32
F32R = mybir.dt.float32r
ALU = mybir.AluOpType
ACT = mybir.ActivationFunctionType
AX_X = mybir.AxisListType.X

P = 128
T = 512
GROUPS = 2
S = T // GROUPS
TT = T // P
D = 2048
KT = D // P
DH = 128
HEADS = 8
KV = 2
PER_KV = HEADS // KV
GRID = 64
NA_COLS = 16
NA_ROWS_MAX = 8
DF = 5632
FT = DF // P
CH = 4
CHUNKS = FT // CH
PLE = 256
EPS = 1e-6
SCALE = DH ** -0.5
NEG = -1e30
HALF = 8
PADC = 128
E_ROWS = 6

C_QA, C_KA, C_VA = 0, HEADS * DH, 2 * HEADS * DH
C_QB = 3 * HEADS * DH
C_KB = C_QB + HEADS * DH
C_VB = C_KB + KV * DH
C_GA = C_VB + KV * DH
C_GB = C_GA + D

HEAD_UNITS = 8
GROUP_UNITS = 2 + PER_KV * HEAD_UNITS
N_BRANCH = KV * GROUP_UNITS
N_OUT = N_BRANCH + KT
N_EMBED_A = N_OUT + KT
N_FFN = N_EMBED_A + 1
IN_UNITS, OUT_UNITS = 2 * CH, KT // 4
CHUNK_UNITS = IN_UNITS + OUT_UNITS
N_EMBED_B = N_FFN + CHUNKS * CHUNK_UNITS
N_PLE = N_EMBED_B + 1
N_END = N_PLE + KT

NORM_MIX = 1 + KV * (1 + PER_KV)
NORM_FFN_IN = NORM_MIX + 1
NORM_FFN = NORM_MIX + 2
NORM_PLE = NORM_MIX + 3

G_PRE, G_POST, G_FFN, G_PFFN, G_PLE = range(5)
B_SCORE, B_PT, B_NORM, B_MISC = 2, 4, 6, 7
IN_BANKS = (4, 5, 6, 7, 0, 1, 2, 3)
OUT_BANKS = (4, 0, 4, 0)
EMBED_A_BANKS = ((2, 3, 7, 0), (1, 2, 3, 7))
EMBED_B_BANKS = ((4, 5, 6, 7), (1, 2, 3, 4))
SCALED_BY_DVE = (0, 8)
Y_BY_POOL = (1, 4, 7, 10, 13)
Y_BY_DVE = tuple(k for k in range(KT) if k not in Y_BY_POOL)
SCALED_BY_POOL = tuple(k for k in range(KT) if k not in SCALED_BY_DVE)
PLE_BANKS = (6, 7)
X_PARTS = ((0, 1), (1, 4), (4, 8), (8, 12), (12, 16))
SPLIT_AFTER = (7, 12)
BIAS_PARTS = HEADS * E_ROWS * GRID // T


def shape_constants():
    half = DH // 2
    inv = (np.float32(10000.0) ** (-np.arange(0, half, 2, dtype=np.float32) / np.float32(half))).astype(np.float32)
    t = np.arange(T) % S
    ang = np.zeros((P, T), np.float32)
    for d in range(DH):
        pos = (t // GRID if d < half else t % GRID).astype(np.float32)
        ang[d] = pos * inv[d % (half // 2)]
    cos, sin = np.cos(ang).astype(np.float32), np.sin(ang).astype(np.float32)
    rot = np.zeros((P, P), np.float32)
    for m in range(P):
        if m % half < half // 2:
            rot[m + half // 2, m] = -1.0
        else:
            rot[m - half // 2, m] = 1.0
    flip = np.zeros((P, P), np.float32)
    for m in range(P):
        flip[(m // GRID) * GRID + GRID - 1 - m % GRID, m] = 1.0
    qc = np.arange(P)[:, None] % GRID
    kc = np.arange(GRID)[None, :]
    first = np.clip(qc - NA_COLS // 2, 0, GRID - NA_COLS)
    mask = np.where((kc >= first) & (kc < first + NA_COLS), 0.0, NEG).astype(np.float32)
    return {"rope_cos": cos, "rope_sin": sin, "rope_rot": rot, "flip": flip, "col_mask": mask,
            "ident": np.eye(P, dtype=np.float32)}


def build(nc, xT, pT, gains, gains_qk, w_in, rpb, w_branch_a, w_branch_b, w_out, w_ffn_in, w_ffn_out,
          w_ple, w_ple_gate, rope_cos, rope_sin, rope_rot, flip, col_mask, ident, yT):
    ctx = ExitStack()
    with ctx:
        KB = 1024
        R_X = 16512
        R_Q = R_X + 64 * KB
        R_O = R_Q + 64 * KB
        R_W = R_O + 32 * KB
        R_S = R_W + 40 * KB

        def at(name, off, shape, dt=F32):
            return nc.alloc_sbuf_tensor_at(name, shape, dt, offset=off)

        act_hi = at("act_hi", R_X, [P, KT, T], F32R)
        act_lo = at("act_lo", R_X + 32 * KB, [P, KT, T], F32R)
        bias = at("bias", R_Q, [P, HEADS, E_ROWS, GRID])
        cos_t = at("cos_t", R_Q + 12 * KB, [P, T])
        sin_t = at("sin_t", R_Q + 14 * KB, [P, T])
        k_rope = at("k_rope", R_Q + 16 * KB, [P, T])
        vb_tok = at("vb_tok", R_Q + 18 * KB, [P, TT, DH])
        qa_f = at("qa_f", R_Q + 20 * KB, [P, T])
        ka_f = at("ka_f", R_Q + 22 * KB, [P, T])
        va_f = at("va_f", R_Q + 24 * KB, [P, T])
        va_tok = at("va_tok", R_Q + 26 * KB, [P, TT, DH])
        q_rope = at("q_rope", R_Q + 28 * KB, [P, T])
        qk_raw = at("qk_raw", R_Q + 30 * KB, [P, T])
        qk_gain = at("qk_gain", R_Q + 32 * KB, [P, T])
        qk_sq = at("qk_sq", R_Q + 34 * KB, [P, T])
        rope_c = at("rope_c", R_Q + 36 * KB, [P, T])
        rope_s = at("rope_s", R_Q + 38 * KB, [P, T])
        x_sq = [rope_c, rope_s]
        na_scores = at("na_scores", R_Q + 40 * KB, [P, TT, S])
        probs = at("probs", R_Q + 44 * KB, [P, TT, S])
        probs_T = at("probs_T", R_Q + 48 * KB, [P, GROUPS, 2, S])
        vb_f = at("vb_f", R_Q + 52 * KB, [P, T])
        rot_t = at("rot_t", R_Q + 54 * KB, [P, P])
        gate_out = at("gate_out", R_Q + 60 * KB, [P, 2, T])
        bias_flipped = at("bias_flipped", R_Q + 40 * KB, [P, HEADS, E_ROWS, GRID])
        flip_t = at("flip_t", R_Q + 55 * KB, [P, P])
        mask_t = at("mask_t", R_Q + 55 * KB + 512, [P, GRID])
        rpb_pad = at("rpb_pad", R_Q + 53 * KB, [HEADS * (2 * NA_ROWS_MAX - 1), PADC])
        head_hi = at("head_hi", R_Q, [P, KT, T], F32R)
        head_lo = at("head_lo", R_Q + 32 * KB, [P, KT, T], F32R)
        x_f = at("x_f", R_O, [P, KT, T])
        head_f = at("head_f", R_O, [P, KT, T])
        gate_in = at("gate_in", R_O, [P, 2, 2, T])
        mix_a = at("mix_a", R_O + 8 * KB, [P, T])
        mix_b = at("mix_b", R_O + 10 * KB, [P, T])
        resid = at("resid", R_O, [P, KT, T])
        hid_hi = at("hid_hi", R_Q, [P, CH, T], F32R)
        hid_lo = at("hid_lo", R_Q + 8 * KB, [P, CH, T], F32R)
        embed = at("embed", R_Q, [P, 8, T])
        sums = at("sums", R_Q + 16 * KB, [P, KT, T])
        p_hi = at("p_hi", R_Q + 48 * KB, [P, 2, T], F32R)
        p_lo = at("p_lo", R_Q + 52 * KB, [P, 2, T], F32R)
        p_f = at("p_f", R_Q + 56 * KB, [P, 2, T])
        tmp = at("tmp", R_Q + 56 * KB, [P, 2, T])
        sq = at("sq", R_Q + 60 * KB, [P, 2, T])
        w_raw = at("w_raw", R_W, [P, 2, HALF, P])
        w_hi = at("w_hi", R_W + 8 * KB, [P, 4, HALF, P], F32R)
        w_lo = at("w_lo", R_W + 24 * KB, [P, 4, HALF, P], F32R)
        ident_t = at("ident_t", R_S, [P, P])
        ones = at("ones", R_S + 512, [P, P])
        rstd = at("rstd", R_S + 1024, [P, T])
        sq_sum = at("sq_sum", R_S + 3 * KB, [P, T])
        diag = at("diag", R_S + 5 * KB, [P, TT, P])
        g_t = at("g_t", R_S + 7 * KB, [P, 5, KT])
        tiny = R_S + 7 * KB + 320
        gqk_t = at("gqk_t", tiny, [P, 2])
        minus_half = at("minus_half", tiny + 32, [P, TT])
        var = at("var", tiny + 64, [P, TT])
        rs = at("rs", tiny + 96, [P, TT])
        top = at("top", tiny + 128, [P, 2, TT])
        neg_top = at("neg_top", tiny + 160, [P, 2, TT])
        psum_p = at("psum_p", tiny + 192, [P, 2, TT])
        inv_p = at("inv_p", tiny + 224, [P, 2, TT])

        bank = ctx.enter_context(nc.psum_tensor("bank", [P, 8, T], F32))

        gate_dram = nc.dram_tensor("gate_dram", [KT, 2, P, T], F32, kind="Internal")
        embed_dram = nc.dram_tensor("embed_dram", [8, P, T], F32, kind="Internal")
        pad_dram = nc.dram_tensor("pad_dram", [HEADS * (2 * NA_ROWS_MAX - 1), PADC], F32, kind="Internal")

        def sem(name):
            return ctx.enter_context(nc.semaphore(name))

        raw_landed = [sem("raw_landed0"), sem("raw_landed1")]
        hi_ready = sem("hi_ready")
        lo_ready = sem("lo_ready")
        unit_done = sem("unit_done")
        unit_read = sem("unit_read")
        x_landed = [sem(f"x_landed{i}") for i in range(5)]
        const_landed = sem("const_landed")
        mask_landed = sem("mask_landed")
        ident_landed = sem("ident_landed")
        gains_landed = sem("gains_landed")
        ones_set = sem("ones_set")
        pad_set = sem("pad_set")
        rpb_landed = sem("rpb_landed")
        pad_stored = sem("pad_stored")
        table_landed = sem("table_landed")
        flipped = sem("flipped")
        bias_read = sem("bias_read")
        x_hi_ready = sem("x_hi_ready")
        x_lo_ready = sem("x_lo_ready")
        x_sq_ready = sem("x_sq_ready")
        x_sq_added = sem("x_sq_added")
        rstd_ready = sem("rstd_ready")
        norm_summed = sem("norm_summed")
        norm_var = sem("norm_var")
        norm_root = sem("norm_root")
        norm_diag = sem("norm_diag")
        norm_spread = sem("norm_spread")
        qk_sq_ready = sem("qk_sq_ready")
        qk_gain_ready = sem("qk_gain_ready")
        qk_rotated = sem("qk_rotated")
        rope_s_ready = sem("rope_s_ready")
        rope_c_ready = sem("rope_c_ready")
        rope_added = sem("rope_added")
        rope_done = sem("rope_done")
        vb_turned = sem("vb_turned")
        vb_tok_ready = sem("vb_tok_ready")
        score_b = sem("score_b")
        top_b = sem("top_b")
        neg_top_b = sem("neg_top_b")
        exp_b = sem("exp_b")
        inv_b = sem("inv_b")
        probs_b = sem("probs_b")
        turned_b = sem("turned_b")
        pT_b = sem("pT_b")
        head_b = sem("head_b")
        head_b_read = sem("head_b_read")
        score_a = sem("score_a")
        biased_a = sem("biased_a")
        top_a = sem("top_a")
        neg_top_a = sem("neg_top_a")
        exp_a = sem("exp_a")
        inv_a = sem("inv_a")
        probs_a = sem("probs_a")
        va_turned = sem("va_turned")
        va_tok_ready = sem("va_tok_ready")
        turned_a = sem("turned_a")
        pT_a = sem("pT_a")
        head_a = sem("head_a")
        head_a_read = sem("head_a_read")
        gate_stored = [sem("gate_stored0"), sem("gate_stored1")]
        head_hi_ready = sem("head_hi_ready")
        head_lo_ready = sem("head_lo_ready")
        gate_landed = [sem("gate_landed0"), sem("gate_landed1")]
        gates_open = sem("gates_open")
        mixed = sem("mixed")
        mix_hi_ready = sem("mix_hi_ready")
        mix_lo_ready = sem("mix_lo_ready")
        resid_landed = sem("resid_landed")
        p_landed = sem("p_landed")
        p_hi_ready = sem("p_hi_ready")
        p_lo_ready = sem("p_lo_ready")
        sq_ready = sem("sq_ready")
        sq_added = sem("sq_added")
        gained = sem("gained")
        scaled_v = sem("scaled_v")
        scaled_p = sem("scaled_p")
        resid_ready = sem("resid_ready")
        resid_hi_ready = sem("resid_hi_ready")
        resid_lo_ready = sem("resid_lo_ready")
        h_sq_ready = sem("h_sq_ready")
        h_sq_summed = sem("h_sq_summed")
        embed_half = sem("embed_half")
        embed_read = sem("embed_read")
        embed_stored = sem("embed_stored")
        embed_landed = sem("embed_landed")
        sums_zero = sem("sums_zero")
        silu_ready = sem("silu_ready")
        hid_ready = sem("hid_ready")
        hid_hi_ready = sem("hid_hi_ready")
        hid_lo_ready = sem("hid_lo_ready")
        ple_sig = sem("ple_sig")
        ple_ready = sem("ple_ready")
        y_scaled_v = sem("y_scaled_v")
        y_scaled_p = sem("y_scaled_p")
        y_ready_v = sem("y_ready_v")
        y_ready_p = sem("y_ready_p")
        y_stored = sem("y_stored")

        w_in_v = w_in.rearrange("(k p) n -> p k n", p=P)
        wa_v = w_branch_a.rearrange("(k p) n -> p k n", p=P)
        wb_v = w_branch_b.rearrange("(k p) n -> p k n", p=P)
        wo_v = w_out.rearrange("(k p) n -> p k n", p=P)
        wi_v = w_ffn_in.rearrange("(k p) n -> p k n", p=P)
        wf_v = w_ffn_out.rearrange("(k p) n -> p k n", p=P)
        wp_v = w_ple.rearrange("(k p) n -> p k n", p=P)
        wg_v = w_ple_gate.rearrange("(k p) n -> p k n", p=P)
        x_v = xT.rearrange("(k p) t -> p k t", p=P)
        p_v = pT.rearrange("(k p) t -> p k t", p=P)
        y_v = yT.rearrange("(k p) t -> p k t", p=P)

        block = ctx.enter_context(nc.Block())

        @block.sync
        def _(sp):
            def fetch(n, half, src, shape=None):
                sp.wait_ge(lo_ready, 2 * n + half + 1)
                dst = w_raw[:, half] if shape is None else w_raw[:, half].rearrange("p s c -> p (s c)").rearrange(
                    "p (k c) -> p k c", k=shape)
                sp.dma_start(dst, src).then_inc(raw_landed[half], 16)

            def fetch_tall(n, view, col):
                for half in range(2):
                    fetch(n, half, view[:, half * HALF:(half + 1) * HALF, bass.ds(col, P)])

            for i, (first, end) in enumerate(X_PARTS):
                sp.dma_start(x_f[:, first:end], x_v[:, first:end]).then_inc(x_landed[i], 16)
                if i == 0:
                    fetch_tall(0, w_in_v, C_KB)
            for j in range(KV):
                n0 = j * GROUP_UNITS
                if j:
                    fetch_tall(n0, w_in_v, C_KB + j * DH)
                fetch_tall(n0 + 1, w_in_v, C_VB + j * DH)
                with sp.Fori(1, PER_KV + 1) as r:
                    n = r * HEAD_UNITS + (n0 + 2 - HEAD_UNITS)
                    h = j * PER_KV - 1
                    fetch_tall(n, w_in_v, r * DH + (C_QB + h * DH))
                    fetch_tall(n + 1, w_in_v, r * DH + (C_KA + h * DH))
                    fetch_tall(n + 2, w_in_v, r * DH + (C_QA + h * DH))
                    fetch_tall(n + 3, w_in_v, r * DH + (C_VA + h * DH))
                    for i in range(2):
                        fetch_tall(n + 4 + i, w_in_v, r * 2 * P + (C_GA + (2 * h + i) * P))
                    for i in range(2):
                        fetch_tall(n + 6 + i, w_in_v, r * 2 * P + (C_GB + (2 * h + i) * P))
            for m in range(2):
                fetch(N_BRANCH + m, 0, wa_v[:, :, m * P:(m + 1) * P])
                fetch(N_BRANCH + m, 1, wb_v[:, :, m * P:(m + 1) * P])
            for slot in range(2):
                sp.wait_ge(gate_stored[slot], 16 * KT)
            sp.wait_ge(head_lo_ready, KT)
            for slot in range(2):
                sp.dma_start(gate_in[:, slot], gate_dram.ap()[slot].rearrange("g p t -> p g t")).then_inc(
                    gate_landed[slot], 16)
            with sp.Fori(1, KT // 2) as i:
                for slot in range(2):
                    n = i * 2 + (N_BRANCH + slot)
                    fetch(n, 0, wa_v[:, :, bass.ds(i * 2 * P + slot * P, P)])
                    fetch(n, 1, wb_v[:, :, bass.ds(i * 2 * P + slot * P, P)])
                    sp.wait_ge(unit_read, n)
                    sp.dma_start(gate_in[:, slot], gate_dram.ap()[bass.ds(i * 2 + slot, 1)].rearrange(
                        "m g p t -> p (m g) t")).then_inc(gate_landed[slot], 16)
            for m in range(2):
                fetch_tall(N_OUT + m, wo_v, m * P)
            sp.wait_ge(mix_lo_ready, KT)
            sp.dma_start(p_f[:], p_v).then_inc(p_landed, 16)
            sp.dma_start(resid[:], x_v).then_inc(resid_landed, 16)
            with sp.Fori(1, KT // 2) as i:
                for m in range(2):
                    fetch_tall(i * 2 + (N_OUT + m), wo_v, i * 2 * P + m * P)

            def fetch_embed(n, first):
                for half in range(2):
                    fetch(n, half, wp_v[:, :, (first + 4 * half) * P:(first + 4 * half + 4) * P], 2)

            def fetch_in(n, f):
                for i in range(CH):
                    fetch_tall(n + 2 * i, wi_v, f * P + i * P)
                    fetch_tall(n + 2 * i + 1, wi_v, f * P + (DF + i * P))

            def fetch_out(n, f):
                for u in range(OUT_UNITS):
                    for half in range(2):
                        fetch(n + u, half, wf_v[:, bass.ds(f + 2 * half, 2), u * 4 * P:(u + 1) * 4 * P], 2)

            fetch_embed(N_EMBED_A, 0)
            fetch_in(N_FFN, 0)
            with sp.Fori(1, CHUNKS) as c:
                n = c * CHUNK_UNITS + (N_FFN - OUT_UNITS)
                fetch_out(n, c * CH - CH)
                fetch_in(n + OUT_UNITS, c * CH)
            fetch_out(N_EMBED_B - OUT_UNITS, FT - CH)
            fetch_embed(N_EMBED_B, 8)
            for m in range(2):
                fetch_tall(N_PLE + m, wg_v, m * P)
            sp.wait_ge(resid_ready, KT + 8)
            sp.dma_start(sums[:, 0:8], embed_dram.ap().rearrange("m p t -> p m t")).then_inc(embed_landed, 16)
            with sp.Fori(1, KT // 2) as i:
                for m in range(2):
                    fetch_tall(i * 2 + (N_PLE + m), wg_v, i * 2 * P + m * P)
            for k in range(KT):
                if k in Y_BY_POOL:
                    sp.wait_ge(y_ready_p, Y_BY_POOL.index(k) + 1)
                else:
                    sp.wait_ge(y_ready_v, Y_BY_DVE.index(k) + 1)
                sp.dma_start(y_v[:, k], resid[:, k]).then_inc(y_stored, 16)
            sp.wait_ge(y_stored, 16 * KT)

        @block.gpsimd
        def _(pool):
            def root(q):
                pool.wait_ge(norm_var, q + 1)
                nc.gpsimd.tensor_tensor(rs[:], var[:], minus_half[:], ALU.pow).then_inc(norm_root, 1)

            nc.gpsimd.memset(rpb_pad[:], 0.0).then_inc(pad_set, 1)
            nc.gpsimd.memset(ones[:], 1.0).then_inc(ones_set, 1)
            nc.gpsimd.memset(minus_half[:], -0.5).then_inc(ones_set, 1)
            for k in range(KT):
                for i, (first, _) in enumerate(X_PARTS):
                    if k == first:
                        pool.wait_ge(x_landed[i], 16)
                if k >= 2:
                    pool.wait_ge(x_sq_added, k - 1)
                nc.gpsimd.tensor_tensor(x_sq[k % 2][:], x_f[:, k], x_f[:, k], ALU.mult).then_inc(x_sq_ready, 1)
            pool.wait_ge(ones_set, 2)
            root(0)
            nc.gpsimd.memset(sq_sum[:], 0.0).then_inc(sq_added, 1)
            with pool.Fori(1, NORM_MIX) as q:
                root(q)
            root(NORM_MIX)

            def scale(which):
                pool.wait_ge(rstd_ready, 2 + 2 * which)
                for k in SCALED_BY_POOL:
                    pool.wait_ge(gained, which * KT + k + 1)
                    nc.gpsimd.tensor_tensor(sums[:, k], sums[:, k], rstd[:], ALU.mult).then_inc(scaled_p, 1)

            scale(0)
            root(NORM_FFN_IN)
            pool.wait_ge(resid_ready, KT)
            nc.gpsimd.memset(sums[:], 0.0).then_inc(sums_zero, 1)
            nc.gpsimd.memset(sq_sum[:], 0.0).then_inc(sq_added, 1)
            root(NORM_FFN)
            nc.gpsimd.memset(sq_sum[:], 0.0).then_inc(sq_added, 1)
            scale(1)
            root(NORM_PLE)
            pool.wait_ge(rstd_ready, 5)
            for i, k in enumerate(Y_BY_POOL):
                pool.wait_ge(gained, 2 * KT + k + 1)
                nc.gpsimd.tensor_tensor(sums[:, k], sums[:, k], rstd[:], ALU.mult).then_inc(y_scaled_p, 1)
                pool.wait_ge(y_scaled_p, i + 1)
                nc.gpsimd.tensor_tensor(resid[:, k], resid[:, k], sums[:, k], ALU.add).then_inc(y_ready_p, 1)

        @block.scalar
        def _(act):
            def split_hi(n, par, half, free=True):
                act.wait_ge(raw_landed[half], 16 * n + 16)
                nc.scalar.copy(w_hi[:, 2 * par + half], w_raw[:, half]).then_inc(hi_ready, 1)

            def next_hi(n, par):
                act.wait_ge(unit_done, n + 1)
                for half in range(2):
                    split_hi(n + 2, par, half)

            act.dma_start(g_t[:], gains).then_inc(gains_landed, 16)
            act.dma_start(gqk_t[:], gains_qk).then_inc(gains_landed, 16)
            act.wait_ge(pad_set, 1)
            act.dma_start(rpb_pad[:, 48:48 + 2 * NA_COLS - 1], rpb).then_inc(rpb_landed, 16)
            act.dma_start(ident_t[:], ident).then_inc(ident_landed, 16)
            act.dma_start(mask_t[:], col_mask).then_inc(mask_landed, 16)
            act.dma_start(flip_t[:], flip).then_inc(mask_landed, 16)
            act.dma_start(cos_t[:], rope_cos).then_inc(const_landed, 16)
            act.dma_start(sin_t[:], rope_sin).then_inc(const_landed, 16)
            act.dma_start(rot_t[:], rope_rot).then_inc(const_landed, 16)

            act.wait_ge(gains_landed, 32)

            def x_hi(k):
                for i, (first, _) in enumerate(X_PARTS):
                    if k == first:
                        act.wait_ge(x_landed[i], 16)
                nc.scalar.activation(act_hi[:, k], x_f[:, k], ACT.Identity,
                                     scale=g_t[:, G_PRE, k:k + 1]).then_inc(x_hi_ready, 1)

            split_hi(0, 0, 0)
            for k in range(KT):
                x_hi(k)
                if k == HALF - 3:
                    split_hi(0, 0, 1)
            act.wait_ge(rpb_landed, 16)
            act.dma_start(pad_dram.ap(), rpb_pad[:]).then_inc(pad_stored, 16)
            split_hi(1, 1, 0)
            split_hi(1, 1, 1)
            act.wait_ge(pad_stored, 16)
            rows = 2 * NA_ROWS_MAX - 1
            for h in range(HEADS):
                for rl in range(2):
                    first = (h * rows + NA_ROWS_MAX - 1 - 2 - rl) * PADC
                    act.dma_start(bias_flipped[rl * GRID:(rl + 1) * GRID, h],
                                  bass.AP(pad_dram, first, [[1, GRID], [PADC, E_ROWS], [1, GRID]])).then_inc(
                                      table_landed, 16)

            def head_norm_inputs(n, g):
                act.wait_ge(unit_read, n + 2)
                nc.scalar.activation(qk_sq[:], qk_raw[:], ACT.Square).then_inc(qk_sq_ready, 1)
                nc.scalar.activation(qk_gain[:], qk_raw[:], ACT.Identity,
                                     scale=gqk_t[:, g:g + 1]).then_inc(qk_gain_ready, 1)

            def exps(ready, value, src, which, scale, done):
                act.wait_ge(ready, value)
                for t in range(TT):
                    ins = nc.scalar.activation(probs[:, t], src[:, t], ACT.Exp, bias=neg_top[:, which, t:t + 1],
                                               scale=scale, accum_out=psum_p[:, which, t:t + 1])
                    ins.then_inc(done, 1)

            def evacuate_pT(ready, value, done):
                act.wait_ge(ready, value)
                for g in range(GROUPS):
                    nc.scalar.copy(probs_T[:, g].rearrange("p a b -> p (a b)"), bank[:, B_PT + g]).then_inc(done, 1)

            def store_gate(n, slot, m, which):
                act.wait_ge(unit_read, n + 2)
                act.dma_start(gate_dram.ap()[bass.ds(m, 1), which].rearrange("m p t -> p (m t)"),
                              gate_out[:, slot]).then_inc(gate_stored[slot], 16)

            scores = bank[:, B_SCORE:B_SCORE + 2].rearrange("p g (q s) -> p (g q) s", q=2)

            def head(j, r, last):
                n0 = j * GROUP_UNITS
                n = r * HEAD_UNITS + (n0 + 2)
                hd = r + j * PER_KV
                next_hi(n, 0)
                head_norm_inputs(n, 0)
                next_hi(n + 1, 1)
                next_hi(n + 2, 0)
                exps(neg_top_b, hd + 1, scores, 0, SCALE, exp_b)
                next_hi(n + 3, 1)
                evacuate_pT(turned_b, hd + 1, pT_b)
                exps(neg_top_a, hd + 1, na_scores, 1, 1.0, exp_a)
                next_hi(n + 4, 0)
                store_gate(n + 4, 0, r * 2 + 2 * j * PER_KV, 0)
                next_hi(n + 5, 1)
                store_gate(n + 5, 1, r * 2 + (2 * j * PER_KV + 1), 0)
                evacuate_pT(turned_a, hd + 1, pT_a)
                next_hi(n + 6, 0)
                store_gate(n + 6, 0, r * 2 + 2 * j * PER_KV, 1)
                act.wait_ge(unit_done, n + 8)
                store_gate(n + 7, 1, r * 2 + (2 * j * PER_KV + 1), 1)
                if not last:
                    next_hi(n + 7, 1)

            for j in range(KV):
                n0 = j * GROUP_UNITS
                next_hi(n0, 0)
                head_norm_inputs(n0, 1)
                next_hi(n0 + 1, 1)
                rolled = PER_KV - (j == KV - 1)
                with act.Fori(0, rolled) as r:
                    head(j, r, False)
            head(KV - 1, PER_KV - 1, True)
            act.wait_ge(head_a_read, HEADS)
            for k in range(KT):
                nc.scalar.copy(head_hi[:, k], head_f[:, k]).then_inc(head_hi_ready, 1)
                if k in SPLIT_AFTER:
                    split_hi(N_BRANCH + 1, 1, SPLIT_AFTER.index(k))
            with act.Fori(0, KT // 2) as i:
                for slot in range(2):
                    n = i * 2 + (N_BRANCH + slot)
                    act.wait_ge(gate_landed[slot], i * 16 + 16)
                    nc.scalar.activation(gate_in[:, slot], gate_in[:, slot], ACT.Sigmoid).then_inc(gates_open, 1)
                    next_hi(n, slot)
                    act.wait_ge(mixed, i * 2 + (slot + 1))
                    nc.scalar.copy(act_hi[:, bass.ds(i * 2 + slot, 1)], mix_a[:].rearrange(
                        "p (a t) -> p a t", a=1)).then_inc(mix_hi_ready, 1)

            def square_and_gain(count, slot, starts, tile, gain):
                act.wait_ge(sq_added, count + starts)
                nc.scalar.activation(sq[:, slot:slot + 1], tile, ACT.Square).then_inc(sq_ready, 1)
                act.wait_ge(sq_ready, count + 1)
                nc.scalar.activation(tile, tile, ACT.Identity, scale=gain).then_inc(gained, 1)

            def out_tile(n, m, par):
                act.wait_ge(unit_read, n + 2)
                square_and_gain(m, par, 1, sums[:, bass.ds(m, 1)], g_t[:, G_POST, bass.ds(m, 1)])
                next_hi(n, par)

            with act.Fori(0, KT // 2 - 1) as i:
                for m in range(2):
                    out_tile(i * 2 + (N_OUT + m), i * 2 + m, m)
            act.wait_ge(p_landed, 16)
            nc.scalar.copy(p_hi[:], p_f[:]).then_inc(p_hi_ready, 1)
            for m in range(KT - 2, KT):
                out_tile(N_OUT + m, m, m % 2)

            def embed_part(first, count, banks):
                for i in range(count):
                    nc.scalar.copy(embed[:, first + i], bank[:, banks[i]]).then_inc(embed_read, 1)

            act.wait_ge(embed_half, 1)
            embed_part(0, 4, EMBED_A_BANKS[0])
            for k in range(KT):
                act.wait_ge(resid_ready, k + 1)
                nc.scalar.activation(act_hi[:, k], resid[:, k], ACT.Identity,
                                     scale=g_t[:, G_FFN, k:k + 1]).then_inc(resid_hi_ready, 1)
                if k >= 2:
                    act.wait_ge(h_sq_summed, k - 1)
                nc.scalar.activation(sq[:, k % 2], resid[:, k], ACT.Square).then_inc(h_sq_ready, 1)
                if k == 8:
                    act.wait_ge(unit_done, N_EMBED_A + 1)
                    split_hi(N_EMBED_A + 2, 0, 0)
            split_hi(N_EMBED_A + 2, 0, 1)
            embed_part(4, 4, EMBED_A_BANKS[1])
            act.wait_ge(embed_read, 8)
            act.dma_start(embed_dram.ap().rearrange("m p t -> p m t"), embed[:]).then_inc(embed_stored, 16)

            def ffn_in(n, f, first=False):
                for i in range(CH):
                    par = (N_FFN + 2 * i) % 2
                    next_hi(n + 2 * i, par)
                    act.wait_ge(unit_read, n + 2 * i + 1)
                    nc.scalar.activation(tmp[:, 0], tmp[:, 0], ACT.Silu).then_inc(silu_ready, 1)
                    act.wait_ge(unit_done, n + 2 * i + 2)
                    split_hi(n + 2 * i + 3, 1 - par, 0)
                    if first and i == 0:
                        act.wait_ge(embed_stored, 16)
                    act.wait_ge(hid_ready, f + i + 1)
                    nc.scalar.copy(hid_hi[:, i], sq[:, 0]).then_inc(hid_hi_ready, 1)
                    split_hi(n + 2 * i + 3, 1 - par, 1)

            def ffn_out(n):
                for u in range(OUT_UNITS):
                    next_hi(n + u, (N_FFN + u) % 2)

            ffn_in(N_FFN, 0, True)
            with act.Fori(1, CHUNKS) as c:
                n = c * CHUNK_UNITS + (N_FFN - OUT_UNITS)
                ffn_out(n)
                ffn_in(n + OUT_UNITS, c * CH)
            for u in range(OUT_UNITS):
                n = N_EMBED_B - OUT_UNITS + u
                next_hi(n, n % 2)
                act.wait_ge(unit_read, n + 1)
                for i in range(4):
                    k = 4 * u + i
                    square_and_gain(KT + k, k % 2, 1, sums[:, k:k + 1], g_t[:, G_PFFN, k:k + 1])
            act.wait_ge(embed_half, 2)
            embed_part(0, 4, EMBED_B_BANKS[0])
            for k in range(KT):
                act.wait_ge(resid_ready, KT + k + 1)
                nc.scalar.copy(act_hi[:, k], resid[:, k]).then_inc(resid_hi_ready, 1)
                if k == 3:
                    act.wait_ge(unit_done, N_EMBED_B + 1)
                    embed_part(4, 4, EMBED_B_BANKS[1])
                if k == 8:
                    split_hi(N_EMBED_B + 2, (N_EMBED_B + 2) % 2, 0)
            split_hi(N_EMBED_B + 2, (N_EMBED_B + 2) % 2, 1)

            def ple_tile(n, m, par, slot, more=True):
                act.wait_ge(unit_done, n + 1)
                nc.scalar.activation(tmp[:, 0], bank[:, PLE_BANKS[slot]], ACT.Sigmoid).then_inc(ple_sig, 1)
                if more:
                    next_hi(n, par)
                act.wait_ge(ple_ready, m + 1)
                square_and_gain(m + 2 * KT, slot, 3, sums[:, bass.ds(m, 1)], g_t[:, G_PLE, bass.ds(m, 1)])

            with act.Fori(0, KT // 2 - 1) as i:
                for m in range(2):
                    ple_tile(i * 2 + (N_PLE + m), i * 2 + m, (N_PLE + m) % 2, m)
            for m in range(KT - 2, KT):
                ple_tile(N_PLE + m, m, (N_PLE + m) % 2, m % 2, False)

        @block.vector
        def _(dve):
            def split_lo(n, par, half):
                dve.wait_ge(hi_ready, 2 * n + half + 1)
                nc.vector.tensor_tensor(w_lo[:, 2 * par + half], w_raw[:, half],
                                        w_hi[:, 2 * par + half].bitcast(F32), ALU.subtract).then_inc(lo_ready, 1)

            def next_lo(n, par):
                for half in range(2):
                    split_lo(n + 2, par, half)

            def mean_square(q, width, src_bank):
                dve.wait_ge(norm_summed, q + 1)
                nc.vector.tensor_scalar(var[:], bank[:, src_bank, 0:TT], 1.0 / width, EPS, ALU.mult,
                                        ALU.add).then_inc(norm_var, 1)

            def diagonal(q, first=False):
                dve.wait_ge(norm_root, q + 1)
                if not first:
                    dve.wait_ge(norm_spread, q)
                nc.vector.tensor_tensor(diag[:], ident_t[:].unsqueeze(1).to_broadcast([P, TT, P]),
                                        rs[:].unsqueeze(2).to_broadcast([P, TT, P]), ALU.mult).then_inc(norm_diag, 1)

            def evacuate(n, par, dst):
                dve.wait_ge(unit_done, n + 1)
                nc.vector.tensor_tensor(dst, bank[:, par], rstd[:], ALU.mult).then_inc(unit_read, 1)

            nc.vector.memset(top[:], 0.0).then_inc(lo_ready, 1)
            nc.vector.memset(neg_top[:], 0.0).then_inc(lo_ready, 1)
            nc.vector.memset(inv_p[:], 0.0).then_inc(unit_read, 1)
            dve.wait_ge(gains_landed, 32)

            def x_lo(k):
                dve.wait_ge(x_hi_ready, k + 1)
                nc.vector.scalar_tensor_tensor(act_lo[:, k], x_f[:, k], g_t[:, G_PRE, k:k + 1],
                                               act_hi[:, k].bitcast(F32), ALU.mult, ALU.subtract).then_inc(x_lo_ready, 1)

            def add_x_square(k):
                dve.wait_ge(x_sq_ready, k + 1)
                if k == 0:
                    nc.vector.tensor_copy(sq_sum[:], x_sq[0][:]).then_inc(x_sq_added, 1)
                else:
                    dve.wait_ge(x_sq_added, k)
                    nc.vector.tensor_tensor(sq_sum[:], sq_sum[:], x_sq[k % 2][:], ALU.add).then_inc(x_sq_added, 1)

            split_lo(0, 0, 0)
            for k in range(KT):
                x_lo(k)
                if k == HALF - 2:
                    split_lo(0, 0, 1)
                if k % 2:
                    add_x_square(k // 2)
            split_lo(1, 1, 0)
            split_lo(1, 1, 1)
            for k in range(HALF, KT):
                add_x_square(k)
            mean_square(0, D, B_NORM)
            dve.wait_ge(ident_landed, 16)
            diagonal(0, True)
            dve.wait_ge(norm_spread, 1)
            nc.vector.tensor_copy(rstd[:], bank[:, B_NORM]).then_inc(rstd_ready, 1)
            dve.wait_ge(rstd_ready, 1)

            def rope(e, q, dst):
                mean_square(q, DH, B_NORM)
                dve.wait_ge(qk_rotated, e + 1)
                nc.vector.tensor_tensor(rope_s[:], bank[:, B_MISC], sin_t[:], ALU.mult).then_inc(rope_s_ready, 1)
                diagonal(q)
                dve.wait_ge(qk_gain_ready, e + 1)
                nc.vector.tensor_tensor(rope_c[:], qk_gain[:], cos_t[:], ALU.mult).then_inc(rope_c_ready, 1)
                dve.wait_ge(rope_c_ready, e + 1)
                nc.vector.tensor_tensor(rope_c[:], rope_c[:], rope_s[:], ALU.add).then_inc(rope_added, 1)
                dve.wait_ge(rope_added, e + 1)
                dve.wait_ge(norm_spread, q + 1)
                nc.vector.tensor_tensor(dst[:], rope_c[:], bank[:, B_NORM], ALU.mult).then_inc(rope_done, 1)

            def normalise(exp_sem, value, which, inv_sem, done):
                dve.wait_ge(exp_sem, value * TT)
                nc.vector.reciprocal(inv_p[:, which], psum_p[:, which]).then_inc(inv_sem, 1)
                dve.wait_ge(inv_sem, value)
                for t in range(TT):
                    nc.vector.tensor_scalar(probs[:, t], probs[:, t], inv_p[:, which, t:t + 1], None,
                                            ALU.mult).then_inc(done, 1)

            def bias_parts(first, end):
                dve.wait_ge(mask_landed, 32)
                for i in range(first, end):
                    dve.wait_ge(flipped, i + 1)
                    nc.vector.tensor_tensor(
                        bias[:].rearrange("p h e c -> p (h e) c")[:, 8 * i:8 * i + 8],
                        bank[:, B_SCORE + i % 4].rearrange("p (a c) -> p a c", c=GRID),
                        mask_t[:].unsqueeze(1).to_broadcast([P, 8, GRID]), ALU.add).then_inc(bias_read, 1)

            scores = bank[:, B_SCORE:B_SCORE + 2].rearrange("p g (q s) -> p (g q) s", q=2)
            def head(j, r, last):
                n0 = j * GROUP_UNITS
                e0 = j * (PER_KV + 1)
                n = r * HEAD_UNITS + (n0 + 2)
                hd = r + j * PER_KV
                evacuate(n, 0, qk_raw[:])
                next_lo(n, 0)
                evacuate(n + 1, 1, ka_f[:])
                next_lo(n + 1, 1)
                rope(r + (e0 + 1), r + (e0 + 2), q_rope)
                evacuate(n + 2, 0, qa_f[:])
                next_lo(n + 2, 0)
                dve.wait_ge(score_b, hd + 1)
                nc.vector.tensor_reduce(top[:, 0], scores, AX_X, ALU.max).then_inc(top_b, 1)
                dve.wait_ge(top_b, hd + 1)
                nc.vector.tensor_scalar(neg_top[:, 0], top[:, 0], -SCALE, None, ALU.mult).then_inc(neg_top_b, 1)
                normalise(exp_b, hd + 1, 0, inv_b, probs_b)
                evacuate(n + 3, 1, va_f[:])
                next_lo(n + 3, 1)
                dve.wait_ge(score_a, hd + 1)
                for g in range(GROUPS):
                    for qi in range(2):
                        nc.vector.scalar_tensor_tensor(
                            na_scores[:, 2 * g + qi], bank[:, B_SCORE + g, qi * S:(qi + 1) * S], SCALE,
                            bias[:].rearrange("p h e c -> p h (e c)")[
                                :, bass.ds(hd, 1), (2 - 2 * qi) * GRID:(6 - 2 * qi) * GRID].rearrange(
                                    "p h c -> p (h c)"),
                            ALU.mult, ALU.add).then_inc(biased_a, 1)
                dve.wait_ge(biased_a, hd * TT + TT)
                nc.vector.tensor_reduce(top[:, 1], na_scores[:], AX_X, ALU.max).then_inc(top_a, 1)
                dve.wait_ge(top_a, hd + 1)
                nc.vector.tensor_scalar(neg_top[:, 1], top[:, 1], -1.0, None, ALU.mult).then_inc(neg_top_a, 1)
                normalise(exp_a, hd + 1, 1, inv_a, probs_a)
                evacuate(n + 4, 0, gate_out[:, 0])
                next_lo(n + 4, 0)
                dve.wait_ge(va_turned, hd + 1)
                nc.vector.tensor_copy(va_tok[:].rearrange("p a b -> p (a b)"), bank[:, B_NORM]).then_inc(va_tok_ready, 1)
                dve.wait_ge(head_b, hd + 1)
                nc.vector.tensor_copy(head_f[:, bass.ds(hd + HEADS, 1)], bank[:, B_MISC:B_MISC + 1]).then_inc(head_b_read, 1)
                evacuate(n + 5, 1, gate_out[:, 1])
                next_lo(n + 5, 1)
                dve.wait_ge(gate_stored[0], hd * 32 + 16)
                evacuate(n + 6, 0, gate_out[:, 0])
                next_lo(n + 6, 0)
                dve.wait_ge(head_a, hd + 1)
                nc.vector.tensor_copy(head_f[:, bass.ds(hd, 1)], bank[:, B_MISC:B_MISC + 1]).then_inc(head_a_read, 1)
                dve.wait_ge(gate_stored[1], hd * 32 + 16)
                evacuate(n + 7, 1, gate_out[:, 1])
                if not last:
                    next_lo(n + 7, 1)
                    for slot in range(2):
                        dve.wait_ge(gate_stored[slot], hd * 32 + 32)

            for j in range(KV):
                n0 = j * GROUP_UNITS
                e0 = j * (PER_KV + 1)
                evacuate(n0, 0, qk_raw[:])
                next_lo(n0, 0)
                if j == 0:
                    bias_parts(0, 4)
                    dve.wait_ge(const_landed, 48)
                rope(e0, e0 + 1, k_rope)
                evacuate(n0 + 1, 1, vb_f[:])
                next_lo(n0 + 1, 1)
                if j == 0:
                    bias_parts(4, BIAS_PARTS)
                dve.wait_ge(vb_turned, j + 1)
                nc.vector.tensor_copy(vb_tok[:].rearrange("p a b -> p (a b)"), bank[:, B_PT]).then_inc(vb_tok_ready, 1)
                rolled = PER_KV - (j == KV - 1)
                with dve.Fori(0, rolled) as r:
                    head(j, r, False)
            head(KV - 1, PER_KV - 1, True)
            for k in range(KT):
                dve.wait_ge(head_hi_ready, k + 1)
                if k == KT - 2:
                    dve.wait_ge(gate_stored[0], 16 * KT)
                    dve.wait_ge(gate_stored[1], 16 * KT)
                nc.vector.tensor_tensor(head_lo[:, k], head_f[:, k], head_hi[:, k].bitcast(F32),
                                        ALU.subtract).then_inc(head_lo_ready, 1)
                if k in SPLIT_AFTER:
                    split_lo(N_BRANCH + 1, 1, SPLIT_AFTER.index(k))
            with dve.Fori(0, KT // 2) as i:
                for slot in range(2):
                    n = i * 2 + (N_BRANCH + slot)
                    m = i * 2 + slot
                    dve.wait_ge(unit_done, n + 1)
                    dve.wait_ge(gates_open, m + 1)
                    nc.vector.tensor_tensor(mix_a[:], bank[:, 2 * slot], gate_in[:, slot, 0], ALU.mult)
                    nc.vector.tensor_tensor(mix_b[:], bank[:, 2 * slot + 1], gate_in[:, slot, 1], ALU.mult).then_inc(unit_read, 1)
                    dve.wait_ge(unit_read, n + 2)
                    nc.vector.tensor_tensor(mix_a[:], mix_a[:], mix_b[:], ALU.add).then_inc(mixed, 1)
                    next_lo(n, slot)
                    dve.wait_ge(mix_hi_ready, m + 1)
                    nc.vector.tensor_tensor(act_lo[:, bass.ds(m, 1)], mix_a[:].rearrange("p (a t) -> p a t", a=1),
                                            act_hi[:, bass.ds(m, 1)].bitcast(F32), ALU.subtract).then_inc(mix_lo_ready, 1)
                    dve.wait_ge(mix_lo_ready, m + 1)

            def add_square(count, slot, starts):
                dve.wait_ge(sq_ready, count + 1)
                dve.wait_ge(sq_added, count + starts)
                nc.vector.tensor_tensor(sq_sum[:], sq_sum[:], sq[:, slot], ALU.add).then_inc(sq_added, 1)

            def out_tile(n, m, par, more=True):
                dve.wait_ge(unit_done, n + 1)
                nc.vector.tensor_copy(sums[:, bass.ds(m, 1)], bank[:, par:par + 1]).then_inc(unit_read, 1)
                if more:
                    next_lo(n, par)
                add_square(m, par, 1)

            with dve.Fori(0, KT // 2 - 1) as i:
                for m in range(2):
                    out_tile(i * 2 + (N_OUT + m), i * 2 + m, m)
            dve.wait_ge(p_hi_ready, 1)
            nc.vector.tensor_tensor(p_lo[:], p_f[:], p_hi[:].bitcast(F32), ALU.subtract).then_inc(p_lo_ready, 1)
            out_tile(N_OUT + KT - 2, KT - 2, 0)
            out_tile(N_OUT + KT - 1, KT - 1, 1, False)

            def keep_rstd(q, b, times):
                dve.wait_ge(norm_spread, q + 1)
                nc.vector.tensor_copy(rstd[:], bank[:, b]).then_inc(rstd_ready, 1)
                dve.wait_ge(rstd_ready, times)

            def residual(which, norm, norm_bank, gain_out, filler):
                par = (filler + 1) % 2
                mean_square(norm, D, norm_bank)
                diagonal(norm)
                split_lo(filler + 1, par, 0)
                keep_rstd(norm, norm_bank, 2 + 2 * which)

                def scale(k):
                    dve.wait_ge(gained, which * KT + k + 1)
                    nc.vector.tensor_tensor(sums[:, k], sums[:, k], rstd[:], ALU.mult).then_inc(scaled_v, 1)

                def low(k):
                    dve.wait_ge(resid_hi_ready, which * KT + k + 1)
                    if gain_out is None:
                        nc.vector.tensor_tensor(act_lo[:, k], resid[:, k], act_hi[:, k].bitcast(F32),
                                                ALU.subtract).then_inc(resid_lo_ready, 1)
                    else:
                        nc.vector.scalar_tensor_tensor(act_lo[:, k], resid[:, k], g_t[:, gain_out, k:k + 1],
                                                       act_hi[:, k].bitcast(F32), ALU.mult,
                                                       ALU.subtract).then_inc(resid_lo_ready, 1)

                scale(SCALED_BY_DVE[0])
                for k in range(KT):
                    if k in SCALED_BY_DVE:
                        dve.wait_ge(scaled_v, which * len(SCALED_BY_DVE) + SCALED_BY_DVE.index(k) + 1)
                    else:
                        dve.wait_ge(scaled_p, which * len(SCALED_BY_POOL) + SCALED_BY_POOL.index(k) + 1)
                    nc.vector.tensor_tensor(resid[:, k], resid[:, k], sums[:, k], ALU.add).then_inc(resid_ready, 1)
                    if k + 1 in SCALED_BY_DVE:
                        scale(k + 1)
                    if k:
                        low(k - 1)
                    if k == 3:
                        split_lo(filler + 1, par, 1)
                    if k == 12:
                        split_lo(filler + 2, 1 - par, 0)
                low(KT - 1)
                split_lo(filler + 2, 1 - par, 1)

            dve.wait_ge(resid_landed, 16)
            residual(0, NORM_MIX, B_NORM, G_FFN, N_EMBED_A)
            mean_square(NORM_FFN_IN, D, B_NORM)
            diagonal(NORM_FFN_IN)
            keep_rstd(NORM_FFN_IN, B_NORM, 3)

            def ffn_in(n, f):
                for i in range(CH):
                    par = (N_FFN + 2 * i) % 2
                    b = IN_BANKS[2 * i]
                    dve.wait_ge(unit_done, n + 2 * i + 1)
                    nc.vector.tensor_tensor(tmp[:, 0], bank[:, b], rstd[:], ALU.mult).then_inc(unit_read, 1)
                    next_lo(n + 2 * i, par)
                    dve.wait_ge(unit_done, n + 2 * i + 2)
                    nc.vector.tensor_tensor(tmp[:, 1], bank[:, IN_BANKS[2 * i + 1]], rstd[:], ALU.mult).then_inc(unit_read, 1)
                    dve.wait_ge(silu_ready, f + i + 1)
                    dve.wait_ge(unit_read, n + 2 * i + 2)
                    if not (isinstance(f, int) and f + i == 0):
                        dve.wait_ge(hid_lo_ready, f + i)
                    nc.vector.tensor_tensor(sq[:, 0], tmp[:, 0], tmp[:, 1], ALU.mult).then_inc(hid_ready, 1)
                    split_lo(n + 2 * i + 3, 1 - par, 0)
                    dve.wait_ge(hid_hi_ready, f + i + 1)
                    nc.vector.tensor_tensor(hid_lo[:, i], sq[:, 0], hid_hi[:, i].bitcast(F32),
                                            ALU.subtract).then_inc(hid_lo_ready, 1)
                    split_lo(n + 2 * i + 3, 1 - par, 1)

            def ffn_out(n, last):
                for u in range(OUT_UNITS):
                    dve.wait_ge(unit_done, n + u + 1)
                    for i in range(4):
                        m = 4 * u + i
                        ins = nc.vector.tensor_tensor(sums[:, m], sums[:, m], bank[:, OUT_BANKS[u] + i], ALU.add)
                    ins.then_inc(unit_read, 1)
                    if last:
                        if u < OUT_UNITS - 1:
                            next_lo(n + u, (n + u) % 2)
                        for i in range(4):
                            add_square(KT + 4 * u + i, (4 * u + i) % 2, 2)
                    else:
                        next_lo(n + u, (N_FFN + u) % 2)

            ffn_in(N_FFN, 0)
            dve.wait_ge(sums_zero, 1)
            with dve.Fori(1, CHUNKS) as c:
                n = c * CHUNK_UNITS + (N_FFN - OUT_UNITS)
                ffn_out(n, False)
                ffn_in(n + OUT_UNITS, c * CH)
            ffn_out(N_EMBED_B - OUT_UNITS, True)
            residual(1, NORM_FFN, 0, None, N_EMBED_B)
            dve.wait_ge(embed_landed, 16)
            dve.wait_ge(embed_read, 16)

            def ple_tile(n, m, par, slot, emb, more=True):
                dve.wait_ge(ple_sig, m + 1)
                nc.vector.tensor_tensor(sums[:, bass.ds(m, 1)], tmp[:, 0:1], emb, ALU.mult).then_inc(ple_ready, 1)
                if more:
                    next_lo(n, par)
                add_square(m + 2 * KT, slot, 3)

            with dve.Fori(0, 4) as i:
                for s in range(2):
                    m = i * 2 + s
                    ple_tile(i * 2 + (N_PLE + s), m, (N_PLE + s) % 2, s, sums[:, bass.ds(m, 1)])
            with dve.Fori(4, 7) as i:
                for s in range(2):
                    ple_tile(i * 2 + (N_PLE + s), i * 2 + s, (N_PLE + s) % 2, s, embed[:, bass.ds(i * 2 + s - 8, 1)])
            for m in range(KT - 2, KT):
                ple_tile(N_PLE + m, m, (N_PLE + m) % 2, m % 2, embed[:, m - 8:m - 7], False)
            mean_square(NORM_PLE, D, 0)
            diagonal(NORM_PLE)
            keep_rstd(NORM_PLE, 0, 5)
            for i, k in enumerate(Y_BY_DVE + (None,)):
                if k is not None:
                    dve.wait_ge(gained, 2 * KT + k + 1)
                    nc.vector.tensor_tensor(sums[:, k], sums[:, k], rstd[:], ALU.mult).then_inc(y_scaled_v, 1)
                if i:
                    done = Y_BY_DVE[i - 1]
                    dve.wait_ge(y_scaled_v, i)
                    nc.vector.tensor_tensor(resid[:, done], resid[:, done], sums[:, done], ALU.add).then_inc(y_ready_v, 1)

        @block.tensor
        def _(pe):
            def unit(n, par, terms, fillers=0, gate=None, hooks=None, free=True,
                     half_sem=None):
                if free:
                    pe.wait_ge(unit_read, n - fillers)
                for idx, (b, hi, lo, start, stop) in enumerate(terms):
                    half, sub = divmod(idx, HALF)
                    slot = 2 * par + half
                    if hooks and idx in hooks:
                        hooks[idx]()
                    if sub == 0:
                        pe.wait_ge(lo_ready, 2 * n + (half + 3))
                    if gate:
                        gate(idx)
                    nc.tensor.matmul(bank[:, b], w_hi[:, slot, sub], hi, start=start, stop=False)
                    nc.tensor.matmul(bank[:, b], w_hi[:, slot, sub], lo, start=False, stop=False)
                    last = nc.tensor.matmul(bank[:, b], w_lo[:, slot, sub], hi, start=False, stop=stop)
                    if half_sem is not None and idx == HALF - 1:
                        last.then_inc(half_sem, 1)
                last.then_inc(unit_done, 1)

            def tall(b):
                return [(b, act_hi[:, k], act_lo[:, k], k == 0, k == KT - 1) for k in range(KT)]

            def sum_tokens(src, b):
                for t in range(TT):
                    last = nc.tensor.matmul(bank[:, b, t:t + 1], src[:, t * P:(t + 1) * P], ones[:, 0:1],
                                            start=True, stop=True)
                last.then_inc(norm_summed, 1)

            def spread(q, b):
                pe.wait_ge(norm_diag, q + 1)
                nc.tensor.matmul(bank[:, b], ones[:], diag[:].rearrange("p a b -> p (a b)"), start=True,
                                 stop=True).then_inc(norm_spread, 1)

            def turn_values(src, b, done):
                for t in range(TT):
                    last = nc.tensor.transpose(bank[:, b, t * P:(t + 1) * P], src[:, t * P:(t + 1) * P], ident_t[:])
                last.then_inc(done, 1)

            def turn_probs(done):
                for g in range(GROUPS):
                    for kc in range(2):
                        for qi in range(2):
                            last = nc.tensor.transpose(bank[:, B_PT + g, kc * S + qi * P:kc * S + (qi + 1) * P],
                                                       probs[:, 2 * g + qi, kc * P:(kc + 1) * P], ident_t[:])
                last.then_inc(done, 1)

            def score(q, k, done):
                for g in range(GROUPS):
                    for qi in range(2):
                        t = 2 * g + qi
                        last = nc.tensor.matmul(bank[:, B_SCORE + g, qi * S:(qi + 1) * S], q[:, t * P:(t + 1) * P],
                                                k[:, g * S:(g + 1) * S], start=True, stop=True)
                last.then_inc(done, 1)

            def values(v_tok, done):
                for g in range(GROUPS):
                    for kc in range(2):
                        last = nc.tensor.matmul(bank[:, B_MISC, g * S:(g + 1) * S], v_tok[:, 2 * g + kc],
                                                probs_T[:, g, kc], start=kc == 0, stop=kc == 1)
                last.then_inc(done, 1)

            def sum_and_rotate(e):
                pe.wait_ge(qk_sq_ready, e + 1)
                sum_tokens(qk_sq, B_NORM)
                pe.wait_ge(qk_gain_ready, e + 1)
                nc.tensor.matmul(bank[:, B_MISC], rot_t[:], qk_gain[:], start=True, stop=True).then_inc(qk_rotated, 1)

            def flip_bias(first, end):
                flat = bias_flipped[:].rearrange("p h e c -> p (h e c)")
                for i in range(first, end):
                    nc.tensor.matmul(bank[:, B_SCORE + i % 4], flip_t[:], flat[:, i * T:(i + 1) * T], start=True,
                                     stop=True).then_inc(flipped, 1)

            def sum_x():
                pe.wait_ge(ones_set, 2)
                pe.wait_ge(x_sq_added, KT)
                sum_tokens(sq_sum, B_NORM)

            def head(j, r):
                n0 = j * GROUP_UNITS
                e0 = j * (PER_KV + 1)
                n = r * HEAD_UNITS + (n0 + 2)
                hd = r + j * PER_KV
                unit(n, 0, tall(0))
                unit(n + 1, 1, tall(1))
                sum_and_rotate(r + (e0 + 1))
                unit(n + 2, 0, tall(0), hooks={HALF: lambda: spread(r + (e0 + 2), B_NORM)})
                pe.wait_ge(rope_done, r + (e0 + 2))
                score(q_rope, k_rope, score_b)
                unit(n + 3, 1, tall(1))
                pe.wait_ge(probs_b, hd * TT + TT)
                turn_probs(turned_b)
                pe.wait_ge(unit_read, n + 4)
                score(qa_f, ka_f, score_a)
                unit(n + 4, 0, tall(0))
                pe.wait_ge(unit_read, n + 5)
                turn_values(va_f, B_NORM, va_turned)
                pe.wait_ge(pT_b, hd * 2 + 2)
                pe.wait_ge(vb_tok_ready, j + 1)
                values(vb_tok, head_b)
                unit(n + 5, 1, tall(1))
                pe.wait_ge(probs_a, hd * TT + TT)
                turn_probs(turned_a)
                unit(n + 6, 0, tall(0))
                pe.wait_ge(pT_a, hd * 2 + 2)
                pe.wait_ge(va_tok_ready, hd + 1)
                pe.wait_ge(head_b_read, hd + 1)
                values(va_tok, head_a)
                unit(n + 7, 1, tall(1))

            for j in range(KV):
                n0 = j * GROUP_UNITS
                e0 = j * (PER_KV + 1)
                if j == 0:
                    unit(0, 0, tall(0), gate=lambda k: pe.wait_ge(x_lo_ready, k + 1), free=False)
                    unit(1, 1, tall(1), hooks={4: sum_x, 12: lambda: spread(0, B_NORM)})
                    pe.wait_ge(const_landed, 48)
                    sum_and_rotate(e0)
                    pe.wait_ge(table_landed, 16 * 2 * HEADS)
                    pe.wait_ge(mask_landed, 32)
                    flip_bias(0, 4)
                else:
                    unit(n0, 0, tall(0))
                    unit(n0 + 1, 1, tall(1), hooks={HALF: lambda: sum_and_rotate(e0)})
                spread(e0 + 1, B_NORM)
                if j == 0:
                    pe.wait_ge(bias_read, 4)
                    flip_bias(4, BIAS_PARTS)
                pe.wait_ge(unit_read, n0 + 3)
                turn_values(vb_f, B_PT, vb_turned)
                with pe.Fori(0, PER_KV) as r:
                    head(j, r)

            def branch(slot):
                return [(2 * slot + k // HEADS, head_hi[:, k], head_lo[:, k], k % HEADS == 0,
                         k % HEADS == HEADS - 1) for k in range(KT)]

            unit(N_BRANCH, 0, branch(0), gate=lambda k: pe.wait_ge(head_lo_ready, k + 1))
            unit(N_BRANCH + 1, 1, branch(1))
            with pe.Fori(1, KT // 2) as i:
                for slot in range(2):
                    unit(i * 2 + (N_BRANCH + slot), slot, branch(slot))
            unit(N_OUT, 0, tall(0), gate=lambda k: pe.wait_ge(mix_lo_ready, k + 1))
            unit(N_OUT + 1, 1, tall(1))
            with pe.Fori(1, KT // 2) as i:
                for m in range(2):
                    unit(i * 2 + (N_OUT + m), m, tall(m))

            def embed_unit(n, banks, squares, norm, b, sum_at, spread_at, taken):
                terms = [(banks[half][m], p_hi[:, k], p_lo[:, k], k == 0, k == 1)
                         for half in range(2) for k in range(2) for m in range(4)]

                def sums_hook():
                    pe.wait_ge(sq_added, squares)
                    sum_tokens(sq_sum, b)

                def gate(idx):
                    if HALF <= idx < HALF + 4 and banks[1][idx - HALF] in banks[0]:
                        pe.wait_ge(embed_read, taken + banks[0].index(banks[1][idx - HALF]) + 1)

                unit(n, n % 2, terms, hooks={sum_at: sums_hook, spread_at: lambda: spread(norm, b)}, gate=gate,
                     free=False, half_sem=embed_half)

            pe.wait_ge(p_lo_ready, 1)
            pe.wait_ge(unit_read, N_EMBED_A)
            embed_unit(N_EMBED_A, EMBED_A_BANKS, KT + 1, NORM_MIX, B_NORM, 4, HALF, 0)

            def sum_h_square(k):
                pe.wait_ge(h_sq_ready, k + 1)
                for t in range(TT):
                    last = nc.tensor.matmul(bank[:, B_NORM, t:t + 1], sq[:, k % 2, t * P:(t + 1) * P],
                                            ones[:, 0:1], start=k == 0 and t == 0, stop=k == KT - 1,
                                            skip_group_check=True)
                last.then_inc(norm_summed if k == KT - 1 else h_sq_summed, 1)

            pe.wait_ge(rstd_ready, 2)
            unit(N_FFN, N_FFN % 2, tall(IN_BANKS[0]), gate=lambda k: pe.wait_ge(resid_lo_ready, k + 1), free=False,
                 hooks={k + 1: (lambda k=k: sum_h_square(k)) for k in range(KT - 1)})
            sum_h_square(KT - 1)
            unit(N_FFN + 1, (N_FFN + 1) % 2, tall(IN_BANKS[1]), free=False,
                 hooks={HALF: lambda: spread(NORM_FFN_IN, B_NORM)})
            pe.wait_ge(embed_read, 8)

            def ffn_in(n, first):
                for i in range(first, IN_UNITS):
                    unit(n + i, (N_FFN + i) % 2, tall(IN_BANKS[i]), fillers=1)

            def ffn_out(n, f):
                for u in range(OUT_UNITS):
                    terms = [(OUT_BANKS[u] + m, hid_hi[:, k], hid_lo[:, k], k == 0, k == CH - 1)
                             for k in range(CH) for m in range(4)]

                    def gate(idx):
                        if idx % 4 == 0:
                            pe.wait_ge(hid_lo_ready, f + (idx // 4 + 1))
                    unit(n + u, (N_FFN + u) % 2, terms, fillers=1, gate=gate if u == 0 else None)

            ffn_in(N_FFN, 2)
            with pe.Fori(1, CHUNKS) as c:
                n = c * CHUNK_UNITS + (N_FFN - OUT_UNITS)
                ffn_out(n, c * CH - CH)
                ffn_in(n + OUT_UNITS, 0)
            ffn_out(N_EMBED_B - OUT_UNITS, FT - CH)
            pe.wait_ge(unit_read, N_EMBED_B - 1)
            embed_unit(N_EMBED_B, EMBED_B_BANKS, 2 * KT + 2, NORM_FFN, 0, HALF, 12, 8)
            pe.wait_ge(embed_read, 12)
            unit(N_PLE, N_PLE % 2, tall(PLE_BANKS[0]), gate=lambda k: pe.wait_ge(resid_lo_ready, KT + k + 1), free=False)
            unit(N_PLE + 1, (N_PLE + 1) % 2, tall(PLE_BANKS[1]), free=False)
            with pe.Fori(1, KT // 2) as i:
                for m in range(2):
                    pe.wait_ge(ple_sig, i * 2 + (m - 1))
                    unit(i * 2 + (N_PLE + m), (N_PLE + m) % 2, tall(PLE_BANKS[m]), free=False)
            pe.wait_ge(sq_added, 3 * KT + 3)
            sum_tokens(sq_sum, 0)
            spread(NORM_PLE, 0)


def kernel(x_prompt, x_sample, p_prompt, p_sample, g_pre_mix, w_in, rpb, g_q, g_k, w_branch_a, w_branch_b,
           w_out, g_post_mix, g_pre_ffn, w_ffn_in, w_ffn_out, g_post_ffn, w_ple, w_ple_gate, g_ple):
    import concourse.bacc as bacc
    from concourse.bass_utils import run_bass_kernel_spmd

    def lay(a):
        return np.ascontiguousarray(a)

    def column(g):
        return np.asarray(g)[0].reshape(KT, P).T

    feeds = {
        "xT": lay(np.concatenate([np.asarray(x_prompt)[0], np.asarray(x_sample)[0]]).T),
        "pT": lay(np.concatenate([np.asarray(p_prompt)[0, 0], np.asarray(p_sample)[0, 0]]).T),
        "gains": lay(np.stack([column(g) for g in (g_pre_mix, g_post_mix, g_pre_ffn, g_post_ffn, g_ple)], axis=1)),
        "gains_qk": lay(np.stack([np.asarray(g_q)[0], np.asarray(g_k)[0]], axis=1)),
        "w_in": lay(np.asarray(w_in)[0]),
        "rpb": lay(np.asarray(rpb)[0].reshape(-1, 2 * NA_COLS - 1)),
        "w_branch_a": lay(np.asarray(w_branch_a)[0]),
        "w_branch_b": lay(np.asarray(w_branch_b)[0]),
        "w_out": lay(np.asarray(w_out)[0]),
        "w_ffn_in": lay(np.asarray(w_ffn_in)[0]),
        "w_ffn_out": lay(np.asarray(w_ffn_out)[0]),
        "w_ple": lay(np.asarray(w_ple)[0]),
        "w_ple_gate": lay(np.asarray(w_ple_gate)[0]),
    }
    feeds.update(shape_constants())
    nc = bacc.Bacc("TRN2", target_bir_lowering=False, num_devices=1)
    aps = {name: nc.dram_tensor(name, a.shape, mybir.dt.from_np(a.dtype), kind="ExternalInput").ap()
           for name, a in feeds.items()}
    aps["yT"] = nc.dram_tensor("yT", (D, T), F32, kind="ExternalOutput").ap()
    build(nc, **aps)
    y = run_bass_kernel_spmd(nc, [feeds], core_ids=[0]).results[0]["yT"]
    return lay(y[:, :S].T)[None], lay(y[:, S:].T)[None]
```

```python
from contextlib import ExitStack

import numpy as np

import concourse.bass as bass
from concourse import mybir

F32 = mybir.dt.float32
F32R = mybir.dt.float32r
ALU = mybir.AluOpType
ACT = mybir.ActivationFunctionType
AX_X = mybir.AxisListType.X

P = 128
T = 512
GROUPS = 2
S = T // GROUPS
TT = T // P
D = 2048
KT = D // P
DH = 128
HEADS = 8
KV = 2
PER_KV = HEADS // KV
GRID = 64
NA_COLS = 16
NA_ROWS_MAX = 8
DF = 5632
FT = DF // P
CH = 4
CHUNKS = FT // CH
PLE = 256
EPS = 1e-6
SCALE = DH ** -0.5
NEG = -1e30
HALF = 8
PADC = 128
E_ROWS = 6

C_QA, C_KA, C_VA = 0, HEADS * DH, 2 * HEADS * DH
C_QB = 3 * HEADS * DH
C_KB = C_QB + HEADS * DH
C_VB = C_KB + KV * DH
C_GA = C_VB + KV * DH
C_GB = C_GA + D

HEAD_UNITS = 8
GROUP_UNITS = 2 + PER_KV * HEAD_UNITS
N_BRANCH = KV * GROUP_UNITS
N_OUT = N_BRANCH + KT
N_EMBED_A = N_OUT + KT
N_FFN = N_EMBED_A + 1
IN_UNITS, OUT_UNITS = 2 * CH, KT // 4
CHUNK_UNITS = IN_UNITS + OUT_UNITS
N_EMBED_B = N_FFN + CHUNKS * CHUNK_UNITS
N_PLE = N_EMBED_B + 1
N_END = N_PLE + KT

NORM_MIX = 1 + KV * (1 + PER_KV)
NORM_FFN_IN = NORM_MIX + 1
NORM_FFN = NORM_MIX + 2
NORM_PLE = NORM_MIX + 3

G_PRE, G_POST, G_FFN, G_PFFN, G_PLE = range(5)
B_SCORE, B_PT, B_NORM, B_MISC = 2, 4, 6, 7
IN_BANKS = (4, 5, 6, 7, 0, 1, 2, 3)
OUT_BANKS = (4, 0, 4, 0)
EMBED_A_BANKS = ((2, 3, 7, 0), (1, 2, 3, 7))
EMBED_B_BANKS = ((4, 5, 6, 7), (1, 2, 3, 4))
SCALED_BY_DVE = (0,)
Y_BY_POOL = (1, 4, 7, 10, 13)
Y_BY_DVE = tuple(k for k in range(KT) if k not in Y_BY_POOL)
SCALED_BY_POOL = tuple(k for k in range(KT) if k not in SCALED_BY_DVE)
PLE_BANKS = (6, 7)
LAG = 5
X_SQ_BY_ACT = 12
X_PARTS = ((0, 1), (1, 4), (4, 8), (8, 12), (12, 16))
BIAS_PARTS = HEADS * E_ROWS * GRID // T


def shape_constants():
    half = DH // 2
    inv = (np.float32(10000.0) ** (-np.arange(0, half, 2, dtype=np.float32) / np.float32(half))).astype(np.float32)
    t = np.arange(T) % S
    ang = np.zeros((P, T), np.float32)
    for d in range(DH):
        pos = (t // GRID if d < half else t % GRID).astype(np.float32)
        ang[d] = pos * inv[d % (half // 2)]
    cos, sin = np.cos(ang).astype(np.float32), np.sin(ang).astype(np.float32)
    rot = np.zeros((P, P), np.float32)
    for m in range(P):
        if m % half < half // 2:
            rot[m + half // 2, m] = -1.0
        else:
            rot[m - half // 2, m] = 1.0
    flip = np.zeros((P, P), np.float32)
    for m in range(P):
        flip[(m // GRID) * GRID + GRID - 1 - m % GRID, m] = 1.0
    qc = np.arange(P)[:, None] % GRID
    kc = np.arange(GRID)[None, :]
    first = np.clip(qc - NA_COLS // 2, 0, GRID - NA_COLS)
    mask = np.where((kc >= first) & (kc < first + NA_COLS), 0.0, NEG).astype(np.float32)
    return {"rope_cos": cos, "rope_sin": sin, "rope_rot": rot, "flip": flip, "col_mask": mask,
            "ident": np.eye(P, dtype=np.float32)}


def build(nc, xT, pT, gains, gains_qk, w_in, rpb, w_branch_a, w_branch_b, w_out, w_ffn_in, w_ffn_out,
          w_ple, w_ple_gate, rope_cos, rope_sin, rope_rot, flip, col_mask, ident, yT):
    ctx = ExitStack()
    with ctx:
        KB = 1024
        R_X = 16512
        R_Q = R_X + 64 * KB
        R_O = R_Q + 64 * KB
        R_W = R_O + 32 * KB
        R_S = R_W + 40 * KB

        def at(name, off, shape, dt=F32):
            return nc.alloc_sbuf_tensor_at(name, shape, dt, offset=off)

        act_hi = at("act_hi", R_X, [P, KT, T], F32R)
        act_lo = at("act_lo", R_X + 32 * KB, [P, KT, T], F32R)
        bias = at("bias", R_Q, [P, HEADS, E_ROWS, GRID])
        cos_t = at("cos_t", R_Q + 12 * KB, [P, T])
        sin_t = at("sin_t", R_Q + 14 * KB, [P, T])
        k_rope = at("k_rope", R_Q + 16 * KB, [P, T])
        vb_tok_hi = at("vb_tok_hi", R_Q + 18 * KB, [P, TT, DH], F32R)
        vb_tok_lo = at("vb_tok_lo", R_Q + 56 * KB, [P, TT, DH], F32R)
        qa_f = at("qa_f", R_Q + 20 * KB, [P, T])
        ka_f = at("ka_f", R_Q + 22 * KB, [P, T])
        va_f = at("va_f", R_Q + 24 * KB, [P, T])
        va_tok_hi = at("va_tok_hi", R_Q + 26 * KB, [P, TT, DH], F32R)
        va_tok_lo = at("va_tok_lo", R_Q + 58 * KB, [P, TT, DH], F32R)
        q_rope = at("q_rope", R_Q + 28 * KB, [P, T])
        qk_raw = at("qk_raw", R_Q + 30 * KB, [P, T])
        qk_hi = at("qk_hi", R_Q + 32 * KB, [P, T], F32R)
        qk_sq = at("qk_sq", R_Q + 34 * KB, [P, T])
        rope_c = at("rope_c", R_Q + 36 * KB, [P, T])
        qk_lo = at("qk_lo", R_Q + 38 * KB, [P, T], F32R)
        rope_s = at("rope_s", R_Q + 38 * KB, [P, T])
        x_sq = at("x_sq", R_Q + 16 * KB, [P, X_SQ_BY_ACT, T])
        x_sq_last = at("x_sq_last", R_Q, [P, KT - X_SQ_BY_ACT, T])
        na_scores = at("na_scores", R_Q + 40 * KB, [P, TT, S])
        probs = at("probs", R_Q + 40 * KB, [P, TT, S])
        probs_T_hi = at("probs_T_hi", R_Q + 44 * KB, [P, GROUPS, 2, S], F32R)
        probs_T_lo = at("probs_T_lo", R_Q + 48 * KB, [P, GROUPS, 2, S], F32R)
        vb_f = at("vb_f", R_Q + 52 * KB, [P, T])
        rot_f = at("rot_f", R_Q + 54 * KB, [P, P])
        rot_t = at("rot_t", R_Q + 54 * KB + 512, [P, P], F32R)
        gate_out = at("gate_out", R_Q + 60 * KB, [P, 2, T])
        bias_flipped = at("bias_flipped", R_Q + 40 * KB, [P, HEADS, E_ROWS, GRID])
        flip_t = at("flip_t", R_Q + 55 * KB, [P, P])
        mask_t = at("mask_t", R_Q + 55 * KB + 512, [P, GRID])
        rpb_pad = at("rpb_pad", R_Q + 53 * KB, [HEADS * (2 * NA_ROWS_MAX - 1), PADC])
        head_hi = at("head_hi", R_Q, [P, KT, T], F32R)
        head_lo = at("head_lo", R_Q + 32 * KB, [P, KT, T], F32R)
        x_f = at("x_f", R_O, [P, KT, T])
        head_f = at("head_f", R_O, [P, KT, T])
        gate_in = at("gate_in", R_O, [P, 2, 2, T])
        mix_a = at("mix_a", R_O + 8 * KB, [P, T])
        mix_b = at("mix_b", R_O + 10 * KB, [P, T])
        resid = at("resid", R_O, [P, KT, T])
        hid_hi = at("hid_hi", R_Q, [P, CH, T], F32R)
        hid_lo = at("hid_lo", R_Q + 8 * KB, [P, CH, T], F32R)
        embed = at("embed", R_Q, [P, 8, T])
        sums = at("sums", R_Q + 16 * KB, [P, KT, T])
        p_hi = at("p_hi", R_Q + 48 * KB, [P, 2, T], F32R)
        p_lo = at("p_lo", R_Q + 52 * KB, [P, 2, T], F32R)
        p_f = at("p_f", R_Q + 56 * KB, [P, 2, T])
        tmp = at("tmp", R_Q + 56 * KB, [P, 2, T])
        sq = at("sq", R_Q + 60 * KB, [P, 2, T])
        w_raw = at("w_raw", R_W, [P, 2, HALF, P])
        w_hi = at("w_hi", R_W + 8 * KB, [P, 4, HALF, P], F32R)
        w_lo = at("w_lo", R_W + 24 * KB, [P, 4, HALF, P], F32R)
        ident_t = at("ident_t", R_S, [P, P])
        ones = at("ones", R_S + 512, [P, P])
        rstd = at("rstd", R_S + 1024, [P, T])
        sq_sum = at("sq_sum", R_S + 3 * KB, [P, T])
        diag = at("diag", R_S + 5 * KB, [P, TT, P])
        g_t = at("g_t", R_S + 7 * KB, [P, 5, KT])
        tiny = R_S + 7 * KB + 320
        gqk_t = at("gqk_t", tiny, [P, 2])
        minus_half = at("minus_half", tiny + 32, [P, TT])
        var = at("var", tiny + 64, [P, TT])
        rs = at("rs", tiny + 96, [P, TT])
        top = at("top", tiny + 128, [P, 2, TT])
        neg_top = at("neg_top", tiny + 160, [P, 2, TT])
        psum_p = at("psum_p", tiny + 192, [P, 2, TT])
        inv_p = at("inv_p", tiny + 224, [P, 2, TT])

        bank = ctx.enter_context(nc.psum_tensor("bank", [P, 8, T], F32))

        gate_dram = nc.dram_tensor("gate_dram", [KT, 2, P, T], F32, kind="Internal")
        embed_dram = nc.dram_tensor("embed_dram", [8, P, T], F32, kind="Internal")
        pad_dram = nc.dram_tensor("pad_dram", [HEADS * (2 * NA_ROWS_MAX - 1), PADC], F32, kind="Internal")

        def sem(name):
            return ctx.enter_context(nc.semaphore(name))

        raw_landed = [sem("raw_landed0"), sem("raw_landed1")]
        hi_ready = sem("hi_ready")
        lo_ready = sem("lo_ready")
        unit_done = sem("unit_done")
        unit_read = sem("unit_read")
        x_landed = [sem(f"x_landed{i}") for i in range(5)]
        const_landed = sem("const_landed")
        mask_landed = sem("mask_landed")
        ident_landed = sem("ident_landed")
        gains_landed = sem("gains_landed")
        ones_set = sem("ones_set")
        warmed = sem("warmed")
        pad_set = sem("pad_set")
        rpb_landed = sem("rpb_landed")
        pad_stored = sem("pad_stored")
        table_landed = sem("table_landed")
        flipped = sem("flipped")
        bias_read = sem("bias_read")
        x_hi_ready = sem("x_hi_ready")
        x_lo_ready = sem("x_lo_ready")
        x_sq_p = sem("x_sq_p")
        x_sq_s = sem("x_sq_s")
        x_sq_added = sem("x_sq_added")
        rstd_ready = sem("rstd_ready")
        norm_summed = sem("norm_summed")
        norm_var = sem("norm_var")
        norm_root = sem("norm_root")
        norm_diag = sem("norm_diag")
        norm_spread = sem("norm_spread")
        qk_sq_ready = sem("qk_sq_ready")
        rot_ready = sem("rot_ready")
        qk_hi_ready = sem("qk_hi_ready")
        qk_lo_ready = sem("qk_lo_ready")
        qk_rotated = sem("qk_rotated")
        rope_s_ready = sem("rope_s_ready")
        rope_c_ready = sem("rope_c_ready")
        rope_added = sem("rope_added")
        rope_done = sem("rope_done")
        vb_turned = sem("vb_turned")
        vb_hi_ready = sem("vb_hi_ready")
        vb_lo_ready = sem("vb_lo_ready")
        score_b = sem("score_b")
        top_b = sem("top_b")
        neg_top_b = sem("neg_top_b")
        exp_b = sem("exp_b")
        inv_b = sem("inv_b")
        probs_b = sem("probs_b")
        turned_b = sem("turned_b")
        pT_hi_b = sem("pT_hi_b")
        pT_lo_b = sem("pT_lo_b")
        head_b = sem("head_b")
        head_b_read = sem("head_b_read")
        score_a = sem("score_a")
        biased_a = sem("biased_a")
        top_a = sem("top_a")
        neg_top_a = sem("neg_top_a")
        exp_a = sem("exp_a")
        inv_a = sem("inv_a")
        probs_a = sem("probs_a")
        va_turned = sem("va_turned")
        va_hi_ready = sem("va_hi_ready")
        va_lo_ready = sem("va_lo_ready")
        turned_a = sem("turned_a")
        pT_hi_a = sem("pT_hi_a")
        pT_lo_a = sem("pT_lo_a")
        head_a = sem("head_a")
        head_a_read = sem("head_a_read")
        gate_stored = [sem("gate_stored0"), sem("gate_stored1")]
        head_hi_ready = sem("head_hi_ready")
        head_lo_ready = sem("head_lo_ready")
        gate_landed = [sem("gate_landed0"), sem("gate_landed1")]
        gates_open = sem("gates_open")
        mixed = sem("mixed")
        mix_hi_ready = sem("mix_hi_ready")
        mix_lo_ready = sem("mix_lo_ready")
        resid_landed = sem("resid_landed")
        p_landed = sem("p_landed")
        p_hi_ready = sem("p_hi_ready")
        p_lo_ready = sem("p_lo_ready")
        sq_ready = sem("sq_ready")
        sq_added = sem("sq_added")
        gained = sem("gained")
        scaled_v = sem("scaled_v")
        scaled_p = sem("scaled_p")
        resid_ready = sem("resid_ready")
        resid_hi_ready = sem("resid_hi_ready")
        resid_lo_ready = sem("resid_lo_ready")
        h_sq_ready = sem("h_sq_ready")
        h_sq_summed = sem("h_sq_summed")
        embed_half = sem("embed_half")
        embed_read = sem("embed_read")
        embed_stored = sem("embed_stored")
        embed_landed = sem("embed_landed")
        sums_zero = sem("sums_zero")
        silu_ready = sem("silu_ready")
        hid_ready = sem("hid_ready")
        hid_hi_ready = sem("hid_hi_ready")
        hid_lo_ready = sem("hid_lo_ready")
        ple_sig = sem("ple_sig")
        ple_ready = sem("ple_ready")
        y_scaled_v = sem("y_scaled_v")
        y_scaled_p = sem("y_scaled_p")
        y_ready_v = sem("y_ready_v")
        y_ready_p = sem("y_ready_p")
        y_stored = sem("y_stored")

        w_in_v = w_in.rearrange("(k p) n -> p k n", p=P)
        wa_v = w_branch_a.rearrange("(k p) n -> p k n", p=P)
        wb_v = w_branch_b.rearrange("(k p) n -> p k n", p=P)
        wo_v = w_out.rearrange("(k p) n -> p k n", p=P)
        wi_v = w_ffn_in.rearrange("(k p) n -> p k n", p=P)
        wf_v = w_ffn_out.rearrange("(k p) n -> p k n", p=P)
        wp_v = w_ple.rearrange("(k p) n -> p k n", p=P)
        wg_v = w_ple_gate.rearrange("(k p) n -> p k n", p=P)
        x_v = xT.rearrange("(k p) t -> p k t", p=P)
        p_v = pT.rearrange("(k p) t -> p k t", p=P)
        y_v = yT.rearrange("(k p) t -> p k t", p=P)

        block = ctx.enter_context(nc.Block())

        @block.sync
        def _(sp):
            def fetch(n, half, src, shape=None):
                sp.wait_ge(lo_ready, 2 * n + half + 1)
                dst = w_raw[:, half] if shape is None else w_raw[:, half].rearrange("p s c -> p (s c)").rearrange(
                    "p (k c) -> p k c", k=shape)
                sp.dma_start(dst, src).then_inc(raw_landed[half], 16)

            def fetch_tall(n, view, col):
                for half in range(2):
                    fetch(n, half, view[:, half * HALF:(half + 1) * HALF, bass.ds(col, P)])

            for i, (first, end) in enumerate(X_PARTS):
                sp.dma_start(x_f[:, first:end], x_v[:, first:end]).then_inc(x_landed[i], 16)
                if i == 0:
                    fetch_tall(0, w_in_v, C_KB)
            sp.dma_start(ident_t[:], ident).then_inc(ident_landed, 16)
            sp.dma_start(mask_t[:], col_mask).then_inc(mask_landed, 16)
            sp.dma_start(flip_t[:], flip).then_inc(mask_landed, 16)
            sp.dma_start(cos_t[:], rope_cos).then_inc(const_landed, 16)
            sp.dma_start(sin_t[:], rope_sin).then_inc(const_landed, 16)
            sp.dma_start(rot_f[:], rope_rot).then_inc(const_landed, 16)
            for j in range(KV):
                n0 = j * GROUP_UNITS
                if j:
                    fetch_tall(n0, w_in_v, C_KB + j * DH)
                fetch_tall(n0 + 1, w_in_v, C_VB + j * DH)
                with sp.Fori(1, PER_KV + 1) as r:
                    n = r * HEAD_UNITS + (n0 + 2 - HEAD_UNITS)
                    h = j * PER_KV - 1
                    fetch_tall(n, w_in_v, r * DH + (C_QB + h * DH))
                    fetch_tall(n + 1, w_in_v, r * DH + (C_KA + h * DH))
                    fetch_tall(n + 2, w_in_v, r * DH + (C_QA + h * DH))
                    fetch_tall(n + 3, w_in_v, r * DH + (C_VA + h * DH))
                    for i in range(2):
                        fetch_tall(n + 4 + i, w_in_v, r * 2 * P + (C_GA + (2 * h + i) * P))
                    for i in range(2):
                        fetch_tall(n + 6 + i, w_in_v, r * 2 * P + (C_GB + (2 * h + i) * P))
            for m in range(2):
                fetch(N_BRANCH + m, 0, wa_v[:, :, m * P:(m + 1) * P])
                fetch(N_BRANCH + m, 1, wb_v[:, :, m * P:(m + 1) * P])
            for slot in range(2):
                sp.wait_ge(gate_stored[slot], 16 * KT)
            sp.wait_ge(head_lo_ready, KT)
            for slot in range(2):
                sp.dma_start(gate_in[:, slot], gate_dram.ap()[slot].rearrange("g p t -> p g t")).then_inc(
                    gate_landed[slot], 16)
            with sp.Fori(1, KT // 2) as i:
                for slot in range(2):
                    n = i * 2 + (N_BRANCH + slot)
                    fetch(n, 0, wa_v[:, :, bass.ds(i * 2 * P + slot * P, P)])
                    fetch(n, 1, wb_v[:, :, bass.ds(i * 2 * P + slot * P, P)])
                    sp.wait_ge(unit_read, n)
                    sp.dma_start(gate_in[:, slot], gate_dram.ap()[bass.ds(i * 2 + slot, 1)].rearrange(
                        "m g p t -> p (m g) t")).then_inc(gate_landed[slot], 16)
            for m in range(2):
                fetch_tall(N_OUT + m, wo_v, m * P)
            sp.wait_ge(mix_lo_ready, KT)
            sp.dma_start(p_f[:], p_v).then_inc(p_landed, 16)
            sp.dma_start(resid[:, 0:2], x_v[:, 0:2]).then_inc(resid_landed, 16)
            with sp.Fori(1, KT // 2) as i:
                for m in range(2):
                    fetch_tall(i * 2 + (N_OUT + m), wo_v, i * 2 * P + m * P)
                sp.dma_start(resid[:, bass.ds(i * 2, 2)], x_v[:, bass.ds(i * 2, 2)]).then_inc(resid_landed, 16)

            def fetch_embed(n, first):
                for half in range(2):
                    fetch(n, half, wp_v[:, :, (first + 4 * half) * P:(first + 4 * half + 4) * P], 2)

            def fetch_in(n, f):
                for i in range(CH):
                    fetch_tall(n + 2 * i, wi_v, f * P + i * P)
                    fetch_tall(n + 2 * i + 1, wi_v, f * P + (DF + i * P))

            def fetch_out(n, f):
                for u in range(OUT_UNITS):
                    for half in range(2):
                        fetch(n + u, half, wf_v[:, bass.ds(f + 2 * half, 2), u * 4 * P:(u + 1) * 4 * P], 2)

            fetch_embed(N_EMBED_A, 0)
            fetch_in(N_FFN, 0)
            with sp.Fori(1, CHUNKS) as c:
                n = c * CHUNK_UNITS + (N_FFN - OUT_UNITS)
                fetch_out(n, c * CH - CH)
                fetch_in(n + OUT_UNITS, c * CH)
            fetch_out(N_EMBED_B - OUT_UNITS, FT - CH)
            fetch_embed(N_EMBED_B, 8)
            for m in range(2):
                fetch_tall(N_PLE + m, wg_v, m * P)
            sp.wait_ge(resid_ready, KT + 8)
            sp.dma_start(sums[:, 0:8], embed_dram.ap().rearrange("m p t -> p m t")).then_inc(embed_landed, 16)
            with sp.Fori(1, KT // 2) as i:
                for m in range(2):
                    fetch_tall(i * 2 + (N_PLE + m), wg_v, i * 2 * P + m * P)
            for k in range(KT):
                if k in Y_BY_POOL:
                    sp.wait_ge(y_ready_p, Y_BY_POOL.index(k) + 1)
                else:
                    sp.wait_ge(y_ready_v, Y_BY_DVE.index(k) + 1)
                sp.dma_start(y_v[:, k], resid[:, k]).then_inc(y_stored, 16)
            sp.wait_ge(y_stored, 16 * KT)

        @block.gpsimd
        def _(pool):
            def root(q):
                pool.wait_ge(norm_var, q + 1)
                nc.gpsimd.tensor_tensor(rs[:], var[:], minus_half[:], ALU.pow).then_inc(norm_root, 1)

            nc.gpsimd.memset(rpb_pad[:], 0.0).then_inc(pad_set, 1)
            nc.gpsimd.memset(ones[:], 1.0).then_inc(ones_set, 1)
            nc.gpsimd.memset(minus_half[:], -0.5).then_inc(ones_set, 1)
            for k in range(X_SQ_BY_ACT):
                for i, (first, _) in enumerate(X_PARTS):
                    if k == first:
                        pool.wait_ge(x_landed[i], 16)
                nc.gpsimd.tensor_tensor(x_sq[:, k], x_f[:, k], x_f[:, k], ALU.mult).then_inc(x_sq_p, 1)
            pool.wait_ge(ones_set, 2)
            root(0)
            nc.gpsimd.memset(sq_sum[:], 0.0).then_inc(sq_added, 1)
            with pool.Fori(1, NORM_MIX) as q:
                root(q)
            root(NORM_MIX)

            def scale(which):
                pool.wait_ge(rstd_ready, 2 + 2 * which)
                for k in SCALED_BY_POOL:
                    pool.wait_ge(gained, which * KT + k + 1)
                    nc.gpsimd.tensor_tensor(sums[:, k], sums[:, k], rstd[:], ALU.mult).then_inc(scaled_p, 1)

            scale(0)
            root(NORM_FFN_IN)
            pool.wait_ge(resid_ready, KT)
            nc.gpsimd.memset(sums[:], 0.0).then_inc(sums_zero, 1)
            nc.gpsimd.memset(sq_sum[:], 0.0).then_inc(sq_added, 1)
            root(NORM_FFN)
            nc.gpsimd.memset(sq_sum[:], 0.0).then_inc(sq_added, 1)
            scale(1)
            root(NORM_PLE)
            pool.wait_ge(rstd_ready, 5)
            for i, k in enumerate(Y_BY_POOL):
                pool.wait_ge(gained, 2 * KT + k + 1)
                nc.gpsimd.tensor_tensor(sums[:, k], sums[:, k], rstd[:], ALU.mult).then_inc(y_scaled_p, 1)
                pool.wait_ge(y_scaled_p, i + 1)
                nc.gpsimd.tensor_tensor(resid[:, k], resid[:, k], sums[:, k], ALU.add).then_inc(y_ready_p, 1)

        @block.scalar
        def _(act):
            def split_hi(n, par, half, free=True):
                act.wait_ge(raw_landed[half], 16 * n + 16)
                nc.scalar.copy(w_hi[:, 2 * par + half], w_raw[:, half]).then_inc(hi_ready, 1)

            def next_hi(n, par):
                act.wait_ge(unit_done, n + 1)
                for half in range(2):
                    split_hi(n + 2, par, half)

            act.dma_start(g_t[:], gains).then_inc(gains_landed, 16)
            act.dma_start(gqk_t[:], gains_qk).then_inc(gains_landed, 16)
            act.wait_ge(pad_set, 1)
            act.dma_start(rpb_pad[:, 48:48 + 2 * NA_COLS - 1], rpb).then_inc(rpb_landed, 16)

            act.wait_ge(ones_set, 2)
            nc.scalar.copy(psum_p[:, 0], minus_half[:]).then_inc(warmed, 1)
            act.wait_ge(warmed, 1)
            act.wait_ge(gains_landed, 32)

            def x_hi(k):
                for i, (first, _) in enumerate(X_PARTS):
                    if k == first:
                        act.wait_ge(x_landed[i], 16)
                nc.scalar.activation(act_hi[:, k], x_f[:, k], ACT.Identity,
                                     scale=g_t[:, G_PRE, k:k + 1]).then_inc(x_hi_ready, 1)

            split_hi(0, 0, 0)
            for k in range(KT):
                x_hi(k)
                if k == HALF - 3:
                    split_hi(0, 0, 1)
                    act.wait_ge(rpb_landed, 16)
                    act.dma_start(pad_dram.ap(), rpb_pad[:]).then_inc(pad_stored, 16)
            split_hi(1, 1, 0)
            for k in range(X_SQ_BY_ACT, KT):
                nc.scalar.activation(x_sq_last[:, k - X_SQ_BY_ACT], x_f[:, k], ACT.Square).then_inc(x_sq_s, 1)
            split_hi(1, 1, 1)
            act.wait_ge(pad_stored, 16)
            rows = 2 * NA_ROWS_MAX - 1
            for h in range(HEADS):
                for rl in range(2):
                    first = (h * rows + NA_ROWS_MAX - 1 - 2 - rl) * PADC
                    act.dma_start(bias_flipped[rl * GRID:(rl + 1) * GRID, h],
                                  bass.AP(pad_dram, first, [[1, GRID], [PADC, E_ROWS], [1, GRID]])).then_inc(
                                      table_landed, 16)

            act.wait_ge(const_landed, 48)
            nc.scalar.copy(rot_t[:], rot_f[:]).then_inc(rot_ready, 1)

            def head_norm_inputs(n, g):
                act.wait_ge(unit_read, n + 2)
                nc.scalar.activation(qk_sq[:], qk_raw[:], ACT.Square).then_inc(qk_sq_ready, 1)
                nc.scalar.activation(qk_hi[:], qk_raw[:], ACT.Identity,
                                     scale=gqk_t[:, g:g + 1]).then_inc(qk_hi_ready, 1)

            def exps(ready, value, src, which, scale, done):
                act.wait_ge(ready, value)
                for t in range(TT):
                    ins = nc.scalar.activation(probs[:, t], src[:, t], ACT.Exp, bias=neg_top[:, which, t:t + 1],
                                               scale=scale, accum_out=psum_p[:, which, t:t + 1])
                    ins.then_inc(done, 1)

            def evacuate_pT(ready, value, done):
                act.wait_ge(ready, value)
                for g in range(GROUPS):
                    nc.scalar.copy(probs_T_hi[:, g].rearrange("p a b -> p (a b)"), bank[:, B_PT + g]).then_inc(done, 1)

            def store_gate(n, slot, m, which):
                act.wait_ge(unit_read, n + 2)
                act.dma_start(gate_dram.ap()[bass.ds(m, 1), which].rearrange("m p t -> p (m t)"),
                              gate_out[:, slot]).then_inc(gate_stored[slot], 16)

            scores = bank[:, B_SCORE:B_SCORE + 2].rearrange("p g (q s) -> p (g q) s", q=2)

            def head(j, r, last):
                n0 = j * GROUP_UNITS
                n = r * HEAD_UNITS + (n0 + 2)
                hd = r + j * PER_KV
                next_hi(n, 0)
                head_norm_inputs(n, 0)
                next_hi(n + 1, 1)
                next_hi(n + 2, 0)
                exps(neg_top_b, hd + 1, scores, 0, SCALE, exp_b)
                next_hi(n + 3, 1)
                evacuate_pT(turned_b, hd + 1, pT_hi_b)
                exps(neg_top_a, hd + 1, na_scores, 1, 1.0, exp_a)
                next_hi(n + 4, 0)
                store_gate(n + 4, 0, r * 2 + 2 * j * PER_KV, 0)
                act.wait_ge(va_turned, hd + 1)
                nc.scalar.copy(va_tok_hi[:].rearrange("p a b -> p (a b)"), bank[:, B_NORM]).then_inc(va_hi_ready, 1)
                next_hi(n + 5, 1)
                store_gate(n + 5, 1, r * 2 + (2 * j * PER_KV + 1), 0)
                evacuate_pT(turned_a, hd + 1, pT_hi_a)
                next_hi(n + 6, 0)
                store_gate(n + 6, 0, r * 2 + 2 * j * PER_KV, 1)
                if last:
                    act.wait_ge(head_a_read, HEADS)
                    for k in range(KT):
                        nc.scalar.copy(head_hi[:, k], head_f[:, k]).then_inc(head_hi_ready, 1)
                act.wait_ge(unit_done, n + 8)
                store_gate(n + 7, 1, r * 2 + (2 * j * PER_KV + 1), 1)
                next_hi(n + 7, 1)

            for j in range(KV):
                n0 = j * GROUP_UNITS
                next_hi(n0, 0)
                head_norm_inputs(n0, 1)
                next_hi(n0 + 1, 1)
                act.wait_ge(vb_turned, j + 1)
                nc.scalar.copy(vb_tok_hi[:].rearrange("p a b -> p (a b)"), bank[:, B_PT]).then_inc(vb_hi_ready, 1)
                rolled = PER_KV - (j == KV - 1)
                with act.Fori(0, rolled) as r:
                    head(j, r, False)
            head(KV - 1, PER_KV - 1, True)
            with act.Fori(0, KT // 2) as i:
                for slot in range(2):
                    n = i * 2 + (N_BRANCH + slot)
                    act.wait_ge(gate_landed[slot], i * 16 + 16)
                    nc.scalar.activation(gate_in[:, slot], gate_in[:, slot], ACT.Sigmoid).then_inc(gates_open, 1)
                    next_hi(n, slot)
                    act.wait_ge(mixed, i * 2 + (slot + 1))
                    nc.scalar.copy(act_hi[:, bass.ds(i * 2 + slot, 1)], mix_a[:].rearrange(
                        "p (a t) -> p a t", a=1)).then_inc(mix_hi_ready, 1)

            def square(count, slot, starts, tile):
                act.wait_ge(sq_added, count + starts)
                nc.scalar.activation(sq[:, slot:slot + 1], tile, ACT.Square).then_inc(sq_ready, 1)

            def give_gain(count, tile, gain):
                act.wait_ge(sq_ready, count + 1)
                nc.scalar.activation(tile, tile, ACT.Identity, scale=gain).then_inc(gained, 1)

            def square_and_gain(count, slot, starts, tile, gain):
                square(count, slot, starts, tile)
                give_gain(count, tile, gain)

            def out_tile(n, m, par):
                act.wait_ge(unit_read, n + 2)
                square_and_gain(m, par, 1, sums[:, bass.ds(m, 1)], g_t[:, G_POST, bass.ds(m, 1)])
                next_hi(n, par)

            with act.Fori(0, KT // 2 - 1) as i:
                for m in range(2):
                    out_tile(i * 2 + (N_OUT + m), i * 2 + m, m)
            act.wait_ge(p_landed, 16)
            nc.scalar.copy(p_hi[:], p_f[:]).then_inc(p_hi_ready, 1)
            for m in range(KT - 2, KT):
                out_tile(N_OUT + m, m, m % 2)

            def embed_part(first, count, banks):
                for i in range(count):
                    nc.scalar.copy(embed[:, first + i], bank[:, banks[i]]).then_inc(embed_read, 1)

            act.wait_ge(embed_half, 1)
            embed_part(0, 4, EMBED_A_BANKS[0])
            for k in range(KT):
                act.wait_ge(resid_ready, k + 1)
                nc.scalar.activation(act_hi[:, k], resid[:, k], ACT.Identity,
                                     scale=g_t[:, G_FFN, k:k + 1]).then_inc(resid_hi_ready, 1)
                if k >= 2:
                    act.wait_ge(h_sq_summed, k - 1)
                nc.scalar.activation(sq[:, k % 2], resid[:, k], ACT.Square).then_inc(h_sq_ready, 1)
                if k == 8:
                    act.wait_ge(unit_done, N_EMBED_A + 1)
                    split_hi(N_EMBED_A + 2, 0, 0)
            split_hi(N_EMBED_A + 2, 0, 1)
            embed_part(4, 4, EMBED_A_BANKS[1])
            act.wait_ge(embed_read, 8)
            act.dma_start(embed_dram.ap().rearrange("m p t -> p m t"), embed[:]).then_inc(embed_stored, 16)

            def ffn_in(n, f, first=False):
                for i in range(CH):
                    par = (N_FFN + 2 * i) % 2
                    next_hi(n + 2 * i, par)
                    act.wait_ge(unit_read, n + 2 * i + 1)
                    nc.scalar.activation(tmp[:, 0], tmp[:, 0], ACT.Silu).then_inc(silu_ready, 1)
                    act.wait_ge(unit_done, n + 2 * i + 2)
                    split_hi(n + 2 * i + 3, 1 - par, 0)
                    if first and i == 0:
                        act.wait_ge(embed_stored, 16)
                    act.wait_ge(hid_ready, f + i + 1)
                    nc.scalar.copy(hid_hi[:, i], sq[:, 0]).then_inc(hid_hi_ready, 1)
                    split_hi(n + 2 * i + 3, 1 - par, 1)

            def ffn_out(n):
                for u in range(OUT_UNITS):
                    next_hi(n + u, (N_FFN + u) % 2)

            ffn_in(N_FFN, 0, True)
            with act.Fori(1, CHUNKS) as c:
                n = c * CHUNK_UNITS + (N_FFN - OUT_UNITS)
                ffn_out(n)
                ffn_in(n + OUT_UNITS, c * CH)
            for u in range(OUT_UNITS):
                n = N_EMBED_B - OUT_UNITS + u
                next_hi(n, n % 2)
                act.wait_ge(unit_read, n + 1)
                for k in range(4 * u, 4 * u + 4):
                    square(KT + k, k % 2, 1, sums[:, k:k + 1])
                for k in range(4 * u, 4 * u + 4):
                    give_gain(KT + k, sums[:, k:k + 1], g_t[:, G_PFFN, k:k + 1])
            act.wait_ge(embed_half, 2)
            embed_part(0, 4, EMBED_B_BANKS[0])
            for k in range(KT):
                act.wait_ge(resid_ready, KT + k + 1)
                nc.scalar.copy(act_hi[:, k], resid[:, k]).then_inc(resid_hi_ready, 1)
                if k == 3:
                    act.wait_ge(unit_done, N_EMBED_B + 1)
                    split_hi(N_EMBED_B + 2, (N_EMBED_B + 2) % 2, 0)
                if k == 6:
                    split_hi(N_EMBED_B + 2, (N_EMBED_B + 2) % 2, 1)
            embed_part(4, 4, EMBED_B_BANKS[1])

            def ple_tile(n, m, par, slot, more=True):
                act.wait_ge(unit_done, n + 1)
                nc.scalar.activation(tmp[:, 0], bank[:, PLE_BANKS[slot]], ACT.Sigmoid).then_inc(ple_sig, 1)
                if more:
                    next_hi(n, par)
                act.wait_ge(ple_ready, m + 1)
                square_and_gain(m + 2 * KT, slot, 3, sums[:, bass.ds(m, 1)], g_t[:, G_PLE, bass.ds(m, 1)])

            with act.Fori(0, KT // 2 - 1) as i:
                for m in range(2):
                    ple_tile(i * 2 + (N_PLE + m), i * 2 + m, (N_PLE + m) % 2, m)
            for m in range(KT - 2, KT):
                ple_tile(N_PLE + m, m, (N_PLE + m) % 2, m % 2, False)

        @block.vector
        def _(dve):
            def split_lo(n, par, half):
                dve.wait_ge(hi_ready, 2 * n + half + 1)
                nc.vector.tensor_tensor(w_lo[:, 2 * par + half], w_raw[:, half],
                                        w_hi[:, 2 * par + half].bitcast(F32), ALU.subtract).then_inc(lo_ready, 1)

            def next_lo(n, par):
                for half in range(2):
                    split_lo(n + 2, par, half)

            def mean_square(q, width, src_bank):
                dve.wait_ge(norm_summed, q + 1)
                nc.vector.tensor_scalar(var[:], bank[:, src_bank, 0:TT], 1.0 / width, EPS, ALU.mult,
                                        ALU.add).then_inc(norm_var, 1)

            def diagonal(q, first=False):
                dve.wait_ge(norm_root, q + 1)
                if not first:
                    dve.wait_ge(norm_spread, q)
                nc.vector.tensor_tensor(diag[:], ident_t[:].unsqueeze(1).to_broadcast([P, TT, P]),
                                        rs[:].unsqueeze(2).to_broadcast([P, TT, P]), ALU.mult).then_inc(norm_diag, 1)

            def evacuate(n, par, dst):
                dve.wait_ge(unit_done, n + 1)
                nc.vector.tensor_tensor(dst, bank[:, par], rstd[:], ALU.mult).then_inc(unit_read, 1)

            nc.vector.memset(top[:], 0.0).then_inc(lo_ready, 1)
            nc.vector.memset(neg_top[:], 0.0).then_inc(lo_ready, 1)
            nc.vector.memset(inv_p[:], 0.0).then_inc(unit_read, 1)
            dve.wait_ge(gains_landed, 32)

            def x_lo(k):
                dve.wait_ge(x_hi_ready, k + 1)
                nc.vector.scalar_tensor_tensor(act_lo[:, k], x_f[:, k], g_t[:, G_PRE, k:k + 1],
                                               act_hi[:, k].bitcast(F32), ALU.mult, ALU.subtract).then_inc(x_lo_ready, 1)

            split_lo(0, 0, 0)
            for k in range(KT):
                x_lo(k)
                if k == HALF - 2:
                    split_lo(0, 0, 1)
            split_lo(1, 1, 0)
            split_lo(1, 1, 1)
            dve.wait_ge(x_sq_p, 8)
            nc.vector.tensor_tensor(x_sq[:, 0:4], x_sq[:, 0:4], x_sq[:, 4:8], ALU.add).then_inc(x_sq_added, 1)
            dve.wait_ge(x_sq_p, 12)
            dve.wait_ge(x_sq_added, 1)
            nc.vector.tensor_tensor(x_sq[:, 0:4], x_sq[:, 0:4], x_sq[:, 8:12], ALU.add).then_inc(x_sq_added, 1)
            dve.wait_ge(x_sq_s, 4)
            dve.wait_ge(x_sq_added, 2)
            nc.vector.tensor_tensor(x_sq[:, 0:4], x_sq[:, 0:4], x_sq_last[:], ALU.add).then_inc(x_sq_added, 1)
            dve.wait_ge(x_sq_added, 3)
            nc.vector.tensor_tensor(x_sq[:, 0:2], x_sq[:, 0:2], x_sq[:, 2:4], ALU.add).then_inc(x_sq_added, 1)
            dve.wait_ge(x_sq_added, 4)
            nc.vector.tensor_tensor(sq_sum[:], x_sq[:, 0], x_sq[:, 1], ALU.add).then_inc(x_sq_added, 1)
            split_lo(2, 0, 0)

            def bias_parts(first, end):
                dve.wait_ge(mask_landed, 32)
                for i in range(first, end):
                    dve.wait_ge(flipped, i + 1)
                    nc.vector.tensor_tensor(
                        bias[:].rearrange("p h e c -> p (h e) c")[:, 8 * i:8 * i + 8],
                        bank[:, B_SCORE + i % 4].rearrange("p (a c) -> p a c", c=GRID),
                        mask_t[:].unsqueeze(1).to_broadcast([P, 8, GRID]), ALU.add).then_inc(bias_read, 1)

            mean_square(0, D, B_NORM)
            split_lo(2, 0, 1)
            dve.wait_ge(ident_landed, 16)
            diagonal(0, True)
            bias_parts(0, 1)
            dve.wait_ge(norm_spread, 1)
            nc.vector.tensor_copy(rstd[:], bank[:, B_NORM]).then_inc(rstd_ready, 1)
            dve.wait_ge(rstd_ready, 1)

            def low_part(e, g):
                dve.wait_ge(qk_hi_ready, e + 1)
                nc.vector.scalar_tensor_tensor(qk_lo[:], qk_raw[:], gqk_t[:, g:g + 1], qk_hi[:].bitcast(F32),
                                               ALU.mult, ALU.subtract).then_inc(qk_lo_ready, 1)

            def rope(e, q, g, dst):
                mean_square(q, DH, B_NORM)
                dve.wait_ge(qk_rotated, e + 1)
                nc.vector.tensor_tensor(rope_s[:], bank[:, B_MISC], sin_t[:], ALU.mult).then_inc(rope_s_ready, 1)
                diagonal(q)
                nc.vector.scalar_tensor_tensor(rope_c[:], qk_raw[:], gqk_t[:, g:g + 1], cos_t[:],
                                               ALU.mult, ALU.mult).then_inc(rope_c_ready, 1)
                dve.wait_ge(rope_c_ready, e + 1)
                nc.vector.tensor_tensor(rope_c[:], rope_c[:], rope_s[:], ALU.add).then_inc(rope_added, 1)
                dve.wait_ge(rope_added, e + 1)
                dve.wait_ge(norm_spread, q + 1)
                nc.vector.tensor_tensor(dst[:], rope_c[:], bank[:, B_NORM], ALU.mult).then_inc(rope_done, 1)

            def low_of_bank(hi_sem, value, lo, hi, b, done):
                dve.wait_ge(hi_sem, value)
                nc.vector.tensor_tensor(lo.rearrange("p a b -> p (a b)"), bank[:, b],
                                        hi.bitcast(F32).rearrange("p a b -> p (a b)"), ALU.subtract).then_inc(done, 1)

            def low_pT(hi_sem, hd, done):
                for g in range(GROUPS):
                    low_of_bank(hi_sem, hd * 2 + (g + 1), probs_T_lo[:, g], probs_T_hi[:, g], B_PT + g, done)

            def normalise(exp_sem, value, which, inv_sem, done):
                dve.wait_ge(exp_sem, value * TT)
                nc.vector.reciprocal(inv_p[:, which], psum_p[:, which]).then_inc(inv_sem, 1)
                dve.wait_ge(inv_sem, value)
                for t in range(TT):
                    nc.vector.tensor_scalar(probs[:, t], probs[:, t], inv_p[:, which, t:t + 1], None,
                                            ALU.mult).then_inc(done, 1)

            def head_low(k):
                dve.wait_ge(head_hi_ready, k + 1)
                nc.vector.tensor_tensor(head_lo[:, k], head_f[:, k], head_hi[:, k].bitcast(F32),
                                        ALU.subtract).then_inc(head_lo_ready, 1)

            scores = bank[:, B_SCORE:B_SCORE + 2].rearrange("p g (q s) -> p (g q) s", q=2)

            def head(j, r, last):
                n0 = j * GROUP_UNITS
                e0 = j * (PER_KV + 1)
                n = r * HEAD_UNITS + (n0 + 2)
                hd = r + j * PER_KV
                evacuate(n, 0, qk_raw[:])
                next_lo(n, 0)
                low_part(r + (e0 + 1), 0)
                evacuate(n + 1, 1, ka_f[:])
                next_lo(n + 1, 1)
                rope(r + (e0 + 1), r + (e0 + 2), 0, q_rope)
                evacuate(n + 2, 0, qa_f[:])
                next_lo(n + 2, 0)
                dve.wait_ge(score_b, hd + 1)
                nc.vector.tensor_reduce(top[:, 0], scores, AX_X, ALU.max).then_inc(top_b, 1)
                dve.wait_ge(top_b, hd + 1)
                nc.vector.tensor_scalar(neg_top[:, 0], top[:, 0], -SCALE, None, ALU.mult).then_inc(neg_top_b, 1)
                normalise(exp_b, hd + 1, 0, inv_b, probs_b)
                evacuate(n + 3, 1, va_f[:])
                next_lo(n + 3, 1)
                dve.wait_ge(score_a, hd + 1)
                for g in range(GROUPS):
                    for qi in range(2):
                        nc.vector.scalar_tensor_tensor(
                            na_scores[:, 2 * g + qi], bank[:, B_SCORE + g, qi * S:(qi + 1) * S], SCALE,
                            bias[:].rearrange("p h e c -> p h (e c)")[
                                :, bass.ds(hd, 1), (2 - 2 * qi) * GRID:(6 - 2 * qi) * GRID].rearrange(
                                    "p h c -> p (h c)"),
                            ALU.mult, ALU.add).then_inc(biased_a, 1)
                dve.wait_ge(biased_a, hd * TT + TT)
                nc.vector.tensor_reduce(top[:, 1], na_scores[:], AX_X, ALU.max).then_inc(top_a, 1)
                dve.wait_ge(top_a, hd + 1)
                nc.vector.tensor_scalar(neg_top[:, 1], top[:, 1], -1.0, None, ALU.mult).then_inc(neg_top_a, 1)
                low_pT(pT_hi_b, hd, pT_lo_b)
                normalise(exp_a, hd + 1, 1, inv_a, probs_a)
                evacuate(n + 4, 0, gate_out[:, 0])
                next_lo(n + 4, 0)
                low_of_bank(va_hi_ready, hd + 1, va_tok_lo[:], va_tok_hi[:], B_NORM, va_lo_ready)
                dve.wait_ge(head_b, hd + 1)
                nc.vector.tensor_copy(head_f[:, bass.ds(hd + HEADS, 1)], bank[:, B_MISC:B_MISC + 1]).then_inc(head_b_read, 1)
                evacuate(n + 5, 1, gate_out[:, 1])
                next_lo(n + 5, 1)
                low_pT(pT_hi_a, hd, pT_lo_a)
                dve.wait_ge(gate_stored[0], hd * 32 + 16)
                evacuate(n + 6, 0, gate_out[:, 0])
                next_lo(n + 6, 0)
                dve.wait_ge(head_a, hd + 1)
                nc.vector.tensor_copy(head_f[:, bass.ds(hd, 1)], bank[:, B_MISC:B_MISC + 1]).then_inc(head_a_read, 1)
                if last:
                    for k in range(KT - 2):
                        head_low(k)
                dve.wait_ge(gate_stored[1], hd * 32 + 16)
                evacuate(n + 7, 1, gate_out[:, 1])
                next_lo(n + 7, 1)
                for slot in range(2):
                    dve.wait_ge(gate_stored[slot], hd * 32 + 32)
                if last:
                    for k in range(KT - 2, KT):
                        head_low(k)

            for j in range(KV):
                n0 = j * GROUP_UNITS
                e0 = j * (PER_KV + 1)
                evacuate(n0, 0, qk_raw[:])
                if j == 0:
                    bias_parts(1, 4)
                    dve.wait_ge(const_landed, 48)
                else:
                    next_lo(n0, 0)
                low_part(e0, 1)
                rope(e0, e0 + 1, 1, k_rope)
                evacuate(n0 + 1, 1, vb_f[:])
                next_lo(n0 + 1, 1)
                if j == 0:
                    bias_parts(4, BIAS_PARTS)
                low_of_bank(vb_hi_ready, j + 1, vb_tok_lo[:], vb_tok_hi[:], B_PT, vb_lo_ready)
                rolled = PER_KV - (j == KV - 1)
                with dve.Fori(0, rolled) as r:
                    head(j, r, False)
            head(KV - 1, PER_KV - 1, True)
            with dve.Fori(0, KT // 2) as i:
                for slot in range(2):
                    n = i * 2 + (N_BRANCH + slot)
                    m = i * 2 + slot
                    dve.wait_ge(unit_done, n + 1)
                    dve.wait_ge(gates_open, m + 1)
                    nc.vector.tensor_tensor(mix_a[:], bank[:, 2 * slot], gate_in[:, slot, 0], ALU.mult)
                    nc.vector.tensor_tensor(mix_b[:], bank[:, 2 * slot + 1], gate_in[:, slot, 1], ALU.mult).then_inc(unit_read, 1)
                    dve.wait_ge(unit_read, n + 2)
                    nc.vector.tensor_tensor(mix_a[:], mix_a[:], mix_b[:], ALU.add).then_inc(mixed, 1)
                    next_lo(n, slot)
                    dve.wait_ge(mix_hi_ready, m + 1)
                    nc.vector.tensor_tensor(act_lo[:, bass.ds(m, 1)], mix_a[:].rearrange("p (a t) -> p a t", a=1),
                                            act_hi[:, bass.ds(m, 1)].bitcast(F32), ALU.subtract).then_inc(mix_lo_ready, 1)
                    dve.wait_ge(mix_lo_ready, m + 1)

            def add_square(count, slot, starts):
                dve.wait_ge(sq_ready, count + 1)
                dve.wait_ge(sq_added, count + starts)
                nc.vector.tensor_tensor(sq_sum[:], sq_sum[:], sq[:, slot], ALU.add).then_inc(sq_added, 1)

            def out_tile(n, m, par, more=True):
                dve.wait_ge(unit_done, n + 1)
                nc.vector.tensor_copy(sums[:, bass.ds(m, 1)], bank[:, par:par + 1]).then_inc(unit_read, 1)
                if more:
                    next_lo(n, par)
                add_square(m, par, 1)

            with dve.Fori(0, KT // 2 - 1) as i:
                for m in range(2):
                    out_tile(i * 2 + (N_OUT + m), i * 2 + m, m)
            dve.wait_ge(p_hi_ready, 1)
            nc.vector.tensor_tensor(p_lo[:], p_f[:], p_hi[:].bitcast(F32), ALU.subtract).then_inc(p_lo_ready, 1)
            out_tile(N_OUT + KT - 2, KT - 2, 0)
            out_tile(N_OUT + KT - 1, KT - 1, 1, False)

            def keep_rstd(q, b, times):
                dve.wait_ge(norm_spread, q + 1)
                nc.vector.tensor_copy(rstd[:], bank[:, b]).then_inc(rstd_ready, 1)
                dve.wait_ge(rstd_ready, times)

            def residual(which, norm, norm_bank, gain_out, filler, splits):
                par = (filler + 1) % 2
                mean_square(norm, D, norm_bank)
                diagonal(norm)
                split_lo(filler + 1, par, 0)
                keep_rstd(norm, norm_bank, 2 + 2 * which)

                def scale(k):
                    dve.wait_ge(gained, which * KT + k + 1)
                    nc.vector.tensor_tensor(sums[:, k], sums[:, k], rstd[:], ALU.mult).then_inc(scaled_v, 1)

                def low(k):
                    dve.wait_ge(resid_hi_ready, which * KT + k + 1)
                    if gain_out is None:
                        nc.vector.tensor_tensor(act_lo[:, k], resid[:, k], act_hi[:, k].bitcast(F32),
                                                ALU.subtract).then_inc(resid_lo_ready, 1)
                    else:
                        nc.vector.scalar_tensor_tensor(act_lo[:, k], resid[:, k], g_t[:, gain_out, k:k + 1],
                                                       act_hi[:, k].bitcast(F32), ALU.mult,
                                                       ALU.subtract).then_inc(resid_lo_ready, 1)

                scale(SCALED_BY_DVE[0])
                for k in range(KT):
                    if k in SCALED_BY_DVE:
                        dve.wait_ge(scaled_v, which * len(SCALED_BY_DVE) + SCALED_BY_DVE.index(k) + 1)
                    else:
                        dve.wait_ge(scaled_p, which * len(SCALED_BY_POOL) + SCALED_BY_POOL.index(k) + 1)
                    nc.vector.tensor_tensor(resid[:, k], resid[:, k], sums[:, k], ALU.add).then_inc(resid_ready, 1)
                    if k + 1 in SCALED_BY_DVE:
                        scale(k + 1)
                    if k:
                        low(k - 1)
                    if k == splits[0]:
                        split_lo(filler + 1, par, 1)
                    if k == splits[1]:
                        split_lo(filler + 2, 1 - par, 0)
                    if k == splits[2]:
                        split_lo(filler + 2, 1 - par, 1)
                low(KT - 1)
                if splits[2] == KT:
                    split_lo(filler + 2, 1 - par, 1)

            dve.wait_ge(resid_landed, 16 * KT // 2)
            residual(0, NORM_MIX, B_NORM, G_FFN, N_EMBED_A, (3, 12, KT))
            mean_square(NORM_FFN_IN, D, B_NORM)
            diagonal(NORM_FFN_IN)
            keep_rstd(NORM_FFN_IN, B_NORM, 3)

            def ffn_in(n, f):
                for i in range(CH):
                    par = (N_FFN + 2 * i) % 2
                    b = IN_BANKS[2 * i]
                    dve.wait_ge(unit_done, n + 2 * i + 1)
                    nc.vector.tensor_tensor(tmp[:, 0], bank[:, b], rstd[:], ALU.mult).then_inc(unit_read, 1)
                    next_lo(n + 2 * i, par)
                    dve.wait_ge(unit_done, n + 2 * i + 2)
                    nc.vector.tensor_tensor(tmp[:, 1], bank[:, IN_BANKS[2 * i + 1]], rstd[:], ALU.mult).then_inc(unit_read, 1)
                    dve.wait_ge(silu_ready, f + i + 1)
                    dve.wait_ge(unit_read, n + 2 * i + 2)
                    if not (isinstance(f, int) and f + i == 0):
                        dve.wait_ge(hid_lo_ready, f + i)
                    nc.vector.tensor_tensor(sq[:, 0], tmp[:, 0], tmp[:, 1], ALU.mult).then_inc(hid_ready, 1)
                    split_lo(n + 2 * i + 3, 1 - par, 0)
                    dve.wait_ge(hid_hi_ready, f + i + 1)
                    nc.vector.tensor_tensor(hid_lo[:, i], sq[:, 0], hid_hi[:, i].bitcast(F32),
                                            ALU.subtract).then_inc(hid_lo_ready, 1)
                    split_lo(n + 2 * i + 3, 1 - par, 1)

            def ffn_out(n, last):
                for u in range(OUT_UNITS):
                    dve.wait_ge(unit_done, n + u + 1)
                    for i in range(4):
                        m = 4 * u + i
                        ins = nc.vector.tensor_tensor(sums[:, m], sums[:, m], bank[:, OUT_BANKS[u] + i], ALU.add)
                    ins.then_inc(unit_read, 1)
                    if last:
                        if u < OUT_UNITS - 1:
                            next_lo(n + u, (n + u) % 2)
                        for i in range(4):
                            add_square(KT + 4 * u + i, (4 * u + i) % 2, 2)
                    else:
                        next_lo(n + u, (N_FFN + u) % 2)

            ffn_in(N_FFN, 0)
            dve.wait_ge(sums_zero, 1)
            with dve.Fori(1, CHUNKS) as c:
                n = c * CHUNK_UNITS + (N_FFN - OUT_UNITS)
                ffn_out(n, False)
                ffn_in(n + OUT_UNITS, c * CH)
            ffn_out(N_EMBED_B - OUT_UNITS, True)
            residual(1, NORM_FFN, 0, None, N_EMBED_B, (2, 4, 9))
            dve.wait_ge(embed_landed, 16)
            dve.wait_ge(embed_read, 16)

            def ple_tile(n, m, par, slot, emb, more=True):
                dve.wait_ge(ple_sig, m + 1)
                nc.vector.tensor_tensor(sums[:, bass.ds(m, 1)], tmp[:, 0:1], emb, ALU.mult).then_inc(ple_ready, 1)
                if more:
                    next_lo(n, par)
                add_square(m + 2 * KT, slot, 3)

            with dve.Fori(0, 4) as i:
                for s in range(2):
                    m = i * 2 + s
                    ple_tile(i * 2 + (N_PLE + s), m, (N_PLE + s) % 2, s, sums[:, bass.ds(m, 1)])
            with dve.Fori(4, 7) as i:
                for s in range(2):
                    ple_tile(i * 2 + (N_PLE + s), i * 2 + s, (N_PLE + s) % 2, s, embed[:, bass.ds(i * 2 + s - 8, 1)])
            for m in range(KT - 2, KT):
                ple_tile(N_PLE + m, m, (N_PLE + m) % 2, m % 2, embed[:, m - 8:m - 7], False)
            mean_square(NORM_PLE, D, 0)
            diagonal(NORM_PLE)
            keep_rstd(NORM_PLE, 0, 5)
            for i, k in enumerate(Y_BY_DVE + (None,)):
                if k is not None:
                    dve.wait_ge(gained, 2 * KT + k + 1)
                    nc.vector.tensor_tensor(sums[:, k], sums[:, k], rstd[:], ALU.mult).then_inc(y_scaled_v, 1)
                if i:
                    done = Y_BY_DVE[i - 1]
                    dve.wait_ge(y_scaled_v, i)
                    nc.vector.tensor_tensor(resid[:, done], resid[:, done], sums[:, done], ALU.add).then_inc(y_ready_v, 1)

        @block.tensor
        def _(pe):
            def unit(n, par, terms, fillers=0, gate=None, hooks=None, free=True,
                     half_sem=None):
                if free:
                    pe.wait_ge(unit_read, n - fillers)
                for idx, (b, hi, lo, start, stop) in enumerate(terms):
                    half, sub = divmod(idx, HALF)
                    slot = 2 * par + half
                    if hooks and idx in hooks:
                        hooks[idx]()
                    if sub == 0:
                        pe.wait_ge(lo_ready, 2 * n + (half + 3))
                    if gate:
                        gate(idx)
                    nc.tensor.matmul(bank[:, b], w_hi[:, slot, sub], hi, start=start, stop=False)
                    nc.tensor.matmul(bank[:, b], w_hi[:, slot, sub], lo, start=False, stop=False)
                    last = nc.tensor.matmul(bank[:, b], w_lo[:, slot, sub], hi, start=False, stop=stop)
                    if half_sem is not None and idx == HALF - 1:
                        last.then_inc(half_sem, 1)
                last.then_inc(unit_done, 1)

            def tall(b):
                return [(b, act_hi[:, k], act_lo[:, k], k == 0, k == KT - 1) for k in range(KT)]

            def sum_tokens(src, b):
                for t in range(TT):
                    last = nc.tensor.matmul(bank[:, b, t:t + 1], src[:, t * P:(t + 1) * P], ones[:, 0:1],
                                            start=True, stop=True)
                last.then_inc(norm_summed, 1)

            def spread(q, b):
                pe.wait_ge(norm_diag, q + 1)
                nc.tensor.matmul(bank[:, b], ones[:], diag[:].rearrange("p a b -> p (a b)"), start=True,
                                 stop=True).then_inc(norm_spread, 1)

            def turn_values(src, b, done):
                for t in range(TT):
                    last = nc.tensor.transpose(bank[:, b, t * P:(t + 1) * P], src[:, t * P:(t + 1) * P], ident_t[:])
                last.then_inc(done, 1)

            def turn_probs(done):
                for g in range(GROUPS):
                    for kc in range(2):
                        for qi in range(2):
                            last = nc.tensor.transpose(bank[:, B_PT + g, kc * S + qi * P:kc * S + (qi + 1) * P],
                                                       probs[:, 2 * g + qi, kc * P:(kc + 1) * P], ident_t[:])
                last.then_inc(done, 1)

            def score(q, k, done):
                for g in range(GROUPS):
                    for qi in range(2):
                        t = 2 * g + qi
                        last = nc.tensor.matmul(bank[:, B_SCORE + g, qi * S:(qi + 1) * S], q[:, t * P:(t + 1) * P],
                                                k[:, g * S:(g + 1) * S], start=True, stop=True)
                last.then_inc(done, 1)

            def values(v_hi, v_lo, done):
                for g in range(GROUPS):
                    out = bank[:, B_MISC, g * S:(g + 1) * S]
                    for kc in range(2):
                        t = 2 * g + kc
                        nc.tensor.matmul(out, v_hi[:, t], probs_T_hi[:, g, kc], start=kc == 0, stop=False)
                        nc.tensor.matmul(out, v_hi[:, t], probs_T_lo[:, g, kc], start=False, stop=False)
                        last = nc.tensor.matmul(out, v_lo[:, t], probs_T_hi[:, g, kc], start=False, stop=kc == 1)
                last.then_inc(done, 1)

            def sum_and_rotate(e):
                pe.wait_ge(qk_sq_ready, e + 1)
                sum_tokens(qk_sq, B_NORM)
                pe.wait_ge(qk_lo_ready, e + 1)
                nc.tensor.matmul(bank[:, B_MISC], rot_t[:], qk_hi[:], start=True, stop=False)
                nc.tensor.matmul(bank[:, B_MISC], rot_t[:], qk_lo[:], start=False, stop=True).then_inc(qk_rotated, 1)

            def flip_bias(first, end):
                flat = bias_flipped[:].rearrange("p h e c -> p (h e c)")
                for i in range(first, end):
                    nc.tensor.matmul(bank[:, B_SCORE + i % 4], flip_t[:], flat[:, i * T:(i + 1) * T], start=True,
                                     stop=True).then_inc(flipped, 1)

            def sum_x():
                pe.wait_ge(ones_set, 2)
                pe.wait_ge(x_sq_added, 5)
                sum_tokens(sq_sum, B_NORM)

            def turn_group_values(j):
                pe.wait_ge(unit_read, j * GROUP_UNITS + 3)
                turn_values(vb_f, B_PT, vb_turned)

            def head(j, r, first=False):
                n0 = j * GROUP_UNITS
                e0 = j * (PER_KV + 1)
                n = r * HEAD_UNITS + (n0 + 2)
                hd = r + j * PER_KV
                if first and j == 0:
                    unit(n, 0, tall(0), hooks={5: lambda: sum_and_rotate(e0), 13: lambda: spread(e0 + 1, B_NORM)})
                    pe.wait_ge(bias_read, 4)
                    flip_bias(5, BIAS_PARTS)
                else:
                    unit(n, 0, tall(0))
                if first:
                    turn_group_values(j)
                unit(n + 1, 1, tall(1))
                sum_and_rotate(r + (e0 + 1))
                unit(n + 2, 0, tall(0), hooks={HALF: lambda: spread(r + (e0 + 2), B_NORM)})
                pe.wait_ge(rope_done, r + (e0 + 2))
                score(q_rope, k_rope, score_b)
                unit(n + 3, 1, tall(1))
                pe.wait_ge(probs_b, hd * TT + TT)
                turn_probs(turned_b)
                pe.wait_ge(unit_read, n + 4)
                score(qa_f, ka_f, score_a)
                unit(n + 4, 0, tall(0))
                pe.wait_ge(unit_read, n + 5)
                turn_values(va_f, B_NORM, va_turned)
                pe.wait_ge(pT_lo_b, hd * 2 + 2)
                pe.wait_ge(vb_lo_ready, j + 1)
                values(vb_tok_hi, vb_tok_lo, head_b)
                unit(n + 5, 1, tall(1))
                pe.wait_ge(probs_a, hd * TT + TT)
                turn_probs(turned_a)
                unit(n + 6, 0, tall(0))
                pe.wait_ge(pT_lo_a, hd * 2 + 2)
                pe.wait_ge(va_lo_ready, hd + 1)
                pe.wait_ge(head_b_read, hd + 1)
                values(va_tok_hi, va_tok_lo, head_a)
                unit(n + 7, 1, tall(1))

            for j in range(KV):
                n0 = j * GROUP_UNITS
                e0 = j * (PER_KV + 1)
                if j == 0:
                    unit(0, 0, tall(0), gate=lambda k: pe.wait_ge(x_lo_ready, k + 1), free=False)
                    unit(1, 1, tall(1), free=False)
                    sum_x()
                    pe.wait_ge(table_landed, 16 * 2 * HEADS)
                    pe.wait_ge(mask_landed, 32)
                    flip_bias(0, 4)
                    spread(0, B_NORM)
                    pe.wait_ge(bias_read, 1)
                    flip_bias(4, 5)
                    pe.wait_ge(rot_ready, 1)
                else:
                    unit(n0, 0, tall(0))
                    unit(n0 + 1, 1, tall(1), hooks={HALF: lambda: sum_and_rotate(e0)})
                    spread(e0 + 1, B_NORM)
                head(j, 0, True)
                with pe.Fori(1, PER_KV) as r:
                    head(j, r)

            def branch(slot):
                return [(2 * slot + k // HEADS, head_hi[:, k], head_lo[:, k], k % HEADS == 0,
                         k % HEADS == HEADS - 1) for k in range(KT)]

            def first_branch(k):
                pe.wait_ge(head_lo_ready, k + 1)
                if k == HEADS:
                    pe.wait_ge(unit_read, N_BRANCH + 1)

            unit(N_BRANCH, 0, branch(0), gate=first_branch)
            unit(N_BRANCH + 1, 1, branch(1))
            with pe.Fori(1, KT // 2) as i:
                for slot in range(2):
                    unit(i * 2 + (N_BRANCH + slot), slot, branch(slot))
            unit(N_OUT, 0, tall(0), gate=lambda k: pe.wait_ge(mix_lo_ready, k + 1))
            unit(N_OUT + 1, 1, tall(1))
            with pe.Fori(1, KT // 2) as i:
                for m in range(2):
                    unit(i * 2 + (N_OUT + m), m, tall(m))

            def embed_unit(n, banks, squares, norm, b, sum_at, spread_at, taken):
                terms = [(banks[half][m], p_hi[:, k], p_lo[:, k], k == 0, k == 1)
                         for half in range(2) for k in range(2) for m in range(4)]

                def sums_hook():
                    pe.wait_ge(sq_added, squares)
                    sum_tokens(sq_sum, b)

                def gate(idx):
                    if HALF <= idx < HALF + 4 and banks[1][idx - HALF] in banks[0]:
                        pe.wait_ge(embed_read, taken + banks[0].index(banks[1][idx - HALF]) + 1)

                unit(n, n % 2, terms, hooks={sum_at: sums_hook, spread_at: lambda: spread(norm, b)}, gate=gate,
                     free=False, half_sem=embed_half)

            pe.wait_ge(p_lo_ready, 1)
            pe.wait_ge(unit_read, N_EMBED_A)
            embed_unit(N_EMBED_A, EMBED_A_BANKS, KT + 1, NORM_MIX, B_NORM, 4, HALF, 0)

            def sum_h_square(k):
                pe.wait_ge(h_sq_ready, k + 1)
                for t in range(TT):
                    last = nc.tensor.matmul(bank[:, B_NORM, t:t + 1], sq[:, k % 2, t * P:(t + 1) * P],
                                            ones[:, 0:1], start=k == 0 and t == 0, stop=k == KT - 1,
                                            skip_group_check=True)
                last.then_inc(norm_summed if k == KT - 1 else h_sq_summed, 1)

            pe.wait_ge(rstd_ready, 2)
            unit(N_FFN, N_FFN % 2, tall(IN_BANKS[0]), gate=lambda k: pe.wait_ge(resid_lo_ready, k + 1), free=False,
                 hooks={k + 1: (lambda k=k: sum_h_square(k)) for k in range(KT - 1)})
            sum_h_square(KT - 1)
            unit(N_FFN + 1, (N_FFN + 1) % 2, tall(IN_BANKS[1]), free=False,
                 hooks={HALF: lambda: spread(NORM_FFN_IN, B_NORM)})
            pe.wait_ge(embed_read, 8)

            def ffn_in(n, first):
                for i in range(first, IN_UNITS):
                    unit(n + i, (N_FFN + i) % 2, tall(IN_BANKS[i]), fillers=1)

            def ffn_out(n, f):
                for u in range(OUT_UNITS):
                    terms = [(OUT_BANKS[u] + m, hid_hi[:, k], hid_lo[:, k], k == 0, k == CH - 1)
                             for k in range(CH) for m in range(4)]

                    def gate(idx):
                        if idx % 4 == 0:
                            pe.wait_ge(hid_lo_ready, f + (idx // 4 + 1))
                    unit(n + u, (N_FFN + u) % 2, terms, fillers=1, gate=gate if u == 0 else None)

            ffn_in(N_FFN, 2)
            with pe.Fori(1, CHUNKS) as c:
                n = c * CHUNK_UNITS + (N_FFN - OUT_UNITS)
                ffn_out(n, c * CH - CH)
                ffn_in(n + OUT_UNITS, 0)
            ffn_out(N_EMBED_B - OUT_UNITS, FT - CH)
            pe.wait_ge(unit_read, N_EMBED_B - 1)
            embed_unit(N_EMBED_B, EMBED_B_BANKS, 2 * KT + 2, NORM_FFN, 0, HALF, 12, 8)
            pe.wait_ge(embed_read, 12)
            for k in range(KT + LAG):
                for u, idx in ((0, k), (1, k - LAG)):
                    if not 0 <= idx < KT:
                        continue
                    half, sub = divmod(idx, HALF)
                    slot = 2 * ((N_PLE + u) % 2) + half
                    b = PLE_BANKS[u]
                    if sub == 0:
                        pe.wait_ge(lo_ready, 2 * (N_PLE + u) + half + 3)
                    if u == 0:
                        pe.wait_ge(resid_lo_ready, KT + k + 1)
                    nc.tensor.matmul(bank[:, b], w_hi[:, slot, sub], act_hi[:, idx], start=idx == 0, stop=False)
                    nc.tensor.matmul(bank[:, b], w_hi[:, slot, sub], act_lo[:, idx], start=False, stop=False)
                    last = nc.tensor.matmul(bank[:, b], w_lo[:, slot, sub], act_hi[:, idx], start=False, stop=idx == KT - 1)
                    if idx == KT - 1:
                        last.then_inc(unit_done, 1)
            with pe.Fori(1, KT // 2) as i:
                for m in range(2):
                    pe.wait_ge(ple_sig, i * 2 + (m - 1))
                    unit(i * 2 + (N_PLE + m), (N_PLE + m) % 2, tall(PLE_BANKS[m]), free=False)
            pe.wait_ge(sq_added, 3 * KT + 3)
            sum_tokens(sq_sum, 0)
            spread(NORM_PLE, 0)


def kernel(x_prompt, x_sample, p_prompt, p_sample, g_pre_mix, w_in, rpb, g_q, g_k, w_branch_a, w_branch_b,
           w_out, g_post_mix, g_pre_ffn, w_ffn_in, w_ffn_out, g_post_ffn, w_ple, w_ple_gate, g_ple):
    import concourse.bacc as bacc
    from concourse.bass_utils import run_bass_kernel_spmd

    def lay(a):
        return np.ascontiguousarray(a)

    def column(g):
        return np.asarray(g)[0].reshape(KT, P).T

    feeds = {
        "xT": lay(np.concatenate([np.asarray(x_prompt)[0], np.asarray(x_sample)[0]]).T),
        "pT": lay(np.concatenate([np.asarray(p_prompt)[0, 0], np.asarray(p_sample)[0, 0]]).T),
        "gains": lay(np.stack([column(g) for g in (g_pre_mix, g_post_mix, g_pre_ffn, g_post_ffn, g_ple)], axis=1)),
        "gains_qk": lay(np.stack([np.asarray(g_q)[0], np.asarray(g_k)[0]], axis=1)),
        "w_in": lay(np.asarray(w_in)[0]),
        "rpb": lay(np.asarray(rpb)[0].reshape(-1, 2 * NA_COLS - 1)),
        "w_branch_a": lay(np.asarray(w_branch_a)[0]),
        "w_branch_b": lay(np.asarray(w_branch_b)[0]),
        "w_out": lay(np.asarray(w_out)[0]),
        "w_ffn_in": lay(np.asarray(w_ffn_in)[0]),
        "w_ffn_out": lay(np.asarray(w_ffn_out)[0]),
        "w_ple": lay(np.asarray(w_ple)[0]),
        "w_ple_gate": lay(np.asarray(w_ple_gate)[0]),
    }
    feeds.update(shape_constants())
    nc = bacc.Bacc("TRN2", target_bir_lowering=False, num_devices=1)
    aps = {name: nc.dram_tensor(name, a.shape, mybir.dt.from_np(a.dtype), kind="ExternalInput").ap()
           for name, a in feeds.items()}
    aps["yT"] = nc.dram_tensor("yT", (D, T), F32, kind="ExternalOutput").ap()
    build(nc, **aps)
    y = run_bass_kernel_spmd(nc, [feeds], core_ids=[0]).results[0]["yT"]
    return lay(y[:, :S].T)[None], lay(y[:, S:].T)[None]
```
